# Optimizing a Trainium2 kernel written in Bass

```python
import math
import jax, jax.numpy as jnp
from jax import lax
import numpy as np
import jax
import jax.numpy as jnp

D_MODEL = 1024
BATCH = 1
SEQ = 512
DEPTH = 1

HEAD_DIM = 64
ATT_GROUPS = ((128, 1), (512, 4), (2048, 16))
HEADS_PER_GROUP = 4
N_ATT_HEADS = HEADS_PER_GROUP * len(ATT_GROUPS)
ATT_WIDTH = N_ATT_HEADS * HEAD_DIM
ATT_MERGED = HEADS_PER_GROUP * HEAD_DIM
BLK = 128
POOL_WINDOWS = (2, 4, 8, 16)
POOL_GROUP_WIDTH = 3 * D_MODEL // 16
POOL_WIDTH = POOL_GROUP_WIDTH * len(POOL_WINDOWS)
D_FF = 4 * D_MODEL
N_IN = 3 * ATT_WIDTH + POOL_WIDTH + 2 * D_MODEL
NORM_EPS = 1e-6
ALIBI_MAX_BIAS = 8.0


def _rmsnorm(x, g):
    xf = x.astype(jnp.float32)
    y = xf * lax.rsqrt(jnp.mean(xf * xf, axis=-1, keepdims=True) + NORM_EPS)
    return (y * g.astype(jnp.float32)).astype(x.dtype)

def _dilated_window_attention(q, k, v, dilation, n_steps, slopes):
    B, S, H, Dh = q.shape
    L = S // dilation
    nb = -(-L // BLK)
    Lp = nb * BLK
    Z = B * dilation

    def to_sub(t):
        t = t.reshape(B, L, dilation, H, Dh).transpose(0, 2, 1, 3, 4).reshape(Z, L, H, Dh)
        return jnp.pad(t, ((0, 0), (0, Lp - L), (0, 0), (0, 0)))

    def band(t):
        prev = jnp.pad(t, ((0, 0), (BLK, 0), (0, 0), (0, 0)))[:, :Lp]
        return jnp.concatenate([prev.reshape(Z, nb, BLK, H, Dh),
                                t.reshape(Z, nb, BLK, H, Dh)], axis=2)

    qb = to_sub(q).reshape(Z, nb, BLK, H, Dh).astype(jnp.float32)
    kb = band(to_sub(k)).astype(jnp.float32)
    vb = band(to_sub(v)).astype(jnp.float32)

    s = jnp.einsum('znqhd,znkhd->znhqk', qb, kb) * (Dh ** -0.5)
    steps = BLK + jnp.arange(BLK)[:, None] - jnp.arange(2 * BLK)[None, :]
    key_idx = (jnp.arange(nb)[:, None, None] * BLK
               + jnp.arange(2 * BLK)[None, None, :] - BLK)
    valid = (steps >= 0) & (steps <= n_steps) & (key_idx >= 0)
    bias = -(slopes[:, None, None] * (steps * dilation).astype(jnp.float32))
    s = jnp.where(valid[None, :, None], s + bias[None, None], -jnp.inf)
    lse = jax.nn.logsumexp(s, axis=-1)
    p = jnp.exp(s - lse[..., None])
    o = jnp.einsum('znhqk,znkhd->znqhd', p, vb).reshape(Z, Lp, H, Dh)[:, :L]
    lse = lse.transpose(0, 1, 3, 2).reshape(Z, Lp, H)[:, :L]
    o = o.reshape(B, dilation, L, H, Dh).transpose(0, 2, 1, 3, 4).reshape(B, S, H, Dh)
    lse = lse.reshape(B, dilation, L, H).transpose(0, 2, 1, 3).reshape(B, S, H)
    return o, lse

def _attention_branch(q, k, v):
    B, S, _ = q.shape
    q = q.reshape(B, S, N_ATT_HEADS, HEAD_DIM)
    k = k.reshape(B, S, N_ATT_HEADS, HEAD_DIM)
    v = v.reshape(B, S, N_ATT_HEADS, HEAD_DIM)
    slopes = 2.0 ** (-ALIBI_MAX_BIAS * (jnp.arange(N_ATT_HEADS, dtype=jnp.float32) + 1.0)
                     / N_ATT_HEADS)
    outs, lses = [], []
    for g, (window, dilation) in enumerate(ATT_GROUPS):
        hs = slice(g * HEADS_PER_GROUP, (g + 1) * HEADS_PER_GROUP)
        o, l = _dilated_window_attention(q[:, :, hs], k[:, :, hs], v[:, :, hs],
                                         dilation, window // dilation, slopes[hs])
        outs.append(o)
        lses.append(l)
    outs = jnp.stack(outs, axis=0)
    wts = jax.nn.softmax(jnp.stack(lses, axis=0), axis=0)
    merged = jnp.sum(wts[..., None] * outs, axis=0)
    return merged.reshape(B, S, ATT_MERGED)

def _pool_branch(pz, w_grp, scale):
    B, S, _ = pz.shape
    pf = pz.astype(jnp.float32).reshape(B, S, len(POOL_WINDOWS), POOL_GROUP_WIDTH)
    c0 = jnp.pad(jnp.cumsum(pf, axis=1), ((0, 0), (1, 0), (0, 0), (0, 0)))
    t = jnp.arange(S)
    pooled = []
    for g, w in enumerate(POOL_WINDOWS):
        lower = jnp.take(c0[:, :, g], jnp.maximum(t + 1 - w, 0), axis=1)
        count = jnp.minimum(t + 1, w).astype(jnp.float32)[None, :, None]
        pooled.append((c0[:, 1:, g] - lower) / count)
    pooled = jnp.stack(pooled, axis=2) - pf
    mixed = jnp.einsum('bsgc,gcd->bsgd', pooled, w_grp.astype(jnp.float32))
    return mixed.reshape(B, S, POOL_WIDTH) * scale.astype(jnp.float32)

def first_inputs(seed: int = 0) -> dict:
    key = jax.random.key(seed)
    ks = jax.random.split(key, 12)
    f32 = jnp.float32

    def nrm(k, shape, fan_in):
        return jax.random.normal(k, shape, f32) * (fan_in ** -0.5)

    def gain(k, shape):
        return 1.0 + 0.02 * jax.random.normal(k, shape, f32)

    return {
        "x": jax.random.normal(ks[0], (BATCH, SEQ, D_MODEL), f32),
        "norm_mix_g": gain(ks[1], (DEPTH, D_MODEL)),
        "w_in": nrm(ks[2], (DEPTH, D_MODEL, N_IN), D_MODEL),
        "w_att_out": nrm(ks[3], (DEPTH, ATT_MERGED, D_MODEL), ATT_MERGED),
        "w_pool_grp": nrm(ks[4], (DEPTH, len(POOL_WINDOWS), POOL_GROUP_WIDTH, POOL_GROUP_WIDTH),
                          POOL_GROUP_WIDTH),
        "pool_scale": 1.0 + 0.1 * jax.random.normal(ks[5], (DEPTH, POOL_WIDTH), f32),
        "w_pool_out": nrm(ks[6], (DEPTH, POOL_WIDTH, D_MODEL), POOL_WIDTH),
        "w_out": nrm(ks[7], (DEPTH, D_MODEL, D_MODEL), D_MODEL),
        "norm_mlp_g": gain(ks[8], (DEPTH, D_MODEL)),
        "w_mlp_in": nrm(ks[9], (DEPTH, D_MODEL, D_FF), D_MODEL),
        "w_mlp_out": nrm(ks[10], (DEPTH, D_FF, D_MODEL), D_FF),
        "norm_final_g": gain(ks[11], (D_MODEL,)),
    }

def first_block(x, norm_mix_g, w_in, w_att_out, w_pool_grp, pool_scale, w_pool_out, w_out,
              norm_mlp_g, w_mlp_in, w_mlp_out, norm_final_g):
    dt = x.dtype
    offs = np.cumsum([ATT_WIDTH, ATT_WIDTH, ATT_WIDTH, POOL_WIDTH, D_MODEL]).tolist()
    h = x
    for l in range(DEPTH):
        u = _rmsnorm(h, norm_mix_g[l])
        z = jnp.einsum('bsd,dn->bsn', u, w_in[l])
        q, k, v, pz, ga, gp = jnp.split(z, offs, axis=-1)
        a = _attention_branch(q, k, v).astype(dt)
        p = _pool_branch(pz, w_pool_grp[l], pool_scale[l]).astype(dt)
        merged = (jax.nn.sigmoid(ga) * jnp.einsum('bsc,cd->bsd', a, w_att_out[l])
                  + jax.nn.sigmoid(gp) * jnp.einsum('bsc,cd->bsd', p, w_pool_out[l]))
        h = h + jnp.einsum('bsd,de->bse', merged, w_out[l])
        m = _rmsnorm(h, norm_mlp_g[l])
        hid = jnp.square(jax.nn.relu(jnp.einsum('bsd,df->bsf', m, w_mlp_in[l])))
        h = h + jnp.einsum('bsf,fd->bsd', hid, w_mlp_out[l])
    return _rmsnorm(h, norm_final_g)


RET_W = 3 * D_MODEL // 8
RET_HEADS = RET_W // HEAD_DIM
HGRN_W = 3 * D_MODEL // 8
HGRN_HEADS = HGRN_W // HEAD_DIM
HGRN_DK = HEAD_DIM
GLA_W = D_MODEL // 4
GLA_HEADS = GLA_W // HEAD_DIM
GLA_DK = HEAD_DIM // 2
GLA_QK = GLA_HEADS * GLA_DK
GLA_GATE_RANK = 16
GLA_TAU = 16.0
D_MIX = RET_W + HGRN_W + GLA_W
CHUNK = 64
ROPE_BASE = 10000.0
EPS = 1e-6
F_MIN = 1e-30
N_GROUPS = 4
EXPERTS_PER_GROUP = 8
N_EXPERTS = N_GROUPS * EXPERTS_PER_GROUP
TOP_K_INNER = 2
D_EXPERT = D_MODEL // 4
N_MOD = 6
IN_PROJ_SIZES = (RET_W,) * 4 + (HGRN_W,) * 4 + (GLA_QK, GLA_QK, GLA_W, GLA_W, GLA_GATE_RANK)
IN_PROJ_DIM = sum(IN_PROJ_SIZES)


def rmsnorm(x, gain):
    xf = x.astype(jnp.float32)
    y = xf * lax.rsqrt(jnp.mean(xf * xf, axis=-1, keepdims=True) + EPS)
    return y.astype(x.dtype) * gain

def split_heads(t, n_heads):
    b, s, w = t.shape
    return t.reshape(b, s, n_heads, w // n_heads).transpose(0, 2, 1, 3).astype(jnp.float32)

def head_rmsnorm(o, gain):
    b, h, s, d = o.shape
    o = o.transpose(0, 2, 1, 3)
    o = o * lax.rsqrt(jnp.mean(o * o, axis=-1, keepdims=True) + EPS)
    return o.reshape(b, s, h * d) * gain.astype(jnp.float32)

def rope_tables(positions, dim):
    inv_freq = ROPE_BASE ** (-jnp.arange(0, dim, 2, dtype=jnp.float32) / dim)
    ang = positions.astype(jnp.float32)[..., None] * inv_freq
    return jnp.cos(ang)[:, None], jnp.sin(ang)[:, None]

def apply_rope(t, cos, sin):
    t1, t2 = jnp.split(t, 2, axis=-1)
    return jnp.concatenate([t1 * cos - t2 * sin, t1 * sin + t2 * cos], axis=-1)

def retention_chunkwise(q, k, v):
    b, h, s, dk = q.shape
    dv = v.shape[-1]
    n = s // CHUNK
    log_gamma = jnp.log1p(-jnp.exp2(-5.0 - jnp.arange(h, dtype=jnp.float32)))
    idx = jnp.arange(CHUNK, dtype=jnp.float32)
    rel = idx[:, None] - idx[None, :]
    decay = jnp.where(rel >= 0, jnp.exp(log_gamma[:, None, None] * jnp.maximum(rel, 0.0)), 0.0)
    zeta = jnp.exp(log_gamma[:, None] * (CHUNK - 1 - idx))
    xi = jnp.exp(log_gamma[:, None] * (idx + 1.0))
    chunk_decay = jnp.exp(log_gamma * CHUNK)[:, None, None]
    qc = q.reshape(b, h, n, CHUNK, dk)
    kc = k.reshape(b, h, n, CHUNK, dk)
    vc = v.reshape(b, h, n, CHUNK, dv)
    scores = jnp.einsum('bhnid,bhnjd->bhnij', qc, kc) * decay[:, None]
    o_intra = jnp.einsum('bhnij,bhnje->bhnie', scores, vc)
    u = jnp.einsum('bhnjd,hj,bhnje->nbhde', kc, zeta, vc)

    def step(r, u_i):
        return r * chunk_decay + u_i, r

    _, r_prev = lax.scan(step, jnp.zeros((b, h, dk, dv), jnp.float32), u)
    o_inter = jnp.einsum('bhnid,nbhde,hi->bhnie', qc, r_prev, xi)
    return (o_intra + o_inter).reshape(b, h, s, dv)

def gated_linear_recurrence_chunkwise(q, k, v, log_a):
    b, h, s, dk = q.shape
    dv = v.shape[-1]
    n = s // CHUNK
    mask = jnp.tril(jnp.ones((CHUNK, CHUNK), dtype=bool))[:, :, None]

    def to_chunks(t):
        return jnp.moveaxis(t.reshape(b, h, n, CHUNK, t.shape[-1]), 2, 0)

    def step(state, inp):
        qc, kc, vc, lac = inp
        cum = jnp.cumsum(lac, axis=-2)
        o_inter = jnp.einsum('bhcd,bhde->bhce', qc * jnp.exp(cum), state)
        diff = cum[:, :, :, None, :] - cum[:, :, None, :, :]
        dec = jnp.where(mask, jnp.exp(jnp.where(mask, diff, 0.0)), 0.0)
        scores = jnp.einsum('bhtd,bhsd,bhtsd->bhts', qc, kc, dec)
        o = o_inter + jnp.einsum('bhts,bhse->bhte', scores, vc)
        cum_last = cum[:, :, -1:, :]
        new_state = (jnp.exp(cum_last[:, :, 0, :])[..., None] * state
                     + jnp.einsum('bhsd,bhse->bhde', kc * jnp.exp(cum_last - cum), vc))
        return new_state, o

    s0 = jnp.zeros((b, h, dk, dv), jnp.float32)
    _, o = lax.scan(step, s0, (to_chunks(q), to_chunks(k), to_chunks(v), to_chunks(log_a)))
    return jnp.moveaxis(o, 0, 2).reshape(b, h, s, dv)

def hybrid_mixer(h, cos, sin, w_in, ret_norm, hgrn_norm, hgrn_lb, gla_wa2, gla_ba, gla_norm, w_out):
    proj = h @ w_in
    splits = np.cumsum(IN_PROJ_SIZES)[:-1].tolist()
    (rq, rk, rv, rg, hq, hf, hi, hg, gq, gk, gv, gg, ga) = jnp.split(proj, splits, axis=-1)

    q = apply_rope(split_heads(rq, RET_HEADS), cos, sin)
    k = apply_rope(split_heads(rk, RET_HEADS), cos, sin) * HEAD_DIM ** -0.5
    o_ret = retention_chunkwise(q, k, split_heads(rv, RET_HEADS))
    o_ret = head_rmsnorm(o_ret, ret_norm) * jax.nn.silu(rg.astype(jnp.float32))

    lb = hgrn_lb.astype(jnp.float32).reshape(HGRN_HEADS, 1, HGRN_DK)
    z = split_heads(hf, HGRN_HEADS)
    f = lb + (1.0 - lb) * jax.nn.sigmoid(z)
    log_f = jnp.log(jnp.maximum(f, F_MIN))
    k = (1.0 - lb) * jax.nn.sigmoid(-z)
    q = jax.nn.silu(split_heads(hq, HGRN_HEADS)) * HGRN_DK ** -0.5
    o_hgrn = gated_linear_recurrence_chunkwise(q, k, split_heads(hi, HGRN_HEADS), log_f)
    o_hgrn = head_rmsnorm(o_hgrn, hgrn_norm) * jax.nn.silu(hg.astype(jnp.float32))

    log_a = jax.nn.log_sigmoid((ga @ gla_wa2 + gla_ba).astype(jnp.float32)) / GLA_TAU
    q = split_heads(gq, GLA_HEADS) * GLA_DK ** -0.5
    o_gla = gated_linear_recurrence_chunkwise(q, split_heads(gk, GLA_HEADS), split_heads(gv, GLA_HEADS),
                                              split_heads(log_a, GLA_HEADS))
    o_gla = head_rmsnorm(o_gla, gla_norm) * jax.nn.silu(gg.astype(jnp.float32))

    merged = jnp.concatenate([o_ret, o_hgrn, o_gla], axis=-1).astype(h.dtype)
    return merged @ w_out

def hierarchical_moe(h, w_rg, b_rg, w_re, b_re, w_gate, w_up, w_down):
    b, s, d = h.shape
    tok = h.reshape(b * s, d)
    g_logits = (tok @ w_rg + b_rg).astype(jnp.float32)
    g_idx = jnp.argmax(g_logits, axis=-1)
    g_w = jnp.max(jax.nn.softmax(g_logits, axis=-1), axis=-1, keepdims=True)
    e_logits = (tok @ w_re + b_re).astype(jnp.float32).reshape(-1, N_GROUPS, EXPERTS_PER_GROUP)
    e_in_group = jnp.einsum('nge,ng->ne', e_logits, jax.nn.one_hot(g_idx, N_GROUPS, dtype=jnp.float32))
    top_val, top_idx = lax.top_k(e_in_group, TOP_K_INNER)
    top_w = jax.nn.softmax(top_val, axis=-1) * g_w
    expert_ids = g_idx[:, None] * EXPERTS_PER_GROUP + top_idx
    combine = jnp.einsum('nk,nke->ne', top_w,
                         jax.nn.one_hot(expert_ids, N_EXPERTS, dtype=jnp.float32)).astype(h.dtype)
    out = jnp.zeros_like(tok)
    for e in range(N_EXPERTS):
        hid = jax.nn.silu(tok @ w_gate[e]) * (tok @ w_up[e])
        out = out + combine[:, e:e + 1] * (hid @ w_down[e])
    return out.reshape(b, s, d)

def second_inputs(seed: int = 0) -> dict:
    key = jax.random.key(seed)
    ks = jax.random.split(key, 24)
    f32 = jnp.float32

    def nrm(k, shape, scale):
        return jax.random.normal(k, shape, f32) * scale

    x = nrm(ks[0], (BATCH, SEQ, D_MODEL), 1.0)
    c = nrm(ks[1], (BATCH, D_MODEL), 1.0)
    positions = (jax.random.randint(ks[2], (BATCH, 1), 0, 1024)
                 + jnp.arange(SEQ, dtype=jnp.int32)[None, :]).astype(jnp.int32)
    w_ada = nrm(ks[3], (DEPTH, D_MODEL, N_MOD * D_MODEL), 0.5 * D_MODEL ** -0.5)
    b_ada = nrm(ks[4], (DEPTH, N_MOD * D_MODEL), 0.02)
    norm_mix = 1.0 + nrm(ks[5], (DEPTH, D_MODEL), 0.02)
    norm_ffn = 1.0 + nrm(ks[6], (DEPTH, D_MODEL), 0.02)
    w_in = nrm(ks[7], (DEPTH, D_MODEL, IN_PROJ_DIM), D_MODEL ** -0.5)
    ret_norm = 1.0 + nrm(ks[8], (DEPTH, RET_W), 0.02)
    hgrn_norm = 1.0 + nrm(ks[9], (DEPTH, HGRN_W), 0.02)
    hgrn_lb_logits = nrm(ks[10], (DEPTH, HGRN_HEADS * HGRN_DK), 1.0)
    gla_wa2 = nrm(ks[11], (DEPTH, GLA_GATE_RANK, GLA_QK), GLA_GATE_RANK ** -0.5)
    gla_ba = nrm(ks[12], (DEPTH, GLA_QK), 0.1)
    gla_norm = 1.0 + nrm(ks[13], (DEPTH, GLA_W), 0.02)
    w_out = nrm(ks[14], (DEPTH, D_MIX, D_MODEL), D_MIX ** -0.5)
    router_group_w = nrm(ks[15], (DEPTH, D_MODEL, N_GROUPS), D_MODEL ** -0.5)
    router_group_b = nrm(ks[16], (DEPTH, N_GROUPS), 0.01)
    router_expert_w = nrm(ks[17], (DEPTH, D_MODEL, N_EXPERTS), D_MODEL ** -0.5)
    router_expert_b = nrm(ks[18], (DEPTH, N_EXPERTS), 0.01)
    expert_w_gate = nrm(ks[19], (DEPTH, N_EXPERTS, D_MODEL, D_EXPERT), D_MODEL ** -0.5)
    expert_w_up = nrm(ks[20], (DEPTH, N_EXPERTS, D_MODEL, D_EXPERT), D_MODEL ** -0.5)
    expert_w_down = nrm(ks[21], (DEPTH, N_EXPERTS, D_EXPERT, D_MODEL), D_EXPERT ** -0.5)
    norm_final = 1.0 + nrm(ks[22], (D_MODEL,), 0.02)
    return {"x": x, "c": c, "positions": positions, "w_ada": w_ada, "b_ada": b_ada,
            "norm_mix": norm_mix, "norm_ffn": norm_ffn, "w_in": w_in, "ret_norm": ret_norm,
            "hgrn_norm": hgrn_norm, "hgrn_lb_logits": hgrn_lb_logits, "gla_wa2": gla_wa2,
            "gla_ba": gla_ba, "gla_norm": gla_norm, "w_out": w_out,
            "router_group_w": router_group_w, "router_group_b": router_group_b,
            "router_expert_w": router_expert_w, "router_expert_b": router_expert_b,
            "expert_w_gate": expert_w_gate, "expert_w_up": expert_w_up,
            "expert_w_down": expert_w_down, "norm_final": norm_final}

def second_block(x, c, positions, w_ada, b_ada, norm_mix, norm_ffn, w_in, ret_norm, hgrn_norm,
              hgrn_lb_logits, gla_wa2, gla_ba, gla_norm, w_out, router_group_w, router_group_b,
              router_expert_w, router_expert_b, expert_w_gate, expert_w_up, expert_w_down,
              norm_final):
    cos, sin = rope_tables(positions, HEAD_DIM)
    lb_w = jax.nn.softmax(hgrn_lb_logits.astype(jnp.float32), axis=0)
    lower_bounds = jnp.cumsum(lb_w, axis=0) - lb_w[0]
    c_act = jax.nn.silu(c)
    for layer in range(DEPTH):
        mod = c_act @ w_ada[layer] + b_ada[layer]
        shift_m, scale_m, gate_m, shift_f, scale_f, gate_f = [m[:, None, :] for m in jnp.split(mod, N_MOD, axis=-1)]
        h = rmsnorm(x, norm_mix[layer]) * (1.0 + scale_m) + shift_m
        x = x + gate_m * hybrid_mixer(h, cos, sin, w_in[layer], ret_norm[layer], hgrn_norm[layer],
                                      lower_bounds[layer], gla_wa2[layer], gla_ba[layer],
                                      gla_norm[layer], w_out[layer])
        h = rmsnorm(x, norm_ffn[layer]) * (1.0 + scale_f) + shift_f
        x = x + gate_f * hierarchical_moe(h, router_group_w[layer], router_group_b[layer],
                                          router_expert_w[layer], router_expert_b[layer],
                                          expert_w_gate[layer], expert_w_up[layer], expert_w_down[layer])
    return rmsnorm(x, norm_final)


def setup_inputs(seed=0):
    out = dict(first_inputs(seed))
    for name, value in second_inputs(seed + 1).items():
        if name != "x":
            out[name + "_2"] = value
    return out


def reference(
    x, norm_mix_g, w_in, w_att_out, w_pool_grp, pool_scale, w_pool_out, w_out, norm_mlp_g,
    w_mlp_in, w_mlp_out, norm_final_g, c_2, positions_2, w_ada_2, b_ada_2, norm_mix_2,
    norm_ffn_2, w_in_2, ret_norm_2, hgrn_norm_2, hgrn_lb_logits_2, gla_wa2_2, gla_ba_2,
    gla_norm_2, w_out_2, router_group_w_2, router_group_b_2, router_expert_w_2,
    router_expert_b_2, expert_w_gate_2, expert_w_up_2, expert_w_down_2, norm_final_2,
):
    x = first_block(
        x, norm_mix_g, w_in, w_att_out, w_pool_grp, pool_scale, w_pool_out, w_out, norm_mlp_g,
        w_mlp_in, w_mlp_out, norm_final_g,
    )
    return second_block(
        x, c_2, positions_2, w_ada_2, b_ada_2, norm_mix_2, norm_ffn_2, w_in_2, ret_norm_2,
        hgrn_norm_2, hgrn_lb_logits_2, gla_wa2_2, gla_ba_2, gla_norm_2, w_out_2,
        router_group_w_2, router_group_b_2, router_expert_w_2, router_expert_b_2,
        expert_w_gate_2, expert_w_up_2, expert_w_down_2, norm_final_2,
    )


_drawn_inputs = setup_inputs


def setup_inputs(seed=0):
    import zlib

    import numpy as np

    out = dict(_drawn_inputs(seed))
    spreads = {}
    factors = {'norm_mix_g': 3.695,
     'norm_mlp_g': 2.948,
     'norm_mix_2': 6.343,
     'norm_ffn_2': 4.684,
     'ret_norm_2': 8.0,
     'hgrn_norm_2': 8.0,
     'gla_ba_2': 7.512,
     'gla_norm_2': 8.0,
     'router_group_b_2': 35.589,
     'router_expert_b_2': 22.605,
     'norm_final_2': 8.824}
    for name, (base, spread) in spreads.items():
        noise = np.random.default_rng([zlib.crc32(name.encode()), seed]).standard_normal(out[name].shape)
        drawn = base * np.exp(spread * noise) if base else spread * noise
        out[name] = jnp.asarray(drawn.astype(out[name].dtype))
    for name, factor in factors.items():
        out[name] = (out[name] * factor).astype(out[name].dtype)
    return out
```

```python
import numpy as np
import concourse.bass as bass
from concourse import mybir
from contextlib import ExitStack

F32 = mybir.dt.float32
F32R = mybir.dt.float32r
I32 = mybir.dt.int32
U32 = mybir.dt.uint32
ACT = mybir.ActivationFunctionType
ALU = mybir.AluOpType
AX = mybir.AxisListType

P = 128
S = 512
D = 1024
NC = S // P
KD = D // P
EPS = 1e-6
UNIT = 2048
NU_A, NU_B, NU_C, NU_D, NU_E, NU_F, NU_G = 4, 6, 3, 1, 16, 4, 32
A0 = 0
B0 = A0 + NU_A
C0 = B0 + NU_B
D0 = C0 + NU_C
E0 = D0 + NU_D
F0 = E0 + NU_E
G0 = F0 + NU_F
H0 = G0 + NU_G
NU_H, NU_I, NU_J, NU_K = 4, 4, 8, 4
I0 = H0 + NU_H
J0 = I0 + NU_I
K0 = J0 + NU_J
M0 = K0 + NU_K
N_EXP = 32
N_GROUP, PER_GROUP = 4, 8
N_LOG = N_GROUP + N_EXP
N_UNITS = M0 + 3 * N_EXP
NEG = -1.0e30
TWO_PI = 2 * np.pi
PI_IN = 3.1415925


def _turn():
    a = 6.28125
    b = float(np.float32(np.round((TWO_PI - a) * 2 ** 21) / 2 ** 21))
    return a, b, float(np.float32(TWO_PI - a - b))


TURN = _turn()
HALF = D // 2
PG = 96


def build(nc, t):
    ctx = ExitStack()
    with ctx:
        def sb(name, shape, dt=F32):
            return ctx.enter_context(nc.sbuf_tensor(name, shape, dt))

        def sem(name):
            return ctx.enter_context(nc.semaphore(name))

        RAW = sb("raw", [P, 2, UNIT])
        WH = sb("w_high", [P, 2, UNIT], F32R)
        WL = sb("w_low", [P, 2, UNIT], F32R)
        UH = sb("u_high", [P, KD, S], F32R)
        UL = sb("u_low", [P, KD, S], F32R)
        VH = sb("v_high", [P, KD, S], F32R)
        VL = sb("v_low", [P, KD, S], F32R)
        X = sb("x", [P, NC, D])
        IDN = sb("ident", [P, P])
        COLS = sb("cols", [P, 64])
        SS = sb("sumsq", [P, 8])
        ATH = sb("att_high", [P, 2, S], F32R)
        ATL = sb("att_low", [P, 2, S], F32R)
        AR = sb("arena", [P, 20992])
        ONESB = sb("block_ones", [P, P])
        CA = sb("c_act", [P, 8])
        MODC = sb("mod_cols", [P, 16])
        LBS = sb("lower_bound", [P, 12])
        PS = ctx.enter_context(nc.psum_tensor("ps", [P, 8, 512], F32))

        def ar(off, n, rows=P):
            return AR[0:rows, off:off + n]

        QK = ar(0, 6144).rearrange("p (a s) -> p a s", a=12)
        VT = ar(6144, 3072).rearrange("p (c n) -> p c n", c=NC)
        PZ = ar(9216, 4096, PG).rearrange("p (a s) -> p a s", a=8)
        PB = ar(13312, 2048, PG).rearrange("p (b h s) -> p b h s", b=2, h=2)
        PINV = ar(15360, 64, PG).rearrange("p (g w) -> p g w", g=4)
        SBUFS = ar(9216, 2048).rearrange("p (b c k) -> p b c k", b=2, c=4)
        PTB = ar(11264, 2048).rearrange("p (b c k) -> p b c k", b=2, c=8)
        OT = ar(13312, 3072).rearrange("p (q g s) -> p q g s", q=2, g=3)
        BIAS = ar(16384, 2048)
        ST = ar(18432, 192).rearrange("p (c k) -> p c k", c=4)
        RW = ar(9216, 512, 48)
        EG = ar(9728, 1536).rearrange("p (g s) -> p g s", g=3)
        MN = ar(11264, 512)
        DG = ar(11776, 1536).rearrange("p (g s) -> p g s", g=3)
        MG = ar(0, 4096).rearrange("p (a s) -> p a s", a=8)
        SGP = ar(4096, 1024).rearrange("p (a s) -> p a s", a=2)
        SGA = ar(5120, 1024).rearrange("p (a s) -> p a s", a=2)
        T1 = ar(6144, 1024).rearrange("p (a s) -> p a s", a=2)
        T2 = ar(7168, 1024).rearrange("p (a s) -> p a s", a=2)
        XN = ar(0, 4096).rearrange("p (c n) -> p c n", c=NC)
        FT = ar(4096, 1024).rearrange("p (b s) -> p b s", b=2)
        RL = ar(5120, 2048).rearrange("p (b a s) -> p b a s", b=2, a=2)
        SQ = ar(7168, 2048).rearrange("p (b a s) -> p b a s", b=2, a=2)

        ACC = ar(9216, 6144)
        ADA = ar(15360, 4096).rearrange("p (b n) -> p b n", b=2)
        NFB = ar(19456, 1024)
        MROW = ar(5120, 4096, 1)
        V2 = ar(0, 4096).rearrange("p (c n) -> p c n", c=NC)
        G2 = ar(4096, 4096).rearrange("p (a s) -> p a s", a=8)
        RQK = ar(8192, 3072).rearrange("p (a s) -> p a s", a=6)
        HQ = ar(11264, 1536).rearrange("p (a s) -> p a s", a=3)
        HF = ar(12800, 1536).rearrange("p (a s) -> p a s", a=3)
        HK = ar(14336, 1536).rearrange("p (a s) -> p a s", a=3)
        PERM = ar(15360, 128)
        GQ, GK, GF = ar(15872, 512), ar(16384, 512), ar(16896, 512)
        TRG = ar(17408, 2048).rearrange("p (a s) -> p a s", a=4)
        SG = ar(17408, 2048).rearrange("p (b a s) -> p b a s", b=2, a=2)
        RT = ar(19456, 512)
        GA = ar(19456, 512, 16)
        COS, SINS = ar(19968, 512), ar(20480, 512)
        AB = ar(17408, 2560).rearrange("p (b n) -> p b n", b=2)
        DT = ar(19968, 512)
        SQT = ar(20480, 512)
        UB, PP = ar(8192, 512), ar(8704, 512)
        QKL = ar(9216, 1024).rearrange("p (b s) -> p b s", b=2)
        MASK = ar(10240, 1024).bitcast(U32).rearrange("p (l s) -> p l s", l=8)
        GMB = ar(17408, 1024)
        ROW_A, ROW_B, ROW_N = ar(4096, 1024), ar(5120, 1024), ar(6144, 1024)
        ROW_G, ROW_F = ar(7168, 1024), ar(8192, 1024)
        WR = ar(9216, KD * N_LOG)
        B_LOG = ar(9504, N_LOG)
        IOTA = ar(9568, 32)
        LG = ar(9728, 4 * N_LOG).rearrange("p (c n) -> p c n", c=NC)
        GPAD = ar(9872, 32).rearrange("p (c n) -> p c n", c=NC)
        GTOP = ar(9904, 32).rearrange("p (c n) -> p c n", c=NC)
        GTI = ar(9936, 32).bitcast(U32).rearrange("p (c n) -> p c n", c=NC)
        OHG = ar(9968, 16).rearrange("p (c n) -> p c n", c=NC)
        EIG = ar(9992, 128).rearrange("p (c g e) -> p c g e", c=NC, g=4)
        ELOG = ar(10120, 32).rearrange("p (c n) -> p c n", c=NC)
        ETOP = ar(10152, 32).rearrange("p (c n) -> p c n", c=NC)
        ETI = ar(10184, 32).bitcast(U32).rearrange("p (c n) -> p c n", c=NC)
        RS = ar(10216, 64).rearrange("p (x c) -> p x c", c=NC)
        OH = ar(10280, 256).rearrange("p (k c e) -> p k c e", k=2, c=NC)
        CMB = ar(10536, 128).rearrange("p (e c) -> p e c", e=N_EXP)
        CMC = ar(10664, 8).rearrange("p (b c) -> p b c", b=2)
        SGM = ar(10752, 1024).rearrange("p (m s) -> p m s", m=2)
        HR = ar(11776, 1024).rearrange("p (m s) -> p m s", m=2)
        OUTA = ar(12800, 4096).rearrange("p (c n) -> p c n", c=NC)
        TMPK = ar(18432, 1024).rearrange("p (b s) -> p b s", b=2)

        loaded = [sem("loaded0"), sem("loaded1")]
        hi_ready, lo_ready, unit_done = sem("hi_ready"), sem("lo_ready"), sem("unit_done")
        const_in = sem("const_in")
        stored = sem("stored")
        act_link, dve_link, pool_link = sem("act_link"), sem("dve_link"), sem("pool_link")
        z_out = sem("z_out")
        block = ctx.enter_context(nc.Block())

        class Link:
            def __init__(self, eng, s):
                self.eng, self.s, self.n = eng, s, 0

            def __call__(self, ins):
                self.n += 1
                ins.then_inc(self.s, 1)
                self.eng.wait_ge(self.s, self.n)

            def inc(self, ins):
                self.n += 1
                ins.then_inc(self.s, 1)

            def wait(self):
                self.eng.wait_ge(self.s, self.n)

        norm_sq = [sem(f"norm_sq{i}") for i in range(5)]
        norm_rs = [sem(f"norm_rs{i}") for i in range(5)]
        norm_xn = [sem(f"norm_xn{i}") for i in range(4)]
        norm_tr = [sem(f"norm_tr{i}") for i in range(4)]
        norm_ft = [sem(f"norm_ft{i}") for i in range(3)]
        norm_hi = [sem(f"norm_hi{i}") for i in range(4)]
        norm_lo = [sem(f"norm_lo{i}") for i in range(4)]

        def norm_act(act, j):
            for c in range(NC):
                act.activation(XN[:, c, :], X[:, c, :], ACT.Square, accum_out=SS[:, c:c + 1]).then_inc(norm_sq[j], 1)
            act.wait_ge(norm_rs[j], 2)
            for c in range(NC):
                act.activation(XN[:, c, :], X[:, c, :], ACT.Copy, scale=SS[:, 4 + c:5 + c]).then_inc(norm_xn[j], 1)
            for k in range(KD):
                act.wait_ge(norm_ft[j], k + 1)
                act.activation(UH[:, k, :], FT[:, k % 2, :], ACT.Copy).then_inc(norm_hi[j], 1)

        def norm_pool(pool, j):
            pool.wait_ge(norm_sq[j], NC)
            pool.tensor_scalar(SS[:, 0:4], SS[:, 0:4], 1.0 / D, EPS, ALU.mult, ALU.add).then_inc(norm_rs[j], 1)
            pool.wait_ge(norm_rs[j], 1)
            pool.tensor_tensor(SS[:, 4:8], SS[:, 0:4], COLS[:, 60:64], ALU.pow).then_inc(norm_rs[j], 1)
            for k in range(KD):
                pool.wait_ge(norm_hi[j], k + 1)
                pool.tensor_tensor(UL[:, k, :], FT[:, k % 2, :], UH[:, k, :].bitcast(F32), ALU.subtract).then_inc(norm_lo[j], 1)

        def norm_pe(pe, j):
            pe.wait_ge(norm_xn[j], NC)
            for k in range(KD):
                b = 4 + k % 4
                if k >= 4:
                    pe.wait_ge(norm_ft[j], k - 3)
                for c in range(NC):
                    last = pe.transpose(PS[:, b, c * P:(c + 1) * P], XN[:, c, k * P:(k + 1) * P], IDN[:, :])
                last.then_inc(norm_tr[j], 1)

        def norm_dve(dve, j, gain=None):
            for k in range(KD):
                dve.wait_ge(norm_tr[j], k + 1)
                if k >= 2:
                    dve.wait_ge(norm_lo[j], k - 1)
                if gain is not None:
                    dve.tensor_scalar(FT[:, k % 2, :], PS[:, 4 + k % 4, :], COLS[:, gain + k:gain + k + 1], None, ALU.mult).then_inc(norm_ft[j], 1)
                else:
                    dve.tensor_scalar(FT[:, k % 2, :], PS[:, 4 + k % 4, :], MODC[:, 8 + k:9 + k], MODC[:, k:k + 1],
                                      ALU.mult, ALU.add).then_inc(norm_ft[j], 1)

        def split_hi(act, base, i, s):
            act.wait_ge(loaded[1 - s], 16 * i + 16 * (base // 2 + s + 1))
            if not (isinstance(i, int) and base + 2 * i + s == 0):
                act.wait_ge(unit_done, 2 * i + base + s)
            act.activation(WH[:, 1 - s, :], RAW[:, 1 - s, :], ACT.Copy).then_inc(hi_ready, 1)

        def split_lo(dve, base, i, s):
            dve.wait_ge(hi_ready, 2 * i + base + s + 2)
            dve.tensor_tensor(WL[:, 1 - s, :], RAW[:, 1 - s, :], WH[:, 1 - s, :].bitcast(F32),
                              ALU.subtract).then_inc(lo_ready, 1)

        def unit_is_in(pe, n):
            pe.wait_ge(hi_ready, n + 1)
            pe.wait_ge(lo_ready, n + 1)

        def three(pe, out, a, b, start, stop):
            pe.matmul(out, a[0], b[0], start=start, stop=False)
            pe.matmul(out, a[0], b[1], start=False, stop=False)
            return pe.matmul(out, a[1], b[0], start=False, stop=stop)

        def wpair(slot, off, n, rows=P):
            return WH[0:rows, slot, off:off + n], WL[0:rows, slot, off:off + n]

        def feature(pe, slot, m, mw, width, src, bank, rows=P, kc=KD):
            for k in range(kc):
                last = three(pe, PS[0:mw, bank, :], wpair(slot, k * width + m * mw, mw, rows),
                             (src[0][0:rows, k, :], src[1][0:rows, k, :]), k == 0, k == kc - 1)
            return last

        def tokens(pe, slot, src, ks, bank, chunk, start, stop):
            for c in range(NC):
                for k in range(4):
                    last = three(pe, PS[:, bank + c, :], (src[0][:, ks + k, P * c:P * c + P], src[1][:, ks + k, P * c:P * c + P]),
                                 wpair(slot, 512 * k, 512), start and k == 0, stop and k == 3)
                if stop and c < NC - 1:
                    last.then_inc(chunk, 1)
            last.then_inc(unit_done, 1)

        def peeled(eng, count, body):
            body(0)
            with eng.Fori(1, count) as i:
                body(i)

        def rounds(eng, body):
            body(0)
            with eng.Fori(1, N_EXP // 2 - 1) as i:
                body(i)
            body(N_EXP // 2 - 1, True)

        def first(i):
            return isinstance(i, int) and i == 0

        U, V, AT = (UH, UL), (VH, VL), (ATH, ATL)

        pooled, pool_hi, pool_lo = sem("pooled"), sem("pool_hi"), sem("pool_lo")
        mix_out, mixed_hi, mixed_lo = [sem(x) for x in ("mix_out", "mixed_hi", "mixed_lo")]
        att_s, att_m, att_e, att_t, att_p, att_o, att_c = [
            sem("att_" + x) for x in ("scored", "maxed", "exped", "transposed", "copied", "summed", "out")]
        st_tr, st_row = sem("stat_tr"), sem("stat_row")
        nm_bc, l_bc, eg_d, eg_e, den_d, wsum, at_d, at_hi, at_lo = [sem(x) for x in (
            "max_bc", "sum_bc", "group_diff", "group_exp", "denominator", "weighted", "att_merged", "at_hi", "at_lo")]
        gp_sig, ga_sig, t1_d, t2_d, mg_d = [sem(x) for x in ("gp_sig", "ga_sig", "pool_gated", "att_gated", "branches")]
        mg_hi, mg_lo, wo_chunk, wo_add = sem("mg_hi"), sem("mg_lo"), sem("wo_chunk"), sem("wo_add")
        relu_d, sq_d, hid_hi, hid_lo, mo_chunk, mo_add = [sem(x) for x in (
            "relu_done", "square_done", "hid_hi", "hid_lo", "mo_chunk", "mo_add")]

        ada_in, ada_d, acc_init = [sem("ada_in0"), sem("ada_in1")], sem("ada_done"), sem("acc_init")
        b_in = sem("b_ada_in")
        ca_sig, ca_d, lb_sub, lb_exp, lb_d = [sem(x) for x in ("c_sigmoid", "c_done", "lb_diff", "lb_exp", "lb_done")]
        late_in, br_sq, br_rs, x2_d = sem("late_in"), sem("between_sq"), sem("between_rs"), sem("x2_done")
        mod_mm, modc_d, mrow_mm, mrow_d, mrow_out = [sem(x) for x in ("mod_cols_mm", "mod_cols_done", "mod_row_mm", "mod_row_done", "mod_row_out")]
        pos_in, trig_r, trig_d = sem("pos_in"), sem("trig_arg"), sem("trig_done")
        z2_out, gsig, g2_out = sem("z2_out"), sem("gate_sig"), sem("gate_out")
        perm_mm, rope_s, rope_c, rope_d = sem("perm_mm"), sem("rope_sin"), sem("rope_cos"), sem("rope_done")
        hsig, hq_d, hf_d = sem("h_sig"), sem("hq_done"), sem("hf_done")
        ga_mm, ga_x, ga_l, ga_m, ga_d = [sem(x) for x in ("ga_mm", "ga_sum", "ga_log", "ga_min", "ga_done")]
        d_in, ret_s, ret_a, ret_o = sem("decay_in"), sem("ret_scored"), sem("ret_decayed"), sem("ret_summed")
        mask_in, lvl_qk, lvl_s, lvl_a, lvl_b, pass_o = [sem(x) for x in (
            "mask_in", "level_qk", "level_scored", "level_diag", "level_off", "pass_summed")]
        a_zero, pass_h = sem("a_zero"), sem("pass_head")
        hn_sq, hn_mm, hn_rt, hn_d, hn_hi, hn_lo = [sem("head_" + x) for x in ("sq", "mean", "root", "gated", "hi", "lo")]
        gm_in, wo2_chunk, wo2_t, wo2_add = sem("gm_in"), sem("wo2_chunk"), sem("wo2_t"), sem("wo2_add")
        moe_in, wr_hi, wr_lo, h2_m, h2_d, lg_mm = [sem(x) for x in ("moe_in", "router_hi", "router_lo", "h2_scaled", "h2_done", "logits_mm")]
        rt_arg, rt_exp = sem("route_arg"), sem("route_exp")
        m_t, cmc_d = sem("expert_silu"), sem("expert_weight")
        m_sig, m_hid, m_hi, m_lo, dn_mm, dn_add = [sem("expert_" + x) for x in ("sig", "hid", "hi", "lo", "down", "added")]
        fin_x, fin_d = sem("final_x"), sem("final_done")

        heads = [(g, q, hh) for g in range(3) for q in range(2) for hh in range(2)]

        def blks(g):
            return [(0, 1)] + [(c, b) for c in range(1, 4) for b in range(2)] if g == 0 else [(c, 0) for c in range(4)]

        def st_col(g, q, hh):
            return (0, 32, 40)[g] + 2 * q + hh

        NCONST = 6

        @block.sync
        def _(sp):
            sp.dma_start(X[:, :, :], t["x"]).then_inc(const_in, 16)
            sp.dma_start(IDN[:, :], t["ident"]).then_inc(const_in, 16)
            sp.dma_start(COLS[:, :], t["cols"]).then_inc(const_in, 16)
            for s in range(2):
                sp.dma_start(RAW[:, s, :], t["w"][s, :, :]).then_inc(loaded[s], 16)
            sp.dma_start(PINV, t["pool_inv"]).then_inc(const_in, 16)
            sp.dma_start(BIAS, t["bias"]).then_inc(const_in, 16)
            sp.dma_start(ONESB[:, :], t["ones_block"]).then_inc(const_in, 16)
            sp.dma_start(NFB, t["norm_final_g"].partition_broadcast(P)).then_inc(late_in, 16)

            def stream(base, i, s):
                sp.wait_ge(hi_ready, 2 * i + base + s + 1)
                sp.wait_ge(lo_ready, 2 * i + base + s + 1)
                sp.dma_start(RAW[:, s, :], t["w"][bass.ds(2 * i + base + s + 2, 1), :, :].rearrange("o p n -> p (o n)")).then_inc(loaded[s], 16)
            with sp.Fori(0, (G0 - 2) // 2) as i:
                for s in range(2):
                    stream(0, i, s)

            def mlp(gi):
                for s in range(8):
                    stream(G0 - 2, 4 * gi + s // 2, s % 2)
                    if s < 6:
                        if first(gi) and s < 2:
                            sp.wait_ge(acc_init, 1)
                        else:
                            sp.wait_ge(ada_d, 6 * gi + s - 1)
                        sp.dma_start(ADA[:, s % 2, :], t["w_ada"][bass.ds(6 * gi + s, 1), :, :].rearrange("o p n -> p (o n)")).then_inc(ada_in[s % 2], 16)
            peeled(sp, 4, mlp)
            for n in range(H0, K0):
                stream(0, (n - 2) // 2, n % 2)
                if n == H0:
                    sp.wait_ge(ada_d, 24)
                    sp.dma_start(TRG[:, 0, :].bitcast(I32), t["positions"].partition_broadcast(P)).then_inc(pos_in, 16)
                    sp.wait_ge(mod_mm, 1)
                    sp.wait_ge(mrow_mm, 8)
                    sp.dma_start(PERM, t["perm"]).then_inc(pos_in, 16)
                    sp.wait_ge(mrow_d, 8)
                    sp.dma_start(t["mod_row"], MROW).then_inc(mrow_out, 16)
            stream(0, (K0 - 2) // 2, 0)
            stream(0, (K0 - 2) // 2, 1)
            for h in range(6):
                if h == 0:
                    sp.wait_ge(rope_d, 6)
                else:
                    sp.wait_ge(ret_a, h)
                sp.dma_start(DT, t["decay"][h, :, :]).then_inc(d_in, 16)
            sp.wait_ge(ret_o, 6)
            sp.dma_start(MASK, t["masks"].bitcast(U32)).then_inc(mask_in, 16)
            sp.wait_ge(pass_o, 5)
            sp.wait_ge(mrow_out, 16)
            sp.dma_start(GMB, t["mod_row"][0, 0:D].partition_broadcast(P)).then_inc(gm_in, 16)
            stream(0, K0 // 2, 0)
            stream(0, K0 // 2, 1)
            sp.wait_ge(hn_lo, 8)
            for r, row in ((1, ROW_B), (2, ROW_A), (3, ROW_G)):
                sp.dma_start(row, t["mod_row"][0, D * r:D * r + D].partition_broadcast(P)).then_inc(moe_in, 16)
            sp.dma_start(ROW_N, t["norm_ffn"].partition_broadcast(P)).then_inc(moe_in, 16)
            sp.dma_start(ROW_F, t["norm_final_2"].partition_broadcast(P)).then_inc(moe_in, 16)
            sp.dma_start(WR, t["w_router"]).then_inc(moe_in, 16)
            sp.dma_start(B_LOG, t["b_router"].partition_broadcast(P)).then_inc(moe_in, 16)
            sp.dma_start(IOTA, t["iota"]).then_inc(moe_in, 16)
            with sp.Fori(0, (N_UNITS - M0) // 2) as i:
                for s in range(2):
                    stream(M0 - 2, i, s)
            for c in range(NC):
                sp.wait_ge(fin_d, c + 1)
                sp.dma_start(t["out"][0, P * c:P * c + P, :], X[:, c, :]).then_inc(stored, 16)
            sp.wait_ge(stored, 16 * NC)

        def pt_copy(act, n):
            nb = len(blks(heads[n][0]))
            act.wait_ge(att_t, n + 1)
            if n >= 2:
                act.wait_ge(att_o, n - 1)
            act.activation(PTB[:, n % 2, 0:nb, :], PS[:, 4:6, :].rearrange("p b (c n) -> p (b c) n", c=4)[:, 0:nb, :],
                           ACT.Copy).then_inc(att_p, 1)

        def pair_out(act, n):
            g, q, hh = heads[n]
            if hh:
                act.wait_ge(att_o, n + 1)
                src = PS[:, 6 + (n // 2) % 2, :]
                dst = OT[:, q, g, :]
                if g:
                    src = src.rearrange("p (r i) -> p r i", r=4)
                    dst = dst.rearrange("p (i r) -> p r i", r=4)
                act.activation(dst, src, ACT.Copy).then_inc(att_c, 1)

        @block.scalar
        def _(act):
            act.wait_ge(const_in, 16 * NCONST)
            act.wait_ge(loaded[0], 16)
            act.activation(WH[:, 0, :], RAW[:, 0, :], ACT.Copy).then_inc(hi_ready, 1)
            norm_act(act, 0)
            for n in range(A0, B0):
                split_hi(act, 0, n // 2, n % 2)
                act.wait_ge(unit_done, n + 1)
                act.activation(PZ[:, 2 * n:2 * n + 2, :], PS[0:PG, 2 * (n % 2):2 * (n % 2) + 2, :], ACT.Copy).then_inc(z_out, 1)
            with act.Fori(0, NU_B // 2) as i:
                for s in range(2):
                    split_hi(act, B0, i, s)
                    act.wait_ge(unit_done, 2 * i + B0 + s + 1)
                    act.activation(QK[:, bass.ds(4 * i + 2 * s, 2), :], PS[:, 2 * s:2 * s + 2, :], ACT.Copy).then_inc(z_out, 1)
            for n in range(C0, D0):
                split_hi(act, 0, n // 2, n % 2)
                act.wait_ge(unit_done, n + 1)
                j = n - C0
                act.activation(VT[:, :, 256 * j:256 * j + 256],
                               PS[:, 2 * (n % 2):2 * (n % 2) + 2, :].rearrange("p b (c n) -> p (b c) n", c=2), ACT.Copy).then_inc(z_out, 1)
                if n == C0:
                    act.wait_ge(pooled, 1)
                    act.activation(VH[0:PG, :, :], PZ, ACT.Copy).then_inc(pool_hi, 1)
            split_hi(act, 0, D0 // 2, D0 % 2)
            act.wait_ge(unit_done, E0)
            for a in range(8):
                act.activation(PZ[:, a, :], PS[0:PG, a, :], ACT.Copy, scale=COLS[0:PG, 8 + a:9 + a]).then_inc(mix_out, 1)
            act.wait_ge(mix_out, 8)
            act.activation(VH[0:PG, :, :], PZ, ACT.Copy).then_inc(mixed_hi, 1)
            for n, (g, q, hh) in enumerate(heads):
                act.wait_ge(att_m, n + 1)
                w = 256 if g == 0 else P
                col = st_col(g, q, hh)
                for c in range(NC):
                    w0 = P if g == 0 and c == 0 else 0
                    act.activation(SBUFS[:, n % 2, c, w0:w], SBUFS[:, n % 2, c, w0:w], ACT.Exp,
                                   bias=ST[:, c, col:col + 1], accum_out=ST[:, c, col + 4:col + 5]).then_inc(att_e, 1)
                if n >= 1:
                    pt_copy(act, n - 1)
                if n >= 2:
                    pair_out(act, n - 2)
            pt_copy(act, 11)
            pair_out(act, 11)
            for q in range(2):
                act.wait_ge(eg_d, 3 * (q + 1))
                act.activation(EG, EG, ACT.Exp).then_inc(eg_e, 1)
                act.wait_ge(at_d, q + 1)
                act.activation(ATH[:, q, :], MN, ACT.Copy).then_inc(at_hi, 1)

            def branches(j):
                for s in range(4):
                    split_hi(act, E0, 2 * j + s // 2, s % 2)
                    if s == 0:
                        act.wait_ge(unit_done, 4 * j + E0 + 1)
                        if not first(j):
                            act.wait_ge(t1_d, j)
                        act.activation(SGP, PS[:, 0:2, :], ACT.Sigmoid).then_inc(gp_sig, 1)
                    if s == 2:
                        act.wait_ge(unit_done, 4 * j + E0 + 3)
                        if not first(j):
                            act.wait_ge(t2_d, j)
                        act.activation(SGA, PS[:, 4:6, :], ACT.Sigmoid).then_inc(ga_sig, 1)
            peeled(act, 4, branches)
            act.activation(CA[:, :], COLS[:, 24:32], ACT.Sigmoid).then_inc(ca_sig, 1)
            act.wait_ge(mg_d, 4)
            for k in range(KD):
                act.activation(UH[:, k, :], MG[:, k, :], ACT.Copy).then_inc(mg_hi, 1)
            for n in range(F0, G0):
                split_hi(act, 0, n // 2, n % 2)
            act.wait_ge(wo_add, 8)
            norm_act(act, 1)

            def mlp(gi):
                for s in range(8):
                    split_hi(act, G0, 4 * gi + s // 2, s % 2)
                    if s < 4:
                        act.wait_ge(unit_done, 8 * gi + G0 + s + 1)
                        act.activation(RL[:, s % 2, :, :], PS[:, 2 * (s % 2):2 * (s % 2) + 2, :], ACT.Relu).then_inc(relu_d, 1)
                        act.wait_ge(sq_d, 4 * gi + s + 1)
                        act.activation(VH[:, 2 * s:2 * s + 2, :], SQ[:, s % 2, :, :], ACT.Copy).then_inc(hid_hi, 1)
            with act.Fori(0, 4) as gi:
                mlp(gi)

            for c in range(NC):
                act.wait_ge(mo_add, 32)
                act.activation(XN[:, c, :], X[:, c, :], ACT.Square, accum_out=SS[:, c:c + 1]).then_inc(br_sq, 1)
            act.wait_ge(x2_d, 4)
            norm_act(act, 2)
            act.wait_ge(lb_sub, 1)
            act.activation(LBS[:, 3:6], LBS[:, 0:3], ACT.Exp).then_inc(lb_exp, 1)
            act.wait_ge(trig_r, 2)
            act.activation(SINS, TRG[:, 2, :], ACT.Sin, scale=COLS[:, 53:54]).then_inc(trig_d, 1)
            act.activation(COS, TRG[:, 3, :], ACT.Sin).then_inc(trig_d, 1)
            for n in range(H0, I0):
                split_hi(act, 0, n // 2, n % 2)
                act.wait_ge(unit_done, n + 1)
                j = n - H0
                act.activation(V2[:, :, 256 * j:256 * j + 256],
                               PS[:, 2 * (n % 2):2 * (n % 2) + 2, :].rearrange("p b (c n) -> p (b c) n", c=2), ACT.Copy).then_inc(z2_out, 1)
            act.wait_ge(trig_d, 2)
            for n in range(I0, J0):
                split_hi(act, 0, n // 2, n % 2)
                act.wait_ge(unit_done, n + 1)
                if n >= I0 + 2:
                    act.wait_ge(g2_out, n - I0 - 1)
                act.activation(SG[:, n % 2, :, :], PS[:, 2 * (n % 2):2 * (n % 2) + 2, :], ACT.Sigmoid).then_inc(gsig, 1)
            for n in range(J0, J0 + 3):
                split_hi(act, 0, n // 2, n % 2)
                act.wait_ge(unit_done, n + 1)
                j = n - J0
                act.activation(RQK[:, 2 * j:2 * j + 2, :], PS[:, 2 * (n % 2):2 * (n % 2) + 2, :], ACT.Copy).then_inc(z2_out, 1)
            for n in range(J0 + 3, J0 + 6):
                split_hi(act, 0, n // 2, n % 2)
                act.wait_ge(unit_done, n + 1)
                j = n - J0 - 3
                act.wait_ge(g2_out, 4)
                if j == 2:
                    act.wait_ge(hf_d, 3)
                act.activation(SG[:, n % 2, :, :], PS[:, 2 * (n % 2):2 * (n % 2) + 2, :], ACT.Sigmoid).then_inc(hsig, 1)
                if j == 2:
                    act.wait_ge(perm_mm, 6)
                act.activation(HK[:, j, :], PS[:, 2 * (n % 2) + 1, :], ACT.Sigmoid, scale=-1.0).then_inc(hsig, 1)
            n = J0 + 6
            split_hi(act, 0, n // 2, n % 2)
            act.wait_ge(unit_done, n + 1)
            act.activation(GQ, PS[:, 0, :], ACT.Copy, scale=float(np.float32(32.0 ** -0.5))).then_inc(z2_out, 1)
            act.activation(GK, PS[:, 1, :], ACT.Copy).then_inc(z2_out, 1)
            n = J0 + 7
            split_hi(act, 0, n // 2, n % 2)
            act.wait_ge(ga_mm, 1)
            act.wait_ge(rope_d, 6)
            act.activation(GA, PS[0:16, 2, :], ACT.Copy).then_inc(z2_out, 1)
            act.wait_ge(unit_done, n + 1)
            act.wait_ge(hf_d, 9)
            act.activation(TRG[:, 0, :], PS[:, 3, :], ACT.Identity, bias=COLS[:, 51:52]).then_inc(ga_x, 1)
            act.wait_ge(ga_x, 1)
            act.activation(TRG[:, 1, :], TRG[:, 0, :], ACT.Abs).then_inc(ga_l, 1)
            act.wait_ge(ga_l, 1)
            act.activation(TRG[:, 1, :], TRG[:, 1, :], ACT.Exp, scale=-1.0).then_inc(ga_l, 1)
            act.wait_ge(ga_l, 2)
            act.activation(TRG[:, 1, :], TRG[:, 1, :], ACT.Ln, bias=1.0).then_inc(ga_l, 1)
            act.wait_ge(ga_m, 1)
            act.activation(GF, TRG[:, 2, :], ACT.Exp, scale=1.0 / 16.0).then_inc(ga_d, 1)

            def head_norm(tile):
                act.wait_ge(ret_o, 2 * tile + 2) if tile < 3 else act.wait_ge(pass_o, tile - 2)
                if tile:
                    act.wait_ge(hn_d, 3 * tile)
                act.activation(SQT, PS[:, 6, :], ACT.Square).then_inc(hn_sq, 1)
                act.wait_ge(hn_mm, tile + 1)
                act.activation(SQT, PS[:, 7, :], ACT.Sqrt, bias=COLS[:, 58:59]).then_inc(hn_rt, 1)
                act.wait_ge(hn_d, 3 * tile + 3)
                act.activation(VH[:, tile, :], G2[:, tile, :], ACT.Copy).then_inc(hn_hi, 1)
            for tile in range(3):
                head_norm(tile)
            for p in range(5):
                if p == 0:
                    act.wait_ge(ret_o, 6)
                for lev in (7, 8):
                    for hh in range(2):
                        cnt = 20 * p + 2 * (lev + 1) + hh
                        act.wait_ge(lvl_s, cnt + 1)
                        if p and lev == 7:
                            act.wait_ge(pass_o, p)
                        b = cnt % 6
                        if lev == 7:
                            act.activation(AB[:, hh, 512:640], PS[:, b, 0:128], ACT.Copy).then_inc(lvl_b, 1)
                            act.activation(AB[:, hh, 1152:1280], PS[:, b, 128:256], ACT.Copy).then_inc(lvl_b, 1)
                        else:
                            act.activation(AB[:, hh, 640:896], PS[:, b, 0:256], ACT.Copy).then_inc(lvl_b, 1)
                            act.activation(AB[:, hh, 896:1152], PS[:, b, 256:512], ACT.Copy).then_inc(lvl_b, 1)
                head_norm(3 + p)
            for n in range(K0, M0):
                split_hi(act, 0, n // 2, n % 2)
            act.wait_ge(wo2_add, 8)
            for c in range(NC):
                act.activation(XN[:, c, :], X[:, c, :], ACT.Square, accum_out=SS[:, c:c + 1]).then_inc(norm_sq[3], 1)
            act.wait_ge(moe_in, 128)
            act.activation(ATH[:, 0, 0:KD * N_LOG], WR, ACT.Copy).then_inc(wr_hi, 1)
            act.wait_ge(norm_rs[3], 2)
            for c in range(NC):
                act.activation(XN[:, c, :], X[:, c, :], ACT.Copy, scale=SS[:, 4 + c:5 + c]).then_inc(norm_xn[3], 1)
            for k in range(KD):
                act.wait_ge(norm_tr[3], k + 1)
                act.activation(UH[:, k, :], PS[:, 4 + k % 4, :], ACT.Copy).then_inc(norm_hi[3], 1)
            act.wait_ge(rt_arg, 1)
            act.activation(RS[:, 4:8, :], RS[:, 0:4, :], ACT.Exp).then_inc(rt_exp, 1)
            act.wait_ge(rt_arg, 2)
            act.activation(RS[:, 9, :], RS[:, 8, :], ACT.Exp).then_inc(rt_exp, 1)

            def experts(i, last=False):
                for s in range(6):
                    e, n = 2 * i + s // 3, 6 * i + M0 + s
                    if not (last and s == 5):
                        split_hi(act, M0, 3 * i + s // 2, s % 2)
                    if s % 3 == 0:
                        act.wait_ge(unit_done, n + 1)
                        for m in range(2):
                            if not (first(i) and s < 3):
                                act.wait_ge(m_hid, 2 * e)
                            act.activation(SGM[:, m, :], PS[:, m, :], ACT.Sigmoid).then_inc(m_sig, 1)
                    elif s % 3 == 1:
                        for m in range(2):
                            act.wait_ge(m_hid, 2 * e + m + 1)
                            act.activation(VH[:, 2 * (s // 3) + m, :], HR[:, m, :], ACT.Copy).then_inc(m_hi, 1)
            rounds(act, experts)
            act.wait_ge(fin_x, NC)
            for c in range(NC):
                act.activation(XN[:, c, :], X[:, c, :], ACT.Square, accum_out=SS[:, c:c + 1]).then_inc(norm_sq[4], 1)
        @block.vector
        def _(dve):
            link = Link(dve, dve_link)
            dve.wait_ge(const_in, 16 * NCONST)
            dve.wait_ge(hi_ready, 1)
            dve.tensor_tensor(WL[:, 0, :], RAW[:, 0, :], WH[:, 0, :].bitcast(F32), ALU.subtract).then_inc(lo_ready, 1)
            norm_dve(dve, 0, 0)
            for n in range(A0, B0):
                split_lo(dve, 0, n // 2, n % 2)
            with dve.Fori(0, NU_B // 2) as i:
                for s in range(2):
                    split_lo(dve, B0, i, s)
            for n in range(C0, D0):
                split_lo(dve, 0, n // 2, n % 2)
                if n == C0:
                    dve.wait_ge(pool_hi, 1)
                    dve.tensor_tensor(VL[0:PG, :, :], PZ, VH[0:PG, :, :].bitcast(F32), ALU.subtract).then_inc(pool_lo, 1)
            split_lo(dve, 0, D0 // 2, D0 % 2)
            dve.wait_ge(mixed_hi, 1)
            dve.tensor_tensor(VL[0:PG, :, :], PZ, VH[0:PG, :, :].bitcast(F32), ALU.subtract).then_inc(mixed_lo, 1)
            dve.wait_ge(mixed_lo, 1)
            link.inc(dve.memset(SBUFS[:, :, 0, 0:P], NEG))
            link(dve.memset(ST, 0.0))
            for n, (g, q, hh) in enumerate(heads):
                dve.wait_ge(att_s, n + 1)
                if n >= 2:
                    dve.wait_ge(att_t, n - 1)
                b = 2 * (n % 2)
                hd = 2 * q + hh
                if g == 0:
                    tab = BIAS[:, 256 * hd:256 * hd + 256]
                    link.inc(dve.scalar_tensor_tensor(SBUFS[:, n % 2, 0, P:2 * P], PS[:, b, P:2 * P], 0.125, tab[:, P:2 * P], ALU.mult, ALU.add))
                    link(dve.scalar_tensor_tensor(SBUFS[:, n % 2, 1:4, :],
                                                  PS[:, b:b + 2, :].rearrange("p b (c n) -> p (b c) n", c=2)[:, 1:4, :], 0.125,
                                                  tab.unsqueeze(1).broadcast_to([P, 3, 256]), ALU.mult, ALU.add))
                    w = 256
                else:
                    o = 1024 + 512 * (g - 1) + P * hd
                    link(dve.scalar_tensor_tensor(SBUFS[:, n % 2, :, 0:P], PS[:, b, :].rearrange("p (c n) -> p c n", c=4), 0.125,
                                                  BIAS[:, o:o + P].unsqueeze(1).broadcast_to([P, 4, P]), ALU.mult, ALU.add))
                    w = P
                col = st_col(g, q, hh)
                dve.tensor_reduce(ST[:, :, col:col + 1], SBUFS[:, n % 2, :, 0:w], AX.X, ALU.max, negate=True).then_inc(att_m, 1)
            dve.wait_ge(st_tr, 1)
            dve.tensor_copy(RW[0:32, :], PS[0:32, 0, :]).then_inc(st_row, 1)
            dve.tensor_copy(RW[32:48, :].rearrange("p (i r) -> p r i", r=4), PS[32:48, 0, :].rearrange("p (r i) -> p r i", r=4)).then_inc(st_row, 1)
            for q in range(2):
                dve.wait_ge(nm_bc, q + 1)
                if q:
                    dve.wait_ge(at_lo, 1)
                link(dve.tensor_copy(MN, PS[:, 1, :]))
                link(dve.tensor_tensor(MN, MN, PS[:, 2, :], ALU.min))
                link(dve.tensor_tensor(MN, MN, PS[:, 3, :], ALU.min))
                if q:
                    dve.wait_ge(wsum, 3)
                for g in range(3):
                    dve.tensor_tensor(EG[:, g, :], MN, PS[:, 1 + g, :], ALU.subtract).then_inc(eg_d, 1)
                dve.wait_ge(eg_e, q + 1)
                dve.wait_ge(l_bc, q + 1)
                dve.tensor_tensor(DG, EG, PS[:, 4:7, :], ALU.mult).then_inc(den_d, 1)
                dve.wait_ge(den_d, q + 1)
                link(dve.tensor_tensor(MN, DG[:, 0, :], DG[:, 1, :], ALU.add))
                link(dve.tensor_tensor(MN, MN, DG[:, 2, :], ALU.add))
                link(dve.reciprocal(MN, MN))
                dve.wait_ge(wsum, 3 * (q + 1))
                dve.tensor_tensor(MN, MN, OT[:, q, 0, :], ALU.mult).then_inc(at_d, 1)
                dve.wait_ge(at_hi, q + 1)
                dve.tensor_tensor(ATL[:, q, :], MN, ATH[:, q, :].bitcast(F32), ALU.subtract).then_inc(at_lo, 1)

            def branches(j):
                for s in range(4):
                    split_lo(dve, E0, 2 * j + s // 2, s % 2)
                    if s == 1:
                        dve.wait_ge(unit_done, 4 * j + E0 + 2)
                        dve.wait_ge(gp_sig, j + 1)
                        if not first(j):
                            dve.wait_ge(mg_d, j)
                        dve.tensor_tensor(T1, SGP, PS[:, 2:4, :], ALU.mult).then_inc(t1_d, 1)
                    if s == 3:
                        dve.wait_ge(unit_done, 4 * j + E0 + 4)
                        dve.wait_ge(ga_sig, j + 1)
                        dve.tensor_tensor(T2, SGA, PS[:, 6:8, :], ALU.mult).then_inc(t2_d, 1)
            peeled(dve, 4, branches)
            for k in range(KD):
                dve.wait_ge(mg_hi, k + 1)
                dve.tensor_tensor(UL[:, k, :], MG[:, k, :], UH[:, k, :].bitcast(F32), ALU.subtract).then_inc(mg_lo, 1)
            for n in range(F0, G0):
                split_lo(dve, 0, n // 2, n % 2)
                if n % 2:
                    h = (n - F0) // 2
                    for c in range(NC):
                        if c < 3:
                            dve.wait_ge(wo_chunk, 3 * h + c + 1)
                        else:
                            dve.wait_ge(unit_done, n + 1)
                        xs = X[:, c, HALF * h:HALF * h + HALF]
                        dve.tensor_tensor(xs, xs, PS[:, 4 * h + c, :], ALU.add).then_inc(wo_add, 1)
            dve.wait_ge(ca_sig, 1)
            dve.tensor_tensor(CA[:, :], CA[:, :], COLS[:, 24:32], ALU.mult).then_inc(ca_d, 1)
            norm_dve(dve, 1, 16)
            dve.wait_ge(ca_d, 1)

            def mlp(gi):
                for s in range(8):
                    split_lo(dve, G0, 4 * gi + s // 2, s % 2)
                    if s < 4:
                        dve.wait_ge(relu_d, 4 * gi + s + 1)
                        if s >= 2 or not first(gi):
                            dve.wait_ge(hid_lo, 4 * gi + s - 1)
                        dve.scalar_tensor_tensor(SQ[:, s % 2, :, :], PS[:, 2 * (s % 2):2 * (s % 2) + 2, :], 0.0, RL[:, s % 2, :, :],
                                                 ALU.max, ALU.mult).then_inc(sq_d, 1)
                    if s < 6:
                        dve.wait_ge(ada_in[s % 2], 48 * gi + 16 * (s // 2 + 1))
                        if first(gi) and s < 3:
                            dve.wait_ge(b_in, 16)
                        else:
                            dve.wait_ge(ada_d, 6 * gi + s - 2)
                        part = ACC[:, UNIT * (s % 3):UNIT * (s % 3) + UNIT]
                        dve.scalar_tensor_tensor(part, ADA[:, s % 2, :], CA[:, bass.ds(2 * gi + s // 3, 1)], part,
                                                 ALU.mult, ALU.add).then_inc(ada_d, 1)
                    if s in (5, 7):
                        h = (s - 5) // 2
                        for c in range(NC):
                            if c < 3:
                                dve.wait_ge(mo_chunk, 6 * gi + 3 * h + c + 1)
                            else:
                                dve.wait_ge(unit_done, 8 * gi + G0 + s + 1)
                            xs = X[:, c, HALF * h:HALF * h + HALF]
                            dve.tensor_tensor(xs, xs, PS[:, 4 * (1 - h) + c, :], ALU.add).then_inc(mo_add, 1)
            peeled(dve, 4, mlp)

            link(dve.tensor_tensor(LBS[:, 0:3], COLS[:, 32:35], COLS[:, 32:35], ALU.subtract))
            dve.tensor_copy(LBS[:, 6:9], LBS[:, 0:3]).then_inc(lb_sub, 1)
            dve.wait_ge(mod_mm, 1)
            link.inc(dve.tensor_copy(MODC[:, 0:8], PS[:, 0, 0:8]))
            link(dve.scalar_tensor_tensor(MODC[:, 8:16], PS[:, 0, 8:16], 1.0, COLS[:, 43:51], ALU.add, ALU.mult))
            for r in range(8):
                dve.wait_ge(mrow_mm, r + 1)
                dve.tensor_copy(MROW[:, 512 * r:512 * r + 512], PS[0:1, 1 + r % 3, :]).then_inc(mrow_d, 1)
            dve.wait_ge(late_in, 16)
            dve.wait_ge(br_rs, 2)
            for c in range(NC):
                dve.scalar_tensor_tensor(X[:, c, :], X[:, c, :], SS[:, 4 + c:5 + c], NFB, ALU.mult, ALU.mult).then_inc(x2_d, 1)
            norm_dve(dve, 2)
            dve.wait_ge(lb_exp, 1)
            link(dve.reciprocal(LBS[:, 6:9], LBS[:, 3:6]))
            link(dve.tensor_tensor(LBS[:, 3:6], LBS[:, 3:6], LBS[:, 6:9], ALU.mult))
            link(dve.tensor_tensor(LBS[:, 0:3], LBS[:, 3:6], LBS[:, 3:6], ALU.subtract))
            dve.tensor_scalar(LBS[:, 9:12], LBS[:, 0:3], -1.0, 1.0, ALU.mult, ALU.add).then_inc(lb_d, 1)
            dve.wait_ge(pos_in, 32)
            link(dve.tensor_copy(TRG[:, 1, :], TRG[:, 0, :].bitcast(I32)))
            link(dve.tensor_scalar(TRG[:, 1, :], TRG[:, 1, :], COLS[:, 52:53], None, ALU.mult))
            for k, quarter in ((2, 0.0), (3, 0.25)):
                if k == 2:
                    dve.wait_ge(x2_d, 4)
                link(dve.tensor_scalar(TRG[:, 0, :].bitcast(I32), TRG[:, 1, :], 1.0 / TWO_PI, quarter, ALU.mult, ALU.add))
                link(dve.tensor_copy(RT, TRG[:, 0, :].bitcast(I32)))
                link(dve.scalar_tensor_tensor(TRG[:, k, :], RT, -TURN[0], TRG[:, 1, :], ALU.mult, ALU.add))
                link(dve.scalar_tensor_tensor(TRG[:, k, :], RT, -TURN[1], TRG[:, k, :], ALU.mult, ALU.add))
                link(dve.scalar_tensor_tensor(TRG[:, k, :], RT, -TURN[2], TRG[:, k, :], ALU.mult, ALU.add))
                if quarter:
                    link(dve.tensor_scalar(TRG[:, k, :], TRG[:, k, :], TWO_PI / 4, None, ALU.add))
                dve.tensor_scalar(TRG[:, k, :], TRG[:, k, :], PI_IN, -PI_IN, ALU.min, ALU.max).then_inc(trig_r, 1)
            for n in range(H0, J0 + 3):
                split_lo(dve, 0, n // 2, n % 2)
                if I0 <= n < J0:
                    dve.wait_ge(gsig, n - I0 + 1)
                    if n == I0:
                        dve.wait_ge(mrow_out, 16)
                    for m in range(2):
                        tile = 2 * (n - I0) + m
                        ins = dve.scalar_tensor_tensor(G2[:, tile, :], PS[:, 2 * (n % 2) + m, :], COLS[:, 35 + tile:36 + tile],
                                                       SG[:, n % 2, m, :], ALU.mult, ALU.mult)
                        if m:
                            ins.then_inc(g2_out, 1)
                        else:
                            link.inc(ins)
            for n in range(J0 + 3, J0 + 6):
                j = n - J0 - 3
                split_lo(dve, 0, n // 2, n % 2)
                for a in (2 * j, 2 * j + 1):
                    dve.wait_ge(perm_mm, a + 1)
                    if a:
                        dve.wait_ge(rope_d, a)
                    dve.tensor_tensor(RT, PS[:, 4 + a % 4, :], SINS, ALU.mult).then_inc(rope_s, 1)
                dve.wait_ge(hsig, 2 * j + 1)
                dve.scalar_tensor_tensor(HQ[:, j, :], PS[:, 2 * (n % 2), :], 0.125, SG[:, n % 2, 0, :], ALU.mult, ALU.mult).then_inc(hq_d, 1)
            split_lo(dve, 0, (J0 + 6) // 2, 0)
            split_lo(dve, 0, (J0 + 7) // 2, 1)
            dve.wait_ge(ga_l, 3)
            dve.scalar_tensor_tensor(TRG[:, 2, :], TRG[:, 0, :], 0.0, TRG[:, 1, :], ALU.min, ALU.subtract).then_inc(ga_m, 1)

            def head_norm(tile):
                dve.wait_ge(hn_rt, tile + 1)
                dve.reciprocal(SQT, SQT).then_inc(hn_d, 1)
                dve.wait_ge(hn_d, 3 * tile + 1)
                dve.tensor_tensor(SQT, SQT, PS[:, 6, :], ALU.mult).then_inc(hn_d, 1)
                dve.wait_ge(hn_d, 3 * tile + 2)
                dve.tensor_tensor(G2[:, tile, :], G2[:, tile, :], SQT, ALU.mult).then_inc(hn_d, 1)
            dve.wait_ge(ga_d, 1)
            for h in range(6):
                b = 3 * (h % 2)
                dve.wait_ge(ret_s, h + 1)
                dve.wait_ge(d_in, 16 * (h + 1))
                if h >= 2:
                    dve.wait_ge(ret_o, h - 1)
                A = AB[:, h % 2, :]
                link.inc(dve.tensor_tensor(A[:, 0:512].rearrange("p (c s) -> p c s", c=4), PS[:, b, :].rearrange("p (c s) -> p c s", c=4),
                                           DT[:, 0:P].unsqueeze(1).broadcast_to([P, 4, P]), ALU.mult))
                link.inc(dve.tensor_tensor(A[:, 512:896], PS[:, b + 1, 0:384], DT[:, P:512], ALU.mult))
                link.inc(dve.tensor_tensor(A[:, 1152:1280], PS[:, b + 1, 384:512], DT[:, P:256], ALU.mult))
                link.wait()
                dve.tensor_tensor(A[:, 896:1152], PS[:, b + 2, 0:256], DT[:, P:384], ALU.mult).then_inc(ret_a, 1)
                if h % 2:
                    head_norm(h // 2)
            dve.wait_ge(ret_o, 6)
            dve.memset(AB[:, :, 0:512], 0.0).then_inc(a_zero, 1)
            dve.wait_ge(a_zero, 1)
            dve.wait_ge(mask_in, 16)
            for p in range(5):
                for lev in range(-1, 7):
                    for hh in range(2):
                        cnt = 20 * p + 2 * (lev + 1) + hh
                        dve.wait_ge(lvl_s, cnt + 1)
                        if p and lev == -1:
                            dve.wait_ge(pass_o, p)
                        dve.copy_predicated(AB[:, hh, 0:512].rearrange("p (c s) -> p c s", c=4),
                                            MASK[:, lev + 1, :].unsqueeze(1).broadcast_to([P, 4, P]),
                                            PS[:, cnt % 6, :].rearrange("p (c s) -> p c s", c=4)).then_inc(lvl_a, 1)
                        dve.wait_ge(lvl_a, 16 * p + 2 * (lev + 1) + hh + 1)
                head_norm(3 + p)
            for n in range(K0, M0):
                split_lo(dve, 0, n // 2, n % 2)
                if n % 2:
                    h = (n - K0) // 2
                    dve.wait_ge(gm_in, 16)
                    for c in range(NC):
                        if c < 3:
                            dve.wait_ge(wo2_chunk, 3 * h + c + 1)
                        else:
                            dve.wait_ge(unit_done, n + 1)
                        x = 4 * h + c
                        if x >= 2:
                            dve.wait_ge(wo2_add, x - 1)
                        dve.tensor_tensor(TMPK[:, x % 2, :], PS[:, 4 * h + c, :], GMB[:, HALF * h:HALF * h + HALF], ALU.mult).then_inc(wo2_t, 1)
            dve.wait_ge(moe_in, 128)
            link(dve.scalar_tensor_tensor(ROW_A, ROW_A, 1.0, ROW_N, ALU.add, ALU.mult))
            for c in range(NC):
                dve.wait_ge(norm_xn[3], c + 1)
                dve.tensor_tensor(XN[:, c, :], XN[:, c, :], ROW_A, ALU.mult).then_inc(h2_m, 1)
            link.inc(dve.memset(OUTA, 0.0))
            link.inc(dve.memset(GPAD, NEG))
            for k in range(KD):
                dve.wait_ge(norm_hi[3], k + 1)
                dve.tensor_tensor(UL[:, k, :], PS[:, 4 + k % 4, :], UH[:, k, :].bitcast(F32), ALU.subtract).then_inc(norm_lo[3], 1)
            dve.wait_ge(lg_mm, 1)
            link(dve.tensor_tensor(LG, PS[:, 0, 0:256].rearrange("p (c n) -> p c n", c=4)[:, :, 0:N_LOG],
                                   B_LOG.unsqueeze(1).broadcast_to([P, NC, N_LOG]), ALU.add))
            link(dve.tensor_copy(GPAD[:, :, 0:4], LG[:, :, 0:4]))
            for c in range(NC):
                link.inc(dve.max(GTOP[:, c, :], GPAD[:, c, :]))
            link.wait()
            for c in range(NC):
                link.inc(dve.max_index(GTI[:, c, :], GTOP[:, c, :], GPAD[:, c, :]))
            dve.tensor_tensor(RS[:, 0:4, :].rearrange("p g c -> p c g"), LG[:, :, 0:4], GTOP[:, :, 0:1].broadcast_to([P, NC, 4]), ALU.subtract).then_inc(rt_arg, 1)
            link.wait()
            link(dve.tensor_copy(RS[:, 10, :], GTI[:, :, 0]))
            link(dve.tensor_tensor(OHG, IOTA[:, 0:4].unsqueeze(1).broadcast_to([P, NC, 4]), RS[:, 10, :].unsqueeze(2).broadcast_to([P, NC, 4]), ALU.is_equal))
            link(dve.tensor_tensor(EIG, LG[:, :, 4:N_LOG].rearrange("p c (g e) -> p c g e", g=4), OHG.unsqueeze(3).broadcast_to([P, NC, 4, 8]), ALU.mult))
            link(dve.tensor_reduce(ELOG, EIG.rearrange("p c g e -> p c e g"), AX.X, ALU.add))
            for c in range(NC):
                link.inc(dve.max(ETOP[:, c, :], ELOG[:, c, :]))
            link.wait()
            for c in range(NC):
                link.inc(dve.max_index(ETI[:, c, :], ETOP[:, c, :], ELOG[:, c, :]))
            dve.tensor_tensor(RS[:, 8, :], ETOP[:, :, 1], ETOP[:, :, 0], ALU.subtract).then_inc(rt_arg, 1)
            link.wait()
            for k in range(2):
                link(dve.tensor_copy(RS[:, 11 + k, :], ETI[:, :, k]))
                link(dve.scalar_tensor_tensor(RS[:, 11 + k, :], RS[:, 10, :], 8.0, RS[:, 11 + k, :], ALU.mult, ALU.add))
                link(dve.tensor_tensor(OH[:, k, :, :], IOTA.unsqueeze(1).broadcast_to([P, NC, N_EXP]), RS[:, 11 + k, :].unsqueeze(2).broadcast_to([P, NC, N_EXP]), ALU.is_equal))
            dve.wait_ge(rt_exp, 1)
            link(dve.tensor_reduce(RS[:, 13, :], RS[:, 4:8, :].rearrange("p g c -> p c g"), AX.X, ALU.add))
            dve.wait_ge(rt_exp, 2)
            link(dve.tensor_scalar(RS[:, 10, :], RS[:, 9, :], 1.0, None, ALU.add))
            link(dve.tensor_tensor(RS[:, 13, :], RS[:, 13, :], RS[:, 10, :], ALU.mult))
            link(dve.reciprocal(RS[:, 14, :], RS[:, 13, :]))
            link(dve.tensor_tensor(RS[:, 15, :], RS[:, 14, :], RS[:, 9, :], ALU.mult))
            for k in range(2):
                link(dve.tensor_tensor(OH[:, k, :, :], OH[:, k, :, :], RS[:, 14 + k, :].unsqueeze(2).broadcast_to([P, NC, N_EXP]), ALU.mult))
            link(dve.tensor_tensor(CMB.rearrange("p e c -> p c e"), OH[:, 0, :, :], OH[:, 1, :, :], ALU.add))

            def experts(i, last=False):
                for s in range(6):
                    x, e, n = s // 3, 2 * i + s // 3, 6 * i + M0 + s
                    if not (last and s == 5):
                        split_lo(dve, M0, 3 * i + s // 2, s % 2)
                    if s % 3 == 0:
                        for m in range(2):
                            dve.wait_ge(m_sig, 2 * e + m + 1)
                            dve.tensor_tensor(SGM[:, m, :], SGM[:, m, :], PS[:, m, :], ALU.mult).then_inc(m_t, 1)
                    elif s % 3 == 1:
                        dve.wait_ge(unit_done, n + 1)
                        dve.wait_ge(m_t, 2 * e + 2)
                        for m in range(2):
                            dve.tensor_tensor(HR[:, m, :], SGM[:, m, :], PS[:, 2 + m, :], ALU.mult).then_inc(m_hid, 1)
                        for m in range(2):
                            dve.wait_ge(m_hi, 2 * e + m + 1)
                            dve.tensor_tensor(VL[:, 2 * x + m, :], HR[:, m, :], VH[:, 2 * x + m, :].bitcast(F32), ALU.subtract).then_inc(m_lo, 1)
                    else:
                        dve.tensor_copy(CMC[:, x, :], CMB[:, bass.ds(e, 1), :].rearrange("p o c -> p (o c)")).then_inc(cmc_d, 1)
                        dve.wait_ge(cmc_d, e + 1)
                        for j in range(8):
                            c, h = j // 2, j % 2
                            if j < 7:
                                dve.wait_ge(dn_mm, 7 * e + j + 1)
                            else:
                                dve.wait_ge(unit_done, n + 1)
                            if not (first(i) and x == 0):
                                dve.wait_ge(dn_add, 8 * e + j - 7)
                            acc = OUTA[:, c, HALF * h:HALF * h + HALF]
                            dve.scalar_tensor_tensor(acc, PS[:, 4 + j % 4, :], CMC[:, x, c:c + 1], acc, ALU.mult, ALU.add).then_inc(dn_add, 1)
            rounds(dve, experts)
            dve.wait_ge(dn_add, 8 * N_EXP)
            for c in range(NC):
                link(dve.tensor_tensor(OUTA[:, c, :], OUTA[:, c, :], ROW_G, ALU.mult))
                dve.tensor_tensor(X[:, c, :], X[:, c, :], OUTA[:, c, :], ALU.add).then_inc(fin_x, 1)
            dve.wait_ge(norm_rs[4], 2)
            dve.wait_ge(fin_x, NC)
            for c in range(NC):
                dve.scalar_tensor_tensor(X[:, c, :], X[:, c, :], SS[:, 4 + c:5 + c], ROW_F, ALU.mult, ALU.mult).then_inc(fin_d, 1)
        @block.gpsimd
        def _(pool):
            link = Link(pool, pool_link)
            pool.wait_ge(const_in, 16 * NCONST)
            norm_pool(pool, 0)
            pool.wait_ge(z_out, NU_A)
            for g in range(4):
                src = PZ[:, 2 * g:2 * g + 2, :]
                cur = src
                for lev in range(g + 1):
                    d = 1 << lev
                    dst = PB[:, lev % 2, :, :]
                    link.inc(pool.tensor_copy(dst[:, :, 0:d], cur[:, :, 0:d]))
                    link(pool.tensor_tensor(dst[:, :, d:S], cur[:, :, d:S], cur[:, :, 0:S - d], ALU.add))
                    cur = dst
                w = 2 << g
                link(pool.tensor_tensor(cur[:, :, 0:16], cur[:, :, 0:16], PINV[:, g, :].unsqueeze(1).broadcast_to([PG, 2, 16]), ALU.mult))
                link(pool.tensor_scalar(cur, cur, 1.0 / w, None, ALU.mult))
                ins = pool.tensor_tensor(src, cur, src, ALU.subtract)
                if g == 3:
                    ins.then_inc(pooled, 1)
                else:
                    link(ins)
            for q in range(2):
                pool.wait_ge(att_c, 6)
                pool.wait_ge(eg_e, q + 1)
                pool.tensor_tensor(OT[:, q, :, :], OT[:, q, :, :], EG, ALU.mult).then_inc(wsum, 1)
                pool.wait_ge(wsum, 3 * q + 1)
                pool.tensor_tensor(OT[:, q, 0, :], OT[:, q, 0, :], OT[:, q, 1, :], ALU.add).then_inc(wsum, 1)
                pool.wait_ge(wsum, 3 * q + 2)
                pool.tensor_tensor(OT[:, q, 0, :], OT[:, q, 0, :], OT[:, q, 2, :], ALU.add).then_inc(wsum, 1)

            with pool.Fori(0, 4) as j:
                pool.wait_ge(t1_d, j + 1)
                pool.wait_ge(t2_d, j + 1)
                pool.tensor_tensor(MG[:, bass.ds(2 * j, 2), :], T1, T2, ALU.add).then_inc(mg_d, 1)
            pool.wait_ge(t1_d, 4)
            pool.wait_ge(at_lo, 2)
            pool.memset(ACC, 0.0).then_inc(acc_init, 1)
            pool.wait_ge(acc_init, 1)
            pool.dma_start(ACC[0:1, :], t["b_ada"]).then_inc(b_in, 16)
            norm_pool(pool, 1)
            with pool.Fori(0, 4) as gi:
                for s in range(4):
                    pool.wait_ge(hid_hi, 4 * gi + s + 1)
                    pool.tensor_tensor(VL[:, 2 * s:2 * s + 2, :], SQ[:, s % 2, :, :], VH[:, 2 * s:2 * s + 2, :].bitcast(F32),
                                       ALU.subtract).then_inc(hid_lo, 1)

            pool.wait_ge(br_sq, NC)
            pool.tensor_scalar(SS[:, 0:4], SS[:, 0:4], 1.0 / D, EPS, ALU.mult, ALU.add).then_inc(br_rs, 1)
            pool.wait_ge(br_rs, 1)
            pool.tensor_tensor(SS[:, 4:8], SS[:, 0:4], COLS[:, 60:64], ALU.pow).then_inc(br_rs, 1)
            norm_pool(pool, 2)
            pool.wait_ge(lb_d, 1)
            pool.wait_ge(trig_d, 2)
            for j in range(3):
                for a in (2 * j, 2 * j + 1):
                    pool.wait_ge(perm_mm, a + 1)
                    pool.tensor_tensor(RQK[:, a, :], RQK[:, a, :], COS, ALU.mult).then_inc(rope_c, 1)
                    pool.wait_ge(rope_c, a + 1)
                    pool.wait_ge(rope_s, a + 1)
                    pool.tensor_tensor(RQK[:, a, :], RQK[:, a, :], RT, ALU.add).then_inc(rope_d, 1)
                pool.wait_ge(hsig, 2 * j + 2)
                n = J0 + 3 + j
                pool.tensor_scalar(HF[:, j, :], SG[:, n % 2, 1, :], LBS[:, 9 + j:10 + j], LBS[:, j:j + 1], ALU.mult, ALU.add).then_inc(hf_d, 1)
                pool.wait_ge(hf_d, 3 * j + 1)
                pool.tensor_scalar(HF[:, j, :], HF[:, j, :], 1e-30, None, ALU.max).then_inc(hf_d, 1)
                pool.tensor_scalar(HK[:, j, :], HK[:, j, :], LBS[:, 9 + j:10 + j], None, ALU.mult).then_inc(hf_d, 1)
            pool.wait_ge(hf_d, 9)
            pool.wait_ge(hq_d, 3)
            pool.wait_ge(ga_d, 1)
            pool.wait_ge(z2_out, 10)
            pool.wait_ge(ret_o, 6)

            def head_lo(tile):
                pool.wait_ge(hn_hi, tile + 1)
                pool.tensor_tensor(VL[:, tile, :], G2[:, tile, :], VH[:, tile, :].bitcast(F32), ALU.subtract).then_inc(hn_lo, 1)
            for tile in range(3):
                head_lo(tile)
            for p in range(5):
                q_, k_, f_ = (HQ[:, p, :], HK[:, p, :], HF[:, p, :]) if p < 3 else (GQ, GK, GF)
                link.inc(pool.tensor_copy(PP, f_))
                link(pool.memset(UB, 1.0))
                for lev in range(9):
                    m = 1 << lev
                    v = lambda x: x.rearrange("p (n two m) -> p n two m", two=2, m=m)
                    if 9 * p + lev >= 2:
                        pool.wait_ge(lvl_s, 20 * ((9 * p + lev - 2) // 9) + 2 * ((9 * p + lev - 2) % 9) + 4)
                    qk = v(QKL[:, lev % 2, :]) if (9 * p + lev) % 2 == lev % 2 else v(QKL[:, (9 * p + lev) % 2, :])
                    link.inc(pool.tensor_tensor(qk[:, :, 0, :], v(k_)[:, :, 0, :], v(UB)[:, :, 0, :], ALU.mult))
                    pool.tensor_tensor(qk[:, :, 1, :], v(q_)[:, :, 1, :], v(PP)[:, :, 1, :], ALU.mult).then_inc(lvl_qk, 1)
                    if lev < 8:
                        sh = [P, S // (2 * m), m]
                        link.wait()
                        pool.wait_ge(lvl_qk, 9 * p + lev + 1)
                        link(pool.tensor_tensor(v(UB)[:, :, 0, :], v(UB)[:, :, 0, :], v(PP)[:, :, 1, m - 1:m].broadcast_to(sh), ALU.mult))
                        link(pool.tensor_tensor(v(PP)[:, :, 1, :], v(PP)[:, :, 1, :], v(PP)[:, :, 0, m - 1:m].broadcast_to(sh), ALU.mult))
                    else:
                        link.wait()
                        pool.wait_ge(lvl_qk, 9 * p + lev + 1)
                head_lo(3 + p)
            for x in range(8):
                h, c = x // 4, x % 4
                pool.wait_ge(wo2_t, x + 1)
                xs = X[:, c, HALF * h:HALF * h + HALF]
                pool.tensor_tensor(xs, xs, TMPK[:, x % 2, :], ALU.add).then_inc(wo2_add, 1)

            def rstd(j):
                pool.wait_ge(norm_sq[j], NC)
                pool.tensor_scalar(SS[:, 0:4], SS[:, 0:4], 1.0 / D, EPS, ALU.mult, ALU.add).then_inc(norm_rs[j], 1)
                pool.wait_ge(norm_rs[j], 1)
                pool.tensor_tensor(SS[:, 4:8], SS[:, 0:4], COLS[:, 60:64], ALU.pow).then_inc(norm_rs[j], 1)
            rstd(3)
            pool.wait_ge(wr_hi, 1)
            pool.tensor_tensor(ATL[:, 0, 0:KD * N_LOG], WR, ATH[:, 0, 0:KD * N_LOG].bitcast(F32), ALU.subtract).then_inc(wr_lo, 1)
            for c in range(NC):
                pool.wait_ge(h2_m, c + 1)
                pool.tensor_tensor(XN[:, c, :], XN[:, c, :], ROW_B, ALU.add).then_inc(h2_d, 1)
            rstd(4)

        @block.tensor
        def _(pe):
            pe.wait_ge(const_in, 16 * NCONST)
            norm_pe(pe, 0)
            pe.wait_ge(norm_lo[0], KD)
            for n in range(A0, B0):
                unit_is_in(pe, n)
                if n >= 2:
                    pe.wait_ge(z_out, n - 1)
                for m in range(2):
                    last = feature(pe, n % 2, m, PG, 2 * PG, U, 2 * (n % 2) + m)
                last.then_inc(unit_done, 1)
            with pe.Fori(0, NU_B // 2) as i:
                for s in range(2):
                    unit_is_in(pe, 2 * i + B0 + s)
                    pe.wait_ge(z_out, 2 * i + B0 + s - 1)
                    for m in range(2):
                        last = feature(pe, s, m, P, 256, U, 2 * s + m)
                    last.then_inc(unit_done, 1)
            for n in range(C0, D0):
                unit_is_in(pe, n)
                pe.wait_ge(z_out, n - 1)
                for c in range(NC):
                    for k in range(KD):
                        tok = slice(P * c, P * c + P) if n == C0 else slice(c, S, 4)
                        last = three(pe, PS[:, 2 * (n % 2) + c // 2, 256 * (c % 2):256 * (c % 2) + 256], (UH[:, k, tok], UL[:, k, tok]),
                                     wpair(n % 2, 256 * k, 256), k == 0, k == KD - 1)
                last.then_inc(unit_done, 1)
            unit_is_in(pe, D0)
            pe.wait_ge(pool_lo, 1)
            pe.wait_ge(z_out, D0)
            for g in range(4):
                for m in range(2):
                    for k in range(2):
                        last = three(pe, PS[0:PG, 2 * g + m, :], wpair(D0 % 2, 192 * (2 * g + k) + PG * m, PG, PG),
                                     (VH[0:PG, 2 * g + k, :], VL[0:PG, 2 * g + k, :]), k == 0, k == 1)
            last.then_inc(unit_done, 1)

            def transposes(n):
                w = len(blks(heads[n][0]))
                pe.wait_ge(att_e, 4 * (n + 1))
                if n:
                    pe.wait_ge(att_p, n)
                for x, (c, b) in enumerate(blks(heads[n][0])):
                    last = pe.transpose(PS[:, 4 + x // 4, P * (x % 4):P * (x % 4) + P], SBUFS[:, n % 2, c, P * b:P * b + P], IDN[:, :])
                last.then_inc(att_t, 1)

            def av(n):
                g, q, hh = heads[n]
                r0 = 64 * hh
                hd = 4 * g + 2 * q + hh
                pe.wait_ge(att_p, n + 1)
                if n >= 4:
                    pe.wait_ge(att_c, n // 2 - 1)
                for x, (c, b) in enumerate(blks(g)):
                    kc = c - 1 + b if g == 0 else c
                    last = pe.matmul(PS[r0:r0 + 64, 6 + (n // 2) % 2, P * c:P * c + P], VT[:, kc, 64 * hd:64 * hd + 64], PTB[:, n % 2, x, :],
                                     start=(b == 0 or c == 0), stop=(b == 1 or g > 0))
                last.then_inc(att_o, 1)

            pe.wait_ge(mix_out, 8)
            for n, (g, q, hh) in enumerate(heads):
                r = slice(64 * hh, 64 * hh + 64)
                b = 2 * (n % 2)
                if n >= 2:
                    pe.wait_ge(att_m, n - 1)
                qt, kt = QK[r, 2 * g + q, :], QK[r, 6 + 2 * g + q, :]
                for c in range(NC):
                    if g == 0:
                        o, k0, kn = (P, 0, P) if c == 0 else (0, P * (c - 1), 2 * P)
                        out = PS[:, b + c // 2, 256 * (c % 2) + o:256 * (c % 2) + o + kn]
                        last = pe.matmul(out, qt[:, P * c:P * c + P], kt[:, k0:k0 + kn], start=True, stop=True)
                    else:
                        last = pe.matmul(PS[:, b, P * c:P * c + P], qt[:, c::4], kt[:, c::4], start=True, stop=True)
                last.then_inc(att_s, 1)
                if n >= 1:
                    transposes(n - 1)
                if n >= 2:
                    av(n - 2)
            transposes(11)
            av(10)
            pe.wait_ge(att_m, 12)
            for c in range(NC):
                last = pe.transpose(PS[0:48, 0, P * c:P * c + P], ST[:, c, :], IDN[:, :])
            last.then_inc(st_tr, 1)
            av(11)
            pe.wait_ge(st_row, 2)

            def stat_rows(bank, q, col):
                for g in range(3):
                    for hh in range(2):
                        r = st_col(g, q, hh) + col
                        last = pe.matmul(PS[64 * hh:64 * hh + 64, bank + g, :], IDN[0:48, r:r + 1].broadcast_to([48, 64]), RW,
                                         start=True, stop=True)
                return last
            for q in range(2):
                if q:
                    pe.wait_ge(eg_d, 3)
                stat_rows(1, q, 0).then_inc(nm_bc, 1)
                if q:
                    pe.wait_ge(den_d, 1)
                else:
                    pe.wait_ge(att_c, 6)
                stat_rows(4, q, 4).then_inc(l_bc, 1)
            pe.wait_ge(mixed_lo, 1)
            pe.wait_ge(at_lo, 2)

            def branches(j):
                for s, (src, rows, kc) in enumerate(((U, P, 8), (V, PG, 8), (U, P, 8), (AT, P, 2))):
                    unit_is_in(pe, 4 * j + E0 + s)
                    if not first(j):
                        pe.wait_ge((gp_sig, t1_d, ga_sig, t2_d)[s], j)
                    for m in range(2):
                        last = feature(pe, s % 2, m, P, 256, src, 2 * s + m, rows, kc)
                    last.then_inc(unit_done, 1)
            peeled(pe, 4, branches)
            pe.wait_ge(t2_d, 4)
            for n in range(F0, G0):
                h, kh = (n - F0) // 2, (n - F0) % 2
                unit_is_in(pe, n)
                pe.wait_ge(mg_lo, 4 * kh + 4)
                tokens(pe, n % 2, U, 4 * kh, 4 * h, wo_chunk, kh == 0, kh == 1)
            norm_pe(pe, 1)
            pe.wait_ge(norm_lo[1], KD)

            def mlp(gi):
                for s in range(8):
                    unit_is_in(pe, 8 * gi + G0 + s)
                    if s < 4:
                        if s >= 2:
                            pe.wait_ge(sq_d, 4 * gi + s - 1)
                        elif not first(gi):
                            pe.wait_ge(mo_add, 8 * gi - 2 + 2 * s)
                        for m in range(2):
                            last = feature(pe, s % 2, m, P, 256, U, 2 * (s % 2) + m)
                        last.then_inc(unit_done, 1)
                    else:
                        h, kh = (s - 4) // 2, s % 2
                        pe.wait_ge(hid_lo, 4 * gi + 2 * kh + 2)
                        pe.wait_ge(sq_d, 4 * gi + 4) if h else None
                        tokens(pe, s % 2, V, 4 * kh, 4 * (1 - h), mo_chunk, kh == 0, kh == 1)
            peeled(pe, 4, mlp)

            pe.wait_ge(ada_d, 24)
            pe.wait_ge(mo_add, 32)
            for k in range(16):
                last = pe.matmul(PS[:, 0, k:k + 1], ACC[:, P * k:P * k + P], COLS[:, 59:60], start=True, stop=True)
            last.then_inc(mod_mm, 1)
            for r, src in enumerate((2 * D, 2 * D + HALF, 3 * D, 3 * D + HALF, 4 * D, 4 * D + HALF, 5 * D, 5 * D + HALF)):
                if r >= 3:
                    pe.wait_ge(mrow_d, r - 2)
                pe.matmul(PS[0:1, 1 + r % 3, :], COLS[:, 59:60], ACC[:, src:src + HALF], start=True, stop=True).then_inc(mrow_mm, 1)
            norm_pe(pe, 2)
            pe.wait_ge(norm_lo[2], KD)
            pe.wait_ge(mrow_d, 8)
            for n in range(H0, J0 + 6):
                unit_is_in(pe, n)
                if n < I0 + 2:
                    if n >= H0 + 2:
                        pe.wait_ge(z2_out, n - H0 - 1)
                elif n < J0 + 2:
                    pe.wait_ge(g2_out, n - I0 - 1)
                elif n < J0 + 5:
                    pe.wait_ge(z2_out, 4 + n - J0 - 1)
                if n >= J0 + 5:
                    pe.wait_ge(hq_d, n - J0 - 4)
                    pe.wait_ge(hsig, 2 * (n - J0 - 4))
                if n < I0:
                    for c in range(NC):
                        for k in range(KD):
                            tok = slice(P * c, P * c + P)
                            last = three(pe, PS[:, 2 * (n % 2) + c // 2, 256 * (c % 2):256 * (c % 2) + 256], (UH[:, k, tok], UL[:, k, tok]),
                                         wpair(n % 2, 256 * k, 256), k == 0, k == KD - 1)
                else:
                    for m in range(2):
                        last = feature(pe, n % 2, m, P, 256, U, 2 * (n % 2) + m)
                last.then_inc(unit_done, 1)
                if n == J0 + 3:
                    pe.wait_ge(z2_out, 7)
                    pe.wait_ge(pos_in, 32)
                    for a in range(6):
                        if a >= 4:
                            pe.wait_ge(rope_s, a - 3)
                        pe.matmul(PS[:, 4 + a % 4, :], PERM, RQK[:, a, :], start=True, stop=True).then_inc(perm_mm, 1)
            n = J0 + 6
            unit_is_in(pe, n)
            pe.wait_ge(hq_d, 2)
            pe.wait_ge(hsig, 4)
            for m in range(2):
                last = feature(pe, 0, m, P, 256, U, m)
            last.then_inc(unit_done, 1)
            n = J0 + 7
            unit_is_in(pe, n)
            pe.wait_ge(hq_d, 3)
            pe.wait_ge(hsig, 6)
            feature(pe, 1, 0, 16, 16, U, 2).then_inc(ga_mm, 1)
            pe.wait_ge(z2_out, 10)
            pe.matmul(PS[:, 3, :], WH[0:16, 1, P:2 * P].bitcast(F32), GA, start=True, stop=False)
            pe.matmul(PS[:, 3, :], WL[0:16, 1, P:2 * P].bitcast(F32), GA, start=False, stop=True).then_inc(unit_done, 1)

            def mean_square(tile):
                pe.wait_ge(hn_sq, tile + 1)
                pe.matmul(PS[:, 7, :], ONESB[:, :], SQT, start=True, stop=True).then_inc(hn_mm, 1)

            def weigh(hh, head, signal):
                A = AB[:, hh, :]
                off = {0: 512, 1: 896, 2: 1152}
                out = PS[64 * (head % 2):64 * (head % 2) + 64, 6, :]
                for cs in range(NC):
                    val = V2[:, cs, 64 * head:64 * head + 64]
                    if cs < 3:
                        n_off = P * (3 - cs)
                        if cs == 0:
                            pe.matmul(out[:, 0:P], val, A[:, 0:P], start=True, stop=False, skip_group_check=True)
                        else:
                            pe.matmul(out[:, P * cs:P * cs + P], val, A[:, P * cs:P * cs + P], start=False, stop=False, skip_group_check=True)
                        last = pe.matmul(out[:, P * (cs + 1):S], val, A[:, off[cs]:off[cs] + n_off], start=False, stop=False, skip_group_check=True)
                    else:
                        last = pe.matmul(out[:, P * cs:S], val, A[:, P * cs:P * cs + P], start=False, stop=True, skip_group_check=True)
                last.then_inc(signal, 1)

            pe.wait_ge(ga_x, 1)
            pe.wait_ge(rope_d, 6)
            for h in range(7):
                if h < 6:
                    b, r0 = 3 * (h % 2), 64 * (h % 2)
                    q_, k_ = RQK[r0:r0 + 64, h // 2, :], RQK[r0:r0 + 64, 3 + h // 2, :]
                    if h >= 2:
                        pe.wait_ge(ret_a, h - 1)
                    else:
                        pe.wait_ge(hq_d, 3)
                    for c in range(NC):
                        pe.matmul(PS[:, b, P * c:P * c + P], k_[:, P * c:P * c + P], q_[:, P * c:P * c + P], start=True, stop=True)
                    pe.matmul(PS[:, b + 1, 0:384], k_[:, 0:P], q_[:, P:S], start=True, stop=True)
                    pe.matmul(PS[:, b + 1, 384:512], k_[:, 2 * P:3 * P], q_[:, 3 * P:S], start=True, stop=True)
                    pe.matmul(PS[:, b + 2, 0:256], k_[:, P:2 * P], q_[:, 2 * P:S], start=True, stop=True).then_inc(ret_s, 1)
                if h >= 3 and h % 2:
                    mean_square(h // 2 - 1)
                if h:
                    pe.wait_ge(ret_a, h)
                    if h >= 3 and h % 2:
                        pe.wait_ge(hn_d, 3 * (h // 2 - 1) + 2)
                    weigh((h - 1) % 2, h - 1, ret_o)
            mean_square(2)

            pe.wait_ge(hf_d, 9)
            for p in range(5):
                q_, k_ = (HQ[:, p, :], HK[:, p, :]) if p < 3 else (GQ, GK)
                for lev in range(-1, 9):
                    for hh in range(2):
                        if p < 3:
                            r = slice(64 * hh, 64 * hh + 64)
                        else:
                            r = slice(64 * (p - 3) + 32 * hh, 64 * (p - 3) + 32 * hh + 32)
                        cnt = 20 * p + 2 * (lev + 1) + hh
                        bank = cnt % 6
                        if cnt >= 6:
                            before = cnt - 6
                            bp, bl, bh = before // 20, (before % 20) // 2 - 1, before % 2
                            if bl < 7:
                                pe.wait_ge(lvl_a, 16 * bp + 2 * (bl + 1) + bh + 1)
                            else:
                                pe.wait_ge(lvl_b, 8 * bp + 4 * (bl - 7) + 2 * bh + 2)
                        elif cnt == 0:
                            pe.wait_ge(ret_a, 6)
                        if lev < 0:
                            left, right = k_, q_
                        else:
                            if hh == 0:
                                pe.wait_ge(lvl_qk, 9 * p + lev + 1)
                            left = right = QKL[:, (9 * p + lev) % 2, :]
                        if lev < 7:
                            for c in range(NC):
                                last = pe.matmul(PS[:, bank, P * c:P * c + P], left[r, P * c:P * c + P], right[r, P * c:P * c + P], start=True, stop=True)
                        elif lev == 7:
                            pe.matmul(PS[:, bank, 0:P], left[r, 0:P], right[r, P:2 * P], start=True, stop=True)
                            last = pe.matmul(PS[:, bank, P:2 * P], left[r, 2 * P:3 * P], right[r, 3 * P:S], start=True, stop=True)
                        else:
                            pe.matmul(PS[:, bank, 0:256], left[r, 0:P], right[r, 256:S], start=True, stop=True)
                            last = pe.matmul(PS[:, bank, 256:512], left[r, P:2 * P], right[r, 256:S], start=True, stop=True)
                        last.then_inc(lvl_s, 1)
                pe.wait_ge(hn_d, 3 * (p + 2) + 2)
                pe.wait_ge(lvl_a, 16 * (p + 1))
                pe.wait_ge(lvl_b, 8 * (p + 1))
                head = 6 + 2 * p
                weigh(0, head, pass_h)
                weigh(1, head + 1, pass_o)
                mean_square(3 + p)

            for n in range(K0, M0):
                h, kh = (n - K0) // 2, (n - K0) % 2
                unit_is_in(pe, n)
                pe.wait_ge(hn_lo, 4 * kh + 4)
                if h:
                    pe.wait_ge(hn_d, 24)
                tokens(pe, n % 2, V, 4 * kh, 4 * h, wo2_chunk, kh == 0, kh == 1)
            pe.wait_ge(h2_d, NC)
            for k in range(KD):
                if k >= 4:
                    pe.wait_ge(norm_lo[3], k - 3)
                for c in range(NC):
                    last = pe.transpose(PS[:, 4 + k % 4, c * P:(c + 1) * P], XN[:, c, k * P:(k + 1) * P], IDN[:, :])
                last.then_inc(norm_tr[3], 1)
            pe.wait_ge(norm_lo[3], KD)
            pe.wait_ge(wr_lo, 1)
            for c in range(NC):
                for k in range(KD):
                    tok = slice(P * c, P * c + P)
                    w = slice(N_LOG * k, N_LOG * k + N_LOG)
                    last = three(pe, PS[:, 0, 64 * c:64 * c + N_LOG], (UH[:, k, tok], UL[:, k, tok]), (ATH[:, 0, w], ATL[:, 0, w]), k == 0, k == KD - 1)
            last.then_inc(lg_mm, 1)
            pe.wait_ge(rt_arg, 2)

            def experts(i, last=False):
                for s in range(6):
                    x, e, n = s // 3, 2 * i + s // 3, 6 * i + M0 + s
                    unit_is_in(pe, n)
                    if s % 3 < 2:
                        if not (first(i) and x == 0):
                            pe.wait_ge(m_hid, 2 * e)
                        for m in range(2):
                            done = feature(pe, s % 2, m, P, 256, U, 2 * (s % 3) + m)
                        done.then_inc(unit_done, 1)
                    else:
                        pe.wait_ge(m_lo, 2 * e + 2)
                        for j in range(8):
                            c, h = j // 2, j % 2
                            if j >= 4 or not (first(i) and x == 0):
                                pe.wait_ge(dn_add, 8 * e + j - 3)
                            for k in range(2):
                                tok = slice(P * c, P * c + P)
                                done = three(pe, PS[:, 4 + j % 4, :], (VH[:, 2 * x + k, tok], VL[:, 2 * x + k, tok]),
                                             wpair(s % 2, D * k + HALF * h, HALF), k == 0, k == 1)
                            if j < 7:
                                done.then_inc(dn_mm, 1)
                        done.then_inc(unit_done, 1)
            rounds(pe, experts)


POOL_TAPS = 16
HEADS_GRP = 4
ATT_HEADS = 12
RET_HEADS = 6
HEAD_DIM = 64


def _rows(w, n0, n, kp=P):
    return w[:, n0:n0 + n].reshape(w.shape[0] // kp, kp, n).transpose(1, 0, 2)


def _unit(a):
    u = np.zeros((P, UNIT), np.float32)
    u[:a.shape[0], :a[0].size] = a.reshape(a.shape[0], -1)
    return u


def _columns(w, *spans):
    return np.concatenate([w[:, a:b] for a, b in spans], 1)


def _square(w, units, h_cols=HALF):
    for h in range(2):
        for kh in range(2):
            units.append(_unit(_rows(w[HALF * kh:HALF * kh + HALF], HALF * h, HALF)))


def _weight_units(t):
    u = []
    w = t["w_in"][0]
    for j in range(4):
        u.append(_unit(_rows(w, 2304 + 192 * j, 192)))
    for j in range(6):
        u.append(_unit(_rows(w, 256 * j, 256)))
    for j in range(3):
        u.append(_unit(_rows(w, 1536 + 256 * j, 256)))
    u.append(_unit(t["w_pool_grp"][0].reshape(4, 2, PG, 2 * PG).transpose(2, 0, 1, 3)))
    for j in range(4):
        u.append(_unit(_rows(w, 4096 + 256 * j, 256)))
        u.append(_unit(_rows(t["w_pool_out"][0], 256 * j, 256, PG)))
        u.append(_unit(_rows(w, 3072 + 256 * j, 256)))
        u.append(_unit(_rows(t["w_att_out"][0], 256 * j, 256)))
    _square(t["w_out"][0], u)
    for g in range(4):
        for s in range(4):
            u.append(_unit(_rows(t["w_mlp_in"][0], D * g + 256 * s, 256)))
        _square(t["w_mlp_out"][0][D * g:D * g + D], u)
    w = t["w_in_2"][0]
    values = _columns(w, (768, 1152), (2304, 2688), (3328, 3584))
    gates = _columns(w, (1152, 1536), (2688, 3072), (3584, 3840))
    for part in (values, gates):
        for j in range(4):
            u.append(_unit(_rows(part, 256 * j, 256)))
    for j in range(3):
        u.append(_unit(_rows(w, 256 * j, 256)))
    for j in range(3):
        u.append(_unit(_rows(_columns(w, (1536 + P * j, 1664 + P * j), (1920 + P * j, 2048 + P * j)), 0, 256)))
    u.append(_unit(_rows(w, 3072, 256)))
    ga = _unit(_rows(w, 3840, 16))
    ga[:16, P:2 * P] = t["gla_wa2_2"][0]
    u.append(ga)
    _square(t["w_out_2"][0], u)
    for e in range(N_EXP):
        u.append(_unit(_rows(t["expert_w_gate_2"][0, e], 0, 256)))
        u.append(_unit(_rows(t["expert_w_up_2"][0, e], 0, 256)))
        u.append(_unit(_rows(t["expert_w_down_2"][0, e], 0, D)))
    return np.stack(u)


def _cols(t):
    f = np.float32
    c = np.zeros((P, 64), f)
    c[:, 0:8] = t["norm_mix_g"][0].reshape(8, P).T
    c[:PG, 8:16] = t["pool_scale"][0].reshape(8, PG).T
    c[:, 16:24] = t["norm_mlp_g"][0].reshape(8, P).T
    c[:, 24:32] = t["c_2"][0].reshape(8, P).T
    c[:, 32:35] = t["hgrn_lb_logits_2"][0].reshape(3, P).T
    c[:, 35:43] = np.concatenate([t["ret_norm_2"][0], t["hgrn_norm_2"][0], t["gla_norm_2"][0]]).reshape(8, P).T
    c[:, 43:51] = t["norm_mix_2"][0].reshape(8, P).T
    c[:, 51] = t["gla_ba_2"][0]
    c[:, 52] = np.tile((f(10000.0) ** (-np.arange(0, 64, 2, dtype=f) / 64)).astype(f), 4)
    c[:, 53] = np.tile(np.repeat([-1.0, 1.0], 32), 2)
    c[:, 58] = EPS
    c[:, 59] = 1.0
    c[:, 60:64] = -0.5
    return c


def _constants():
    f = np.float32
    c = {"ident": np.eye(P, dtype=f)}
    inv = np.ones((PG, 4, POOL_TAPS), f)
    for g in range(4):
        w = 2 << g
        for i in range(POOL_TAPS):
            inv[:, g, i] = w / min(i + 1, w)
    c["pool_inv"] = inv
    slopes = (2.0 ** (-8.0 * (np.arange(ATT_HEADS) + 1.0) / ATT_HEADS)).astype(f)
    bias = np.full((P, 2048), NEG, f)
    q = np.arange(P)[:, None]
    band = P + q - np.arange(2 * P)[None]
    own = q - np.arange(P)[None]
    for h in range(HEADS_GRP):
        bias[:, 256 * h:256 * h + 256] = np.where((band >= 0) & (band <= P), -(slopes[h] * band.astype(f)), f(NEG))
        far = (4 * own).astype(f)
        bias[:, 1024 + P * h:1024 + P * h + P] = np.where(own >= 0, -(slopes[4 + h] * far), f(NEG))
        bias[:, 1536 + P * h:1536 + P * h + P] = np.where((own >= 0) & (own % 4 == 0), -(slopes[8 + h] * far), f(NEG))
    c["bias"] = bias
    blocks = np.zeros((P, P), f)
    blocks[:64, :64] = blocks[64:, 64:] = 1 / 64
    c["ones_block"] = blocks
    perm = np.zeros((P, P), f)
    for m in range(P):
        perm[((m // 32) ^ 1) * 32 + m % 32, m] = 1
    c["perm"] = perm
    decay = np.zeros((RET_HEADS, P, S), f)
    key, tok = np.arange(P)[:, None], np.arange(S)[None]
    for h in range(RET_HEADS):
        lg = np.log1p(-2.0 ** (-5.0 - h))
        decay[h] = np.where(tok >= key, HEAD_DIM ** -0.5 * np.exp(lg * np.maximum(tok - key, 0)), 0)
    c["decay"] = decay
    masks = np.zeros((P, 8, P), np.int32)
    tok = np.arange(P)[None]
    masks[:, 0] = key == tok
    for lev in range(7):
        m = 1 << lev
        masks[:, 1 + lev] = (key // (2 * m) == tok // (2 * m)) & ((key // m) % 2 == 0) & ((tok // m) % 2 == 1)
    c["masks"] = masks
    c["iota"] = np.tile(np.arange(N_EXP, dtype=f), (P, 1))
    return c


def kernel(**inputs):
    import concourse.bacc as bacc
    from concourse.bass_utils import run_bass_kernel_spmd

    t = {name: np.asarray(a) for name, a in inputs.items()}
    data = _constants()
    data["x"] = np.ascontiguousarray(t["x"][0].reshape(NC, P, D).transpose(1, 0, 2))
    data["w"] = _weight_units(t)
    data["cols"] = _cols(t)
    data["w_ada"] = np.ascontiguousarray(t["w_ada_2"][0].reshape(KD, P, 3, UNIT).transpose(0, 2, 1, 3).reshape(3 * KD, P, UNIT))
    data["b_ada"] = t["b_ada_2"]
    data["norm_final_g"] = t["norm_final_g"]
    data["positions"] = t["positions_2"][0]
    data["norm_ffn"] = t["norm_ffn_2"][0]
    data["norm_final_2"] = t["norm_final_2"]
    data["w_router"] = np.ascontiguousarray(_rows(
        np.concatenate([t["router_group_w_2"][0], t["router_expert_w_2"][0]], 1), 0, N_LOG).reshape(P, KD * N_LOG))
    data["b_router"] = np.concatenate([t["router_group_b_2"][0], t["router_expert_b_2"][0]])

    nc = bacc.Bacc("TRN2", target_bir_lowering=False, num_devices=1, dynamic_dma_scratch_size=4096)
    aps, arrays = {}, {}
    for name, a in data.items():
        arrays["in_" + name] = a
        aps[name] = nc.dram_tensor("in_" + name, list(a.shape), mybir.dt.from_np(a.dtype), kind="ExternalInput").ap()
    aps["mod_row"] = nc.dram_tensor("mod_row", [1, 4 * D], F32, kind="Internal").ap()
    aps["out"] = nc.dram_tensor("out", [1, S, D], F32, kind="ExternalOutput").ap()
    build(nc, aps)
    result = run_bass_kernel_spmd(nc, [arrays], core_ids=[0])
    return result.results[0]["out"]
```

```python
import numpy as np
import concourse.bass as bass
from concourse import mybir
from contextlib import ExitStack

F32 = mybir.dt.float32
F32R = mybir.dt.float32r
I32 = mybir.dt.int32
U32 = mybir.dt.uint32
ACT = mybir.ActivationFunctionType
ALU = mybir.AluOpType
AX = mybir.AxisListType

P = 128
S = 512
D = 1024
NC = S // P
KD = D // P
EPS = 1e-6
UNIT = 2048
NU_A, NU_B, NU_C, NU_D, NU_E, NU_F, NU_G = 4, 6, 3, 1, 16, 4, 32
A0 = 0
B0 = A0 + NU_A
C0 = B0 + NU_B
D0 = C0 + NU_C
E0 = D0 + NU_D
F0 = E0 + NU_E
G0 = F0 + NU_F
H0 = G0 + NU_G
NU_H, NU_I, NU_J, NU_K = 4, 4, 8, 4
I0 = H0 + NU_H
J0 = I0 + NU_I
K0 = J0 + NU_J
M0 = K0 + NU_K
N_EXP = 32
N_GROUP, PER_GROUP = 4, 8
N_LOG = N_GROUP + N_EXP
BLOCK = 64
MAX_BLOCKS = N_EXP + 2 * S // BLOCK
E_UNIT = 3 * UNIT
NEG = -1.0e30
TWO_PI = 2 * np.pi
PI_IN = 3.1415925


def _turn():
    a = 6.28125
    b = float(np.float32(np.round((TWO_PI - a) * 2 ** 21) / 2 ** 21))
    return a, b, float(np.float32(TWO_PI - a - b))


TURN = _turn()
HALF = D // 2
PG = 96


def build(nc, t):
    ctx = ExitStack()
    with ctx:
        def sb(name, shape, dt=F32):
            return ctx.enter_context(nc.sbuf_tensor(name, shape, dt))

        def sem(name):
            return ctx.enter_context(nc.semaphore(name))

        RAW = sb("raw", [P, 2, UNIT])
        WH = sb("w_high", [P, 2, UNIT], F32R)
        WL = sb("w_low", [P, 2, UNIT], F32R)
        UH = sb("u_high", [P, KD, S], F32R)
        UL = sb("u_low", [P, KD, S], F32R)
        VH = sb("v_high", [P, KD, S], F32R)
        VL = sb("v_low", [P, KD, S], F32R)
        X = sb("x", [P, NC, D])
        IDN = sb("ident", [P, P])
        COLS = sb("cols", [P, 64])
        SS = sb("sumsq", [P, 8])
        ATH = sb("att_high", [P, 2, S], F32R)
        ATL = sb("att_low", [P, 2, S], F32R)
        AR = sb("arena", [P, 20992])
        ONESB = sb("block_ones", [P, P])
        CA = sb("c_act", [P, 8])
        MODC = sb("mod_cols", [P, 16])
        LBS = sb("lower_bound", [P, 12])
        PS = ctx.enter_context(nc.psum_tensor("ps", [P, 8, 512], F32))

        def ar(off, n, rows=P):
            return AR[0:rows, off:off + n]

        QK = ar(0, 6144).rearrange("p (a s) -> p a s", a=12)
        VT = ar(6144, 3072).rearrange("p (c n) -> p c n", c=NC)
        PZ = ar(9216, 4096, PG).rearrange("p (a s) -> p a s", a=8)
        PB = ar(13312, 2048, PG).rearrange("p (b h s) -> p b h s", b=2, h=2)
        PINV = ar(15360, 64, PG).rearrange("p (g w) -> p g w", g=4)
        SBUFS = ar(9216, 2048).rearrange("p (b c k) -> p b c k", b=2, c=4)
        PTB = ar(11264, 2048).rearrange("p (b c k) -> p b c k", b=2, c=8)
        OT = ar(13312, 3072).rearrange("p (q g s) -> p q g s", q=2, g=3)
        BIAS = ar(16384, 2048)
        ST = ar(18432, 192).rearrange("p (c k) -> p c k", c=4)
        RW = ar(9216, 512, 48)
        EG = ar(9728, 1536).rearrange("p (g s) -> p g s", g=3)
        MN = ar(11264, 512)
        DG = ar(11776, 1536).rearrange("p (g s) -> p g s", g=3)
        MG = ar(0, 4096).rearrange("p (a s) -> p a s", a=8)
        SGP = ar(4096, 1024).rearrange("p (a s) -> p a s", a=2)
        SGA = ar(5120, 1024).rearrange("p (a s) -> p a s", a=2)
        T1 = ar(6144, 1024).rearrange("p (a s) -> p a s", a=2)
        T2 = ar(7168, 1024).rearrange("p (a s) -> p a s", a=2)
        XN = ar(0, 4096).rearrange("p (c n) -> p c n", c=NC)
        FT = ar(4096, 1024).rearrange("p (b s) -> p b s", b=2)
        RL = ar(5120, 2048).rearrange("p (b a s) -> p b a s", b=2, a=2)
        SQ = ar(7168, 2048).rearrange("p (b a s) -> p b a s", b=2, a=2)

        ACC = ar(9216, 6144)
        ADA = ar(15360, 4096).rearrange("p (b n) -> p b n", b=2)
        NFB = ar(19456, 1024)
        MROW = ar(5120, 4096, 1)
        V2 = ar(0, 4096).rearrange("p (c n) -> p c n", c=NC)
        G2 = ar(4096, 4096).rearrange("p (a s) -> p a s", a=8)
        RQK = ar(8192, 3072).rearrange("p (a s) -> p a s", a=6)
        HQ = ar(11264, 1536).rearrange("p (a s) -> p a s", a=3)
        HF = ar(12800, 1536).rearrange("p (a s) -> p a s", a=3)
        HK = ar(14336, 1536).rearrange("p (a s) -> p a s", a=3)
        PERM = ar(15360, 128)
        GQ, GK, GF = ar(15872, 512), ar(16384, 512), ar(16896, 512)
        TRG = ar(17408, 2048).rearrange("p (a s) -> p a s", a=4)
        SG = ar(17408, 2048).rearrange("p (b a s) -> p b a s", b=2, a=2)
        RT = ar(19456, 512)
        GA = ar(19456, 512, 16)
        COS, SINS = ar(19968, 512), ar(20480, 512)
        AB = ar(17408, 2560).rearrange("p (b n) -> p b n", b=2)
        DT = ar(19968, 512)
        SQT = ar(20480, 512)
        UB, PP = ar(8192, 512), ar(8704, 512)
        QKL = ar(9216, 1024).rearrange("p (b s) -> p b s", b=2)
        MASK = ar(10240, 1024).bitcast(U32).rearrange("p (l s) -> p l s", l=8)
        GMB = ar(17408, 1024)
        ROW_A, ROW_B, ROW_N = ar(4096, 1024), ar(5120, 1024), ar(6144, 1024)
        WR = ar(7168, KD * N_LOG)
        TRI, ONES, TOK = ar(7680, P), ar(7808, P), ar(7936, NC)
        T64, JHOT, BHOT = ar(8064, 64), ar(8192, 512).rearrange("p (x j) -> p x j", x=8), ar(8704, 416).rearrange("p (x b) -> p x b", x=8)
        GE = ar(9216, 416).rearrange("p (x b) -> p x b", x=8)
        SLX = ar(9728, 256).rearrange("p (x e) -> p x e", x=8)
        POSX = ar(9984, 128).rearrange("p (c e) -> p c e", c=NC)
        OHS = ar(10112, 128).rearrange("p (c e) -> p c e", c=NC)
        NBC = ar(10240, 256).rearrange("p (e n) -> p e n", e=N_EXP)
        ECMP = ar(10496, 52 * N_EXP, 1).rearrange("p (b e) -> p b e", b=52)
        EXRAW = [ar(0, E_UNIT), ar(E_UNIT, E_UNIT)]
        ROW_G, ROW_F = ar(12288, 1024), ar(13312, 1024)
        XG = ar(14336, 2048, BLOCK).rearrange("p (b n) -> p b n", b=2)
        YB = ar(16384, 2048, BLOCK).rearrange("p (b n) -> p b n", b=2)
        SGM, HR = ar(18432, 256, BLOCK), ar(18688, 256, BLOCK)
        YC = ar(0, 8192).rearrange("p (c k n) -> p c k n", c=NC, k=2)
        YW = ar(8192, 4096).rearrange("p (c n) -> p c n", c=NC)
        LG = ar(19456, 4 * N_LOG).rearrange("p (c n) -> p c n", c=NC)
        GPAD = ar(19600, 32).rearrange("p (c n) -> p c n", c=NC)
        GTOP = ar(19632, 32).rearrange("p (c n) -> p c n", c=NC)
        GTI = ar(19664, 32).bitcast(U32).rearrange("p (c n) -> p c n", c=NC)
        OHG = ar(19696, 16).rearrange("p (c n) -> p c n", c=NC)
        EIG = ar(19712, 128).rearrange("p (c g e) -> p c g e", c=NC, g=4)
        ELOG = ar(19840, 32).rearrange("p (c n) -> p c n", c=NC)
        ETOP = ar(19872, 32).rearrange("p (c n) -> p c n", c=NC)
        ETI = ar(19904, 32).bitcast(U32).rearrange("p (c n) -> p c n", c=NC)
        RS = ar(19936, 64).rearrange("p (x c) -> p x c", c=NC)
        OH = ar(20000, 256).rearrange("p (k c e) -> p k c e", k=2, c=NC)
        NB, ENDA, ENDB = ar(20256, 32), ar(20288, 64), ar(20352, 64)
        SLOT, BP = ar(20416, 8), ar(20424, 8)
        SLOTI = ar(20432, 8).bitcast(U32)
        B_LOG = ar(20440, N_LOG)
        IOTA = ar(20480, 64)
        IDXT = ar(20544, 52, BLOCK).bitcast(U32)
        IDXC = ar(20600, 2, BLOCK).bitcast(U32)
        EB, EBI = ar(20608, 52, 1), ar(20664, 52, 1).bitcast(I32)
        NR, NRI = ar(20720, 32, 1), ar(20756, 1, 1).bitcast(I32)
        WU = lambda w, u: w[:, 4 * u:4 * u + 4, :].rearrange("p k s -> p (k s)")
        EHI = [[WH[:, 0, :], WH[:, 1, :], WU(UH, 0)], [WU(UH, 1), WU(VH, 0), WU(VH, 1)]]
        ELO = [[WL[:, 0, :], WL[:, 1, :], WU(UL, 0)], [WU(UL, 1), WU(VL, 0), WU(VL, 1)]]
        XTH = ATH[:, 0, :].rearrange("p (k s) -> p k s", k=KD)
        XTL = ATL[:, 0, :].rearrange("p (k s) -> p k s", k=KD)
        HTH = ATH[:, 1, 0:2 * BLOCK].rearrange("p (k s) -> p k s", k=2)
        HTL = ATL[:, 1, 0:2 * BLOCK].rearrange("p (k s) -> p k s", k=2)
        TMPK = ar(18432, 1024).rearrange("p (b s) -> p b s", b=2)

        loaded = [sem("loaded0"), sem("loaded1")]
        hi_ready, lo_ready, unit_done = sem("hi_ready"), sem("lo_ready"), sem("unit_done")
        const_in = sem("const_in")
        stored = sem("stored")
        dve_link, pool_link = sem("dve_link"), sem("pool_link")
        z_out = sem("z_out")
        block = ctx.enter_context(nc.Block())

        class Link:
            def __init__(self, eng, s):
                self.eng, self.s, self.n = eng, s, 0

            def __call__(self, ins):
                self.n += 1
                ins.then_inc(self.s, 1)
                self.eng.wait_ge(self.s, self.n)

            def inc(self, ins):
                self.n += 1
                ins.then_inc(self.s, 1)

            def wait(self):
                self.eng.wait_ge(self.s, self.n)

        norm_sq, norm_rs, norm_xn, norm_tr, norm_ft, norm_hi, norm_lo = [
            sem("norm_" + x) for x in ("sq", "rstd", "scaled", "transposed", "gained", "hi", "lo")]

        def norm_act(act, j):
            for c in range(NC):
                act.activation(XN[:, c, :], X[:, c, :], ACT.Square, accum_out=SS[:, c:c + 1]).then_inc(norm_sq, 1)
            act.wait_ge(norm_rs, 2 * j + 2)
            for c in range(NC):
                act.activation(XN[:, c, :], X[:, c, :], ACT.Copy, scale=SS[:, 4 + c:5 + c]).then_inc(norm_xn, 1)
            for k in range(KD):
                act.wait_ge(norm_ft, KD * j + k + 1)
                act.activation(UH[:, k, :], FT[:, k % 2, :], ACT.Copy).then_inc(norm_hi, 1)

        def norm_pool(pool, j):
            pool.wait_ge(norm_sq, NC * j + NC)
            pool.tensor_scalar(SS[:, 0:4], SS[:, 0:4], 1.0 / D, EPS, ALU.mult, ALU.add).then_inc(norm_rs, 1)
            pool.wait_ge(norm_rs, 2 * j + 1)
            pool.tensor_tensor(SS[:, 4:8], SS[:, 0:4], COLS[:, 60:64], ALU.pow).then_inc(norm_rs, 1)
            for k in range(KD):
                pool.wait_ge(norm_hi, KD * j + k + 1)
                pool.tensor_tensor(UL[:, k, :], FT[:, k % 2, :], UH[:, k, :].bitcast(F32), ALU.subtract).then_inc(norm_lo, 1)

        def norm_pe(pe, j):
            pe.wait_ge(norm_xn, NC * j + NC)
            for k in range(KD):
                b = 4 + k % 4
                if k >= 4:
                    pe.wait_ge(norm_ft, KD * j + k - 3)
                for c in range(NC):
                    last = pe.transpose(PS[:, b, c * P:(c + 1) * P], XN[:, c, k * P:(k + 1) * P], IDN[:, :])
                last.then_inc(norm_tr, 1)

        def norm_dve(dve, j, gain=None):
            for k in range(KD):
                dve.wait_ge(norm_tr, KD * j + k + 1)
                if k >= 2:
                    dve.wait_ge(norm_lo, KD * j + k - 1)
                if gain is not None:
                    dve.tensor_scalar(FT[:, k % 2, :], PS[:, 4 + k % 4, :], COLS[:, gain + k:gain + k + 1], None, ALU.mult).then_inc(norm_ft, 1)
                else:
                    dve.tensor_scalar(FT[:, k % 2, :], PS[:, 4 + k % 4, :], MODC[:, 8 + k:9 + k], MODC[:, k:k + 1],
                                      ALU.mult, ALU.add).then_inc(norm_ft, 1)

        def split_hi(act, base, i, s):
            act.wait_ge(loaded[1 - s], 16 * i + 16 * (base // 2 + s + 1))
            if not (isinstance(i, int) and base + 2 * i + s == 0):
                act.wait_ge(unit_done, 2 * i + base + s)
            act.activation(WH[:, 1 - s, :], RAW[:, 1 - s, :], ACT.Copy).then_inc(hi_ready, 1)

        def split_lo(dve, base, i, s):
            dve.wait_ge(hi_ready, 2 * i + base + s + 2)
            dve.tensor_tensor(WL[:, 1 - s, :], RAW[:, 1 - s, :], WH[:, 1 - s, :].bitcast(F32),
                              ALU.subtract).then_inc(lo_ready, 1)

        def unit_is_in(pe, n):
            pe.wait_ge(hi_ready, n + 1)
            pe.wait_ge(lo_ready, n + 1)

        def three(pe, out, a, b, start, stop):
            pe.matmul(out, a[0], b[0], start=start, stop=False)
            pe.matmul(out, a[0], b[1], start=False, stop=False)
            return pe.matmul(out, a[1], b[0], start=False, stop=stop)

        def wpair(slot, off, n, rows=P):
            return WH[0:rows, slot, off:off + n], WL[0:rows, slot, off:off + n]

        def feature(pe, slot, m, mw, width, src, bank, rows=P, kc=KD):
            for k in range(kc):
                last = three(pe, PS[0:mw, bank, :], wpair(slot, k * width + m * mw, mw, rows),
                             (src[0][0:rows, k, :], src[1][0:rows, k, :]), k == 0, k == kc - 1)
            return last

        def tokens(pe, slot, src, ks, bank, chunk, start, stop):
            for c in range(NC):
                for k in range(4):
                    last = three(pe, PS[:, bank + c, :], (src[0][:, ks + k, P * c:P * c + P], src[1][:, ks + k, P * c:P * c + P]),
                                 wpair(slot, 512 * k, 512), start and k == 0, stop and k == 3)
                if stop and c < NC - 1:
                    last.then_inc(chunk, 1)
            last.then_inc(unit_done, 1)

        def peeled(eng, count, body):
            body(0)
            with eng.Fori(1, count) as i:
                body(i)

        def first(i):
            return isinstance(i, int) and i == 0

        U, V, AT = (UH, UL), (VH, VL), (ATH, ATL)

        pooled, pool_hi, pool_lo = sem("pooled"), sem("pool_hi"), sem("pool_lo")
        mix_out, mixed_hi, mixed_lo = [sem(x) for x in ("mix_out", "mixed_hi", "mixed_lo")]
        att_s, att_m, att_e, att_t, att_p, att_o, att_c = [
            sem("att_" + x) for x in ("scored", "maxed", "exped", "transposed", "copied", "summed", "out")]
        st_tr, st_row = sem("stat_tr"), sem("stat_row")
        nm_bc, l_bc, eg_d, eg_e, den_d, wsum, at_d, at_hi, at_lo = [sem(x) for x in (
            "max_bc", "sum_bc", "group_diff", "group_exp", "denominator", "weighted", "att_merged", "at_hi", "at_lo")]
        gp_sig, ga_sig, t1_d, t2_d, mg_d = [sem(x) for x in ("gp_sig", "ga_sig", "pool_gated", "att_gated", "branches")]
        mg_hi, mg_lo, wo_chunk, wo_add = sem("mg_hi"), sem("mg_lo"), sem("wo_chunk"), sem("wo_add")
        relu_d, sq_d, hid_hi, hid_lo, mo_chunk, mo_add = [sem(x) for x in (
            "relu_done", "square_done", "hid_hi", "hid_lo", "mo_chunk", "mo_add")]

        ada_in, ada_d, acc_init = [sem("ada_in0"), sem("ada_in1")], sem("ada_done"), sem("acc_init")
        b_in = sem("b_ada_in")
        ca_sig, ca_d, lb_sub, lb_exp, lb_d = [sem(x) for x in ("c_sigmoid", "c_done", "lb_diff", "lb_exp", "lb_done")]
        late_in, br_sq, br_rs, x2_d = sem("late_in"), sem("between_sq"), sem("between_rs"), sem("x2_done")
        mod_mm, mrow_mm, mrow_d, mrow_out = [sem(x) for x in ("mod_cols_mm", "mod_row_mm", "mod_row_done", "mod_row_out")]
        pos_in, trig_r, trig_d = sem("pos_in"), sem("trig_arg"), sem("trig_done")
        z2_out, gsig, g2_out = sem("z2_out"), sem("gate_sig"), sem("gate_out")
        perm_mm, rope_s, rope_c, rope_d = sem("perm_mm"), sem("rope_sin"), sem("rope_cos"), sem("rope_done")
        hsig, hq_d, hf_d = sem("h_sig"), sem("hq_done"), sem("hf_done")
        ga_mm, ga_x, ga_l, ga_m, ga_d = [sem(x) for x in ("ga_mm", "ga_sum", "ga_log", "ga_min", "ga_done")]
        d_in, ret_s, ret_a, ret_o = sem("decay_in"), sem("ret_scored"), sem("ret_decayed"), sem("ret_summed")
        mask_in, lvl_qk, lvl_s, lvl_a, lvl_b, pass_o = [sem(x) for x in (
            "mask_in", "level_qk", "level_scored", "level_diag", "level_off", "pass_summed")]
        a_zero, pass_h = sem("a_zero"), sem("pass_head")
        hn_sq, hn_mm, hn_rt, hn_d, hn_hi, hn_lo = [sem("head_" + x) for x in ("sq", "mean", "root", "gated", "hi", "lo")]
        gm_in, wo2_chunk, wo2_t, wo2_add = sem("gm_in"), sem("wo2_chunk"), sem("wo2_t"), sem("wo2_add")
        moe_in, wr_hi, wr_lo, h2_m, h2_d, lg_mm = [sem(x) for x in ("moe_in", "router_hi", "router_lo", "h2_scaled", "h2_done", "logits_mm")]
        rt_arg, rt_exp = sem("route_arg"), sem("route_exp")
        oh_d, pos_mm, jb_d, idx_mm, route_d, idx_d = [sem("route_" + x) for x in ("onehot", "pos_mm", "slots", "idx_mm", "experts", "idx")]
        hd_out, xg_in = sem("h2_out"), [sem("x_in0"), sem("x_in1")]
        xt_tr, xt_hi, xt_lo = [sem("xt_" + x) for x in ("tr", "hi", "lo")]
        m_sig, m_silu, m_hid, ht_tr, m_hi, m_lo, y_cp = [sem("expert_" + x) for x in ("sig", "silu", "hid", "tr", "hi", "lo", "y")]
        y_fill, m_down = sem("y_fill"), sem("expert_down")
        xw_in = [[loaded[x], ada_in[x], sem(f"expert_down_in{x}")] for x in range(2)]
        xw_base = (16 * (M0 // 2), 16 * 12, 0)
        y_out, yc_in = [sem("y_out0"), sem("y_out1")], [sem(f"yc_in{c}") for c in range(NC)]
        fin_x, fin_d = sem("final_x"), sem("final_done")

        heads = [(g, q, hh) for g in range(3) for q in range(2) for hh in range(2)]

        def blks(g):
            return [(0, 1)] + [(c, b) for c in range(1, 4) for b in range(2)] if g == 0 else [(c, 0) for c in range(4)]

        def st_col(g, q, hh):
            return (0, 32, 40)[g] + 2 * q + hh

        NCONST = 6

        @block.sync
        def _(sp):
            sp.dma_start(X[:, :, :], t["x"]).then_inc(const_in, 16)
            sp.dma_start(IDN[:, :], t["ident"]).then_inc(const_in, 16)
            sp.dma_start(COLS[:, :], t["cols"]).then_inc(const_in, 16)
            for s in range(2):
                sp.dma_start(RAW[:, s, :], t["w"][s, :, :]).then_inc(loaded[s], 16)
            sp.dma_start(PINV, t["pool_inv"]).then_inc(const_in, 16)
            sp.dma_start(BIAS, t["bias"]).then_inc(const_in, 16)
            sp.dma_start(ONESB[:, :], t["ones_block"]).then_inc(const_in, 16)
            sp.dma_start(NFB, t["norm_final_g"].partition_broadcast(P)).then_inc(late_in, 16)

            def stream(base, i, s):
                sp.wait_ge(hi_ready, 2 * i + base + s + 1)
                sp.wait_ge(lo_ready, 2 * i + base + s + 1)
                sp.dma_start(RAW[:, s, :], t["w"][bass.ds(2 * i + base + s + 2, 1), :, :].rearrange("o p n -> p (o n)")).then_inc(loaded[s], 16)
            with sp.Fori(0, (G0 - 2) // 2) as i:
                for s in range(2):
                    stream(0, i, s)

            def mlp(gi):
                for s in range(8):
                    stream(G0 - 2, 4 * gi + s // 2, s % 2)
                    if s < 6:
                        if first(gi) and s < 2:
                            sp.wait_ge(acc_init, 1)
                        else:
                            sp.wait_ge(ada_d, 6 * gi + s - 1)
                        sp.dma_start(ADA[:, s % 2, :], t["w_ada"][bass.ds(6 * gi + s, 1), :, :].rearrange("o p n -> p (o n)")).then_inc(ada_in[s % 2], 16)
            peeled(sp, 4, mlp)
            for n in range(H0, K0):
                stream(0, (n - 2) // 2, n % 2)
                if n == H0:
                    sp.wait_ge(ada_d, 24)
                    sp.dma_start(TRG[:, 0, :].bitcast(I32), t["positions"].partition_broadcast(P)).then_inc(pos_in, 16)
                    sp.wait_ge(mod_mm, 1)
                    sp.wait_ge(mrow_mm, 8)
                    sp.dma_start(PERM, t["perm"]).then_inc(pos_in, 16)
                    sp.wait_ge(mrow_d, 8)
                    sp.dma_start(t["mod_row"], MROW).then_inc(mrow_out, 16)
            stream(0, (K0 - 2) // 2, 0)
            stream(0, (K0 - 2) // 2, 1)
            for h in range(6):
                if h == 0:
                    sp.wait_ge(rope_d, 6)
                else:
                    sp.wait_ge(ret_a, h)
                sp.dma_start(DT, t["decay"][h, :, :]).then_inc(d_in, 16)
            used = 2 * S // BLOCK * BLOCK
            for r in range((MAX_BLOCKS * BLOCK - used) // S):
                sp.dma_start(t["y"][used + S * r:used + S * r + S, :].rearrange("(p c) n -> p c n", c=NC), t["x"]).then_inc(y_fill, 16)
            sp.wait_ge(ret_o, 6)
            sp.dma_start(MASK, t["masks"].bitcast(U32)).then_inc(mask_in, 16)
            sp.wait_ge(pass_o, 5)
            sp.wait_ge(mrow_out, 16)
            sp.dma_start(GMB, t["mod_row"][0, 0:D].partition_broadcast(P)).then_inc(gm_in, 16)
            stream(0, K0 // 2, 0)
            stream(0, K0 // 2, 1)
            sp.wait_ge(hn_lo, 8)
            for r, row in ((1, ROW_B), (2, ROW_A), (3, ROW_G)):
                sp.dma_start(row, t["mod_row"][0, D * r:D * r + D].partition_broadcast(P)).then_inc(moe_in, 16)
            sp.dma_start(ROW_N, t["norm_ffn"].partition_broadcast(P)).then_inc(moe_in, 16)
            sp.dma_start(ROW_F, t["norm_final_2"].partition_broadcast(P)).then_inc(moe_in, 16)
            sp.dma_start(WR, t["w_router"]).then_inc(moe_in, 16)
            sp.dma_start(B_LOG, t["b_router"].partition_broadcast(P)).then_inc(moe_in, 16)
            sp.dma_start(IOTA, t["iota"]).then_inc(moe_in, 16)
            sp.dma_start(AR[:, 7680:8128], t["route_consts"]).then_inc(moe_in, 16)
            for c in range(NC):
                sp.wait_ge(h2_d, c + 1)
                sp.dma_start(t["h2"][P * c:P * c + P, :], XN[:, c, :]).then_inc(hd_out, 16)
            sp.wait_ge(hd_out, 16 * NC)
            sp.wait_ge(norm_tr, KD * 3 + KD)
            sp.wait_ge(route_d, 1)
            n2 = sp.value_load(NRI, min_val=0, max_val=MAX_BLOCKS // 2 - 2) + 2

            def expert_weights(i, x):
                b = 2 * i + x
                if first(i) and x:
                    sp.wait_ge(idx_d, 1)
                e = sp.value_load(EBI[0:1, bass.ds(b, 1)], min_val=0, max_val=N_EXP - 1)
                for part in range(3):
                    w = slice(UNIT * part, UNIT * part + UNIT)
                    if not first(i):
                        sp.wait_ge(lo_ready, 3 * b + M0 + part - 5)
                    sp.dma_start(EXRAW[x][:, w], t["w_exp"][bass.ds(e, 1), :, w].rearrange("o p n -> p (o n)")).then_inc(xw_in[x][part], 16)
            for x in range(2):
                expert_weights(0, x)
            with sp.Fori(1, n2) as i:
                for x in range(2):
                    expert_weights(i, x)
            for c in range(NC):
                sp.wait_ge(fin_d, c + 1)
                sp.dma_start(t["out"][0, P * c:P * c + P, :], X[:, c, :]).then_inc(stored, 16)
            sp.wait_ge(stored, 16 * NC)

        def pt_copy(act, n):
            nb = len(blks(heads[n][0]))
            act.wait_ge(att_t, n + 1)
            if n >= 2:
                act.wait_ge(att_o, n - 1)
            act.activation(PTB[:, n % 2, 0:nb, :], PS[:, 4:6, :].rearrange("p b (c n) -> p (b c) n", c=4)[:, 0:nb, :],
                           ACT.Copy).then_inc(att_p, 1)

        def pair_out(act, n):
            g, q, hh = heads[n]
            if hh:
                act.wait_ge(att_o, n + 1)
                src = PS[:, 6 + (n // 2) % 2, :]
                dst = OT[:, q, g, :]
                if g:
                    src = src.rearrange("p (r i) -> p r i", r=4)
                    dst = dst.rearrange("p (i r) -> p r i", r=4)
                act.activation(dst, src, ACT.Copy).then_inc(att_c, 1)

        @block.scalar
        def _(act):
            act.wait_ge(const_in, 16 * NCONST)
            act.wait_ge(loaded[0], 16)
            act.activation(WH[:, 0, :], RAW[:, 0, :], ACT.Copy).then_inc(hi_ready, 1)
            norm_act(act, 0)
            for n in range(A0, B0):
                split_hi(act, 0, n // 2, n % 2)
                act.wait_ge(unit_done, n + 1)
                act.activation(PZ[:, 2 * n:2 * n + 2, :], PS[0:PG, 2 * (n % 2):2 * (n % 2) + 2, :], ACT.Copy).then_inc(z_out, 1)
            with act.Fori(0, NU_B // 2) as i:
                for s in range(2):
                    split_hi(act, B0, i, s)
                    act.wait_ge(unit_done, 2 * i + B0 + s + 1)
                    act.activation(QK[:, bass.ds(4 * i + 2 * s, 2), :], PS[:, 2 * s:2 * s + 2, :], ACT.Copy).then_inc(z_out, 1)
            for n in range(C0, D0):
                split_hi(act, 0, n // 2, n % 2)
                act.wait_ge(unit_done, n + 1)
                j = n - C0
                act.activation(VT[:, :, 256 * j:256 * j + 256],
                               PS[:, 2 * (n % 2):2 * (n % 2) + 2, :].rearrange("p b (c n) -> p (b c) n", c=2), ACT.Copy).then_inc(z_out, 1)
                if n == C0:
                    act.wait_ge(pooled, 1)
                    act.activation(VH[0:PG, :, :], PZ, ACT.Copy).then_inc(pool_hi, 1)
            split_hi(act, 0, D0 // 2, D0 % 2)
            act.wait_ge(unit_done, E0)
            for a in range(8):
                act.activation(PZ[:, a, :], PS[0:PG, a, :], ACT.Copy, scale=COLS[0:PG, 8 + a:9 + a]).then_inc(mix_out, 1)
            act.wait_ge(mix_out, 8)
            act.activation(VH[0:PG, :, :], PZ, ACT.Copy).then_inc(mixed_hi, 1)
            for n, (g, q, hh) in enumerate(heads):
                act.wait_ge(att_m, n + 1)
                w = 256 if g == 0 else P
                col = st_col(g, q, hh)
                for c in range(NC):
                    w0 = P if g == 0 and c == 0 else 0
                    act.activation(SBUFS[:, n % 2, c, w0:w], SBUFS[:, n % 2, c, w0:w], ACT.Exp,
                                   bias=ST[:, c, col:col + 1], accum_out=ST[:, c, col + 4:col + 5]).then_inc(att_e, 1)
                if n >= 1:
                    pt_copy(act, n - 1)
                if n >= 2:
                    pair_out(act, n - 2)
            pt_copy(act, 11)
            pair_out(act, 11)
            for q in range(2):
                act.wait_ge(eg_d, 3 * (q + 1))
                act.activation(EG, EG, ACT.Exp).then_inc(eg_e, 1)
                act.wait_ge(at_d, q + 1)
                act.activation(ATH[:, q, :], MN, ACT.Copy).then_inc(at_hi, 1)

            def branches(j):
                for s in range(4):
                    split_hi(act, E0, 2 * j + s // 2, s % 2)
                    if s == 0:
                        act.wait_ge(unit_done, 4 * j + E0 + 1)
                        if not first(j):
                            act.wait_ge(t1_d, j)
                        act.activation(SGP, PS[:, 0:2, :], ACT.Sigmoid).then_inc(gp_sig, 1)
                    if s == 2:
                        act.wait_ge(unit_done, 4 * j + E0 + 3)
                        if not first(j):
                            act.wait_ge(t2_d, j)
                        act.activation(SGA, PS[:, 4:6, :], ACT.Sigmoid).then_inc(ga_sig, 1)
            peeled(act, 4, branches)
            act.activation(CA[:, :], COLS[:, 24:32], ACT.Sigmoid).then_inc(ca_sig, 1)
            act.wait_ge(mg_d, 4)
            for k in range(KD):
                act.activation(UH[:, k, :], MG[:, k, :], ACT.Copy).then_inc(mg_hi, 1)
            for n in range(F0, G0):
                split_hi(act, 0, n // 2, n % 2)
            act.wait_ge(wo_add, 8)
            norm_act(act, 1)

            def mlp(gi):
                for s in range(8):
                    split_hi(act, G0, 4 * gi + s // 2, s % 2)
                    if s < 4:
                        act.wait_ge(unit_done, 8 * gi + G0 + s + 1)
                        act.activation(RL[:, s % 2, :, :], PS[:, 2 * (s % 2):2 * (s % 2) + 2, :], ACT.Relu).then_inc(relu_d, 1)
                        act.wait_ge(sq_d, 4 * gi + s + 1)
                        act.activation(VH[:, 2 * s:2 * s + 2, :], SQ[:, s % 2, :, :], ACT.Copy).then_inc(hid_hi, 1)
            with act.Fori(0, 4) as gi:
                mlp(gi)

            for c in range(NC):
                act.wait_ge(mo_add, 32)
                act.activation(XN[:, c, :], X[:, c, :], ACT.Square, accum_out=SS[:, c:c + 1]).then_inc(br_sq, 1)
            act.wait_ge(x2_d, 4)
            norm_act(act, 2)
            act.wait_ge(lb_sub, 1)
            act.activation(LBS[:, 3:6], LBS[:, 0:3], ACT.Exp).then_inc(lb_exp, 1)
            act.wait_ge(trig_r, 2)
            act.activation(SINS, TRG[:, 2, :], ACT.Sin, scale=COLS[:, 53:54]).then_inc(trig_d, 1)
            act.activation(COS, TRG[:, 3, :], ACT.Sin).then_inc(trig_d, 1)
            for n in range(H0, I0):
                split_hi(act, 0, n // 2, n % 2)
                act.wait_ge(unit_done, n + 1)
                j = n - H0
                act.activation(V2[:, :, 256 * j:256 * j + 256],
                               PS[:, 2 * (n % 2):2 * (n % 2) + 2, :].rearrange("p b (c n) -> p (b c) n", c=2), ACT.Copy).then_inc(z2_out, 1)
            act.wait_ge(trig_d, 2)
            for n in range(I0, J0):
                split_hi(act, 0, n // 2, n % 2)
                act.wait_ge(unit_done, n + 1)
                if n >= I0 + 2:
                    act.wait_ge(g2_out, n - I0 - 1)
                act.activation(SG[:, n % 2, :, :], PS[:, 2 * (n % 2):2 * (n % 2) + 2, :], ACT.Sigmoid).then_inc(gsig, 1)
            for n in range(J0, J0 + 3):
                split_hi(act, 0, n // 2, n % 2)
                act.wait_ge(unit_done, n + 1)
                j = n - J0
                act.activation(RQK[:, 2 * j:2 * j + 2, :], PS[:, 2 * (n % 2):2 * (n % 2) + 2, :], ACT.Copy).then_inc(z2_out, 1)
            for n in range(J0 + 3, J0 + 6):
                split_hi(act, 0, n // 2, n % 2)
                act.wait_ge(unit_done, n + 1)
                j = n - J0 - 3
                act.wait_ge(g2_out, 4)
                if j == 2:
                    act.wait_ge(hf_d, 3)
                act.activation(SG[:, n % 2, :, :], PS[:, 2 * (n % 2):2 * (n % 2) + 2, :], ACT.Sigmoid).then_inc(hsig, 1)
                if j == 2:
                    act.wait_ge(perm_mm, 6)
                act.activation(HK[:, j, :], PS[:, 2 * (n % 2) + 1, :], ACT.Sigmoid, scale=-1.0).then_inc(hsig, 1)
            n = J0 + 6
            split_hi(act, 0, n // 2, n % 2)
            act.wait_ge(unit_done, n + 1)
            act.activation(GQ, PS[:, 0, :], ACT.Copy, scale=float(np.float32(32.0 ** -0.5))).then_inc(z2_out, 1)
            act.activation(GK, PS[:, 1, :], ACT.Copy).then_inc(z2_out, 1)
            n = J0 + 7
            split_hi(act, 0, n // 2, n % 2)
            act.wait_ge(ga_mm, 1)
            act.wait_ge(rope_d, 6)
            act.activation(GA, PS[0:16, 2, :], ACT.Copy).then_inc(z2_out, 1)
            act.wait_ge(unit_done, n + 1)
            act.wait_ge(hf_d, 9)
            act.activation(TRG[:, 0, :], PS[:, 3, :], ACT.Identity, bias=COLS[:, 51:52]).then_inc(ga_x, 1)
            act.wait_ge(ga_x, 1)
            act.activation(TRG[:, 1, :], TRG[:, 0, :], ACT.Abs).then_inc(ga_l, 1)
            act.wait_ge(ga_l, 1)
            act.activation(TRG[:, 1, :], TRG[:, 1, :], ACT.Exp, scale=-1.0).then_inc(ga_l, 1)
            act.wait_ge(ga_l, 2)
            act.activation(TRG[:, 1, :], TRG[:, 1, :], ACT.Ln, bias=1.0).then_inc(ga_l, 1)
            act.wait_ge(ga_m, 1)
            act.activation(GF, TRG[:, 2, :], ACT.Exp, scale=1.0 / 16.0).then_inc(ga_d, 1)

            def head_norm(tile):
                act.wait_ge(ret_o, 2 * tile + 2) if tile < 3 else act.wait_ge(pass_o, tile - 2)
                if tile:
                    act.wait_ge(hn_d, 3 * tile)
                act.activation(SQT, PS[:, 6, :], ACT.Square).then_inc(hn_sq, 1)
                act.wait_ge(hn_mm, tile + 1)
                act.activation(SQT, PS[:, 7, :], ACT.Sqrt, bias=COLS[:, 58:59]).then_inc(hn_rt, 1)
                act.wait_ge(hn_d, 3 * tile + 3)
                act.activation(VH[:, tile, :], G2[:, tile, :], ACT.Copy).then_inc(hn_hi, 1)
            for tile in range(3):
                head_norm(tile)
            for p in range(5):
                if p == 0:
                    act.wait_ge(ret_o, 6)
                for lev in (7, 8):
                    for hh in range(2):
                        cnt = 20 * p + 2 * (lev + 1) + hh
                        act.wait_ge(lvl_s, cnt + 1)
                        if p and lev == 7:
                            act.wait_ge(pass_o, p)
                        b = cnt % 6
                        if lev == 7:
                            act.activation(AB[:, hh, 512:640], PS[:, b, 0:128], ACT.Copy).then_inc(lvl_b, 1)
                            act.activation(AB[:, hh, 1152:1280], PS[:, b, 128:256], ACT.Copy).then_inc(lvl_b, 1)
                        else:
                            act.activation(AB[:, hh, 640:896], PS[:, b, 0:256], ACT.Copy).then_inc(lvl_b, 1)
                            act.activation(AB[:, hh, 896:1152], PS[:, b, 256:512], ACT.Copy).then_inc(lvl_b, 1)
                head_norm(3 + p)
            for n in range(K0, M0 - 1):
                split_hi(act, 0, n // 2, n % 2)
            act.wait_ge(wo2_add, 8)
            for c in range(NC):
                act.activation(XN[:, c, :], X[:, c, :], ACT.Square, accum_out=SS[:, c:c + 1]).then_inc(norm_sq, 1)
            act.wait_ge(moe_in, 144)
            act.activation(ATH[:, 0, 0:KD * N_LOG], WR, ACT.Copy).then_inc(wr_hi, 1)
            act.wait_ge(norm_rs, 2 * 3 + 2)
            for c in range(NC):
                act.activation(XN[:, c, :], X[:, c, :], ACT.Copy, scale=SS[:, 4 + c:5 + c]).then_inc(norm_xn, 1)
            for k in range(KD):
                act.wait_ge(norm_tr, KD * 3 + k + 1)
                act.activation(UH[:, k, :], PS[:, 4 + k % 4, :], ACT.Copy).then_inc(norm_hi, 1)
            act.wait_ge(rt_arg, 1)
            act.activation(RS[:, 4:8, :], RS[:, 0:4, :], ACT.Exp).then_inc(rt_exp, 1)
            act.wait_ge(rt_arg, 2)
            act.activation(RS[:, 9, :], RS[:, 8, :], ACT.Exp).then_inc(rt_exp, 1)

            act.wait_ge(route_d, 1)
            n2 = act.value_load(NRI, min_val=0, max_val=MAX_BLOCKS // 2 - 2) + 2

            def x_hi(b):
                act.wait_ge(xt_tr, b + 1)
                act.activation(ATH[:, 0, :], PS[:, 2, :], ACT.Copy).then_inc(xt_hi, 1)

            def w_hi(i, x, part):
                b = 2 * i + x
                act.wait_ge(xw_in[x][part], 16 * i + xw_base[part] + 16)
                if not first(i):
                    if part < 2:
                        act.wait_ge(unit_done, 2 * b + M0 + part - 3)
                    else:
                        act.wait_ge(m_down, b - 1)
                act.activation(EHI[x][part], EXRAW[x][:, UNIT * part:UNIT * part + UNIT], ACT.Copy).then_inc(hi_ready, 1)

            def gate(b, x):
                act.wait_ge(unit_done, 2 * b + M0 + 2)
                act.activation(SGM, PS[0:BLOCK, x, 0:256], ACT.Sigmoid).then_inc(m_sig, 1)

            def hidden_hi(b):
                act.wait_ge(ht_tr, b + 1)
                act.activation(HTH, PS[:, 3, 0:2 * BLOCK].rearrange("p (k s) -> p k s", k=2), ACT.Copy).then_inc(m_hi, 1)

            def out(i, x):
                b = 2 * i + x - 2
                act.wait_ge(m_down, b + 1)
                if not (isinstance(i, int) and i == 1):
                    act.wait_ge(y_out[x], 16 * (i - 1))
                act.activation(YB[:, x, :], PS[0:BLOCK, 4 + 2 * x:6 + 2 * x, :].rearrange("p b n -> p (b n)"), ACT.Copy).then_inc(y_cp, 1)
                act.wait_ge(y_cp, b + 1)
                act.dma_start(t["y"][bass.ds(b * BLOCK, BLOCK), :], YB[:, x, :]).then_inc(y_out[x], 16)

            def step(i, x):
                w_hi(i, x, 0)
                w_hi(i, x, 1)
                if not (first(i) and x == 0):
                    gate(2 * i + x - 1, 1 - x)
                    x_hi(2 * i + x)
                    if not first(i):
                        out(i, x)
                    hidden_hi(2 * i + x - 1)
                w_hi(i, x, 2)
            x_hi(0)
            act.wait_ge(y_fill, 16 * ((MAX_BLOCKS - 2 * S // BLOCK) * BLOCK // S))
            for i in range(2):
                for x in range(2):
                    step(i, x)
            with act.Fori(2, n2) as i:
                for x in range(2):
                    step(i, x)
            gate(2 * n2 - 1, 1)
            x_hi(2 * n2)
            out(n2, 0)
            hidden_hi(2 * n2 - 1)
            out(n2, 1)
            act.wait_ge(fin_x, NC)
            for c in range(NC):
                act.activation(XN[:, c, :], X[:, c, :], ACT.Square, accum_out=SS[:, c:c + 1]).then_inc(norm_sq, 1)
        @block.vector
        def _(dve):
            link = Link(dve, dve_link)
            dve.wait_ge(const_in, 16 * NCONST)
            dve.wait_ge(hi_ready, 1)
            dve.tensor_tensor(WL[:, 0, :], RAW[:, 0, :], WH[:, 0, :].bitcast(F32), ALU.subtract).then_inc(lo_ready, 1)
            norm_dve(dve, 0, 0)
            for n in range(A0, B0):
                split_lo(dve, 0, n // 2, n % 2)
            with dve.Fori(0, NU_B // 2) as i:
                for s in range(2):
                    split_lo(dve, B0, i, s)
            for n in range(C0, D0):
                split_lo(dve, 0, n // 2, n % 2)
                if n == C0:
                    dve.wait_ge(pool_hi, 1)
                    dve.tensor_tensor(VL[0:PG, :, :], PZ, VH[0:PG, :, :].bitcast(F32), ALU.subtract).then_inc(pool_lo, 1)
            split_lo(dve, 0, D0 // 2, D0 % 2)
            dve.wait_ge(mixed_hi, 1)
            dve.tensor_tensor(VL[0:PG, :, :], PZ, VH[0:PG, :, :].bitcast(F32), ALU.subtract).then_inc(mixed_lo, 1)
            dve.wait_ge(mixed_lo, 1)
            link.inc(dve.memset(SBUFS[:, :, 0, 0:P], NEG))
            link(dve.memset(ST, 0.0))
            for n, (g, q, hh) in enumerate(heads):
                dve.wait_ge(att_s, n + 1)
                if n >= 2:
                    dve.wait_ge(att_t, n - 1)
                b = 2 * (n % 2)
                hd = 2 * q + hh
                if g == 0:
                    tab = BIAS[:, 256 * hd:256 * hd + 256]
                    link.inc(dve.scalar_tensor_tensor(SBUFS[:, n % 2, 0, P:2 * P], PS[:, b, P:2 * P], 0.125, tab[:, P:2 * P], ALU.mult, ALU.add))
                    link(dve.scalar_tensor_tensor(SBUFS[:, n % 2, 1:4, :],
                                                  PS[:, b:b + 2, :].rearrange("p b (c n) -> p (b c) n", c=2)[:, 1:4, :], 0.125,
                                                  tab.unsqueeze(1).broadcast_to([P, 3, 256]), ALU.mult, ALU.add))
                    w = 256
                else:
                    o = 1024 + 512 * (g - 1) + P * hd
                    link(dve.scalar_tensor_tensor(SBUFS[:, n % 2, :, 0:P], PS[:, b, :].rearrange("p (c n) -> p c n", c=4), 0.125,
                                                  BIAS[:, o:o + P].unsqueeze(1).broadcast_to([P, 4, P]), ALU.mult, ALU.add))
                    w = P
                col = st_col(g, q, hh)
                dve.tensor_reduce(ST[:, :, col:col + 1], SBUFS[:, n % 2, :, 0:w], AX.X, ALU.max, negate=True).then_inc(att_m, 1)
            dve.wait_ge(st_tr, 1)
            dve.tensor_copy(RW[0:32, :], PS[0:32, 0, :]).then_inc(st_row, 1)
            dve.tensor_copy(RW[32:48, :].rearrange("p (i r) -> p r i", r=4), PS[32:48, 0, :].rearrange("p (r i) -> p r i", r=4)).then_inc(st_row, 1)
            for q in range(2):
                dve.wait_ge(nm_bc, q + 1)
                if q:
                    dve.wait_ge(at_lo, 1)
                link(dve.tensor_copy(MN, PS[:, 1, :]))
                link(dve.tensor_tensor(MN, MN, PS[:, 2, :], ALU.min))
                link(dve.tensor_tensor(MN, MN, PS[:, 3, :], ALU.min))
                if q:
                    dve.wait_ge(wsum, 3)
                for g in range(3):
                    dve.tensor_tensor(EG[:, g, :], MN, PS[:, 1 + g, :], ALU.subtract).then_inc(eg_d, 1)
                dve.wait_ge(eg_e, q + 1)
                dve.wait_ge(l_bc, q + 1)
                dve.tensor_tensor(DG, EG, PS[:, 4:7, :], ALU.mult).then_inc(den_d, 1)
                dve.wait_ge(den_d, q + 1)
                link(dve.tensor_tensor(MN, DG[:, 0, :], DG[:, 1, :], ALU.add))
                link(dve.tensor_tensor(MN, MN, DG[:, 2, :], ALU.add))
                link(dve.reciprocal(MN, MN))
                dve.wait_ge(wsum, 3 * (q + 1))
                dve.tensor_tensor(MN, MN, OT[:, q, 0, :], ALU.mult).then_inc(at_d, 1)
                dve.wait_ge(at_hi, q + 1)
                dve.tensor_tensor(ATL[:, q, :], MN, ATH[:, q, :].bitcast(F32), ALU.subtract).then_inc(at_lo, 1)

            def branches(j):
                for s in range(4):
                    split_lo(dve, E0, 2 * j + s // 2, s % 2)
                    if s == 1:
                        dve.wait_ge(unit_done, 4 * j + E0 + 2)
                        dve.wait_ge(gp_sig, j + 1)
                        if not first(j):
                            dve.wait_ge(mg_d, j)
                        dve.tensor_tensor(T1, SGP, PS[:, 2:4, :], ALU.mult).then_inc(t1_d, 1)
                    if s == 3:
                        dve.wait_ge(unit_done, 4 * j + E0 + 4)
                        dve.wait_ge(ga_sig, j + 1)
                        dve.tensor_tensor(T2, SGA, PS[:, 6:8, :], ALU.mult).then_inc(t2_d, 1)
            peeled(dve, 4, branches)
            for k in range(KD):
                dve.wait_ge(mg_hi, k + 1)
                dve.tensor_tensor(UL[:, k, :], MG[:, k, :], UH[:, k, :].bitcast(F32), ALU.subtract).then_inc(mg_lo, 1)
            for n in range(F0, G0):
                split_lo(dve, 0, n // 2, n % 2)
                if n % 2:
                    h = (n - F0) // 2
                    for c in range(NC):
                        if c < 3:
                            dve.wait_ge(wo_chunk, 3 * h + c + 1)
                        else:
                            dve.wait_ge(unit_done, n + 1)
                        xs = X[:, c, HALF * h:HALF * h + HALF]
                        dve.tensor_tensor(xs, xs, PS[:, 4 * h + c, :], ALU.add).then_inc(wo_add, 1)
            dve.wait_ge(ca_sig, 1)
            dve.tensor_tensor(CA[:, :], CA[:, :], COLS[:, 24:32], ALU.mult).then_inc(ca_d, 1)
            norm_dve(dve, 1, 16)
            dve.wait_ge(ca_d, 1)

            def mlp(gi):
                for s in range(8):
                    split_lo(dve, G0, 4 * gi + s // 2, s % 2)
                    if s < 4:
                        dve.wait_ge(relu_d, 4 * gi + s + 1)
                        if s >= 2 or not first(gi):
                            dve.wait_ge(hid_lo, 4 * gi + s - 1)
                        dve.scalar_tensor_tensor(SQ[:, s % 2, :, :], PS[:, 2 * (s % 2):2 * (s % 2) + 2, :], 0.0, RL[:, s % 2, :, :],
                                                 ALU.max, ALU.mult).then_inc(sq_d, 1)
                    if s < 6:
                        dve.wait_ge(ada_in[s % 2], 48 * gi + 16 * (s // 2 + 1))
                        if first(gi) and s < 3:
                            dve.wait_ge(b_in, 16)
                        else:
                            dve.wait_ge(ada_d, 6 * gi + s - 2)
                        part = ACC[:, UNIT * (s % 3):UNIT * (s % 3) + UNIT]
                        dve.scalar_tensor_tensor(part, ADA[:, s % 2, :], CA[:, bass.ds(2 * gi + s // 3, 1)], part,
                                                 ALU.mult, ALU.add).then_inc(ada_d, 1)
                    if s in (5, 7):
                        h = (s - 5) // 2
                        for c in range(NC):
                            if c < 3:
                                dve.wait_ge(mo_chunk, 6 * gi + 3 * h + c + 1)
                            else:
                                dve.wait_ge(unit_done, 8 * gi + G0 + s + 1)
                            xs = X[:, c, HALF * h:HALF * h + HALF]
                            dve.tensor_tensor(xs, xs, PS[:, 4 * (1 - h) + c, :], ALU.add).then_inc(mo_add, 1)
            peeled(dve, 4, mlp)

            link(dve.tensor_tensor(LBS[:, 0:3], COLS[:, 32:35], COLS[:, 32:35], ALU.subtract))
            dve.tensor_copy(LBS[:, 6:9], LBS[:, 0:3]).then_inc(lb_sub, 1)
            dve.wait_ge(mod_mm, 1)
            link.inc(dve.tensor_copy(MODC[:, 0:8], PS[:, 0, 0:8]))
            link(dve.scalar_tensor_tensor(MODC[:, 8:16], PS[:, 0, 8:16], 1.0, COLS[:, 43:51], ALU.add, ALU.mult))
            for r in range(8):
                dve.wait_ge(mrow_mm, r + 1)
                dve.tensor_copy(MROW[:, 512 * r:512 * r + 512], PS[0:1, 1 + r % 3, :]).then_inc(mrow_d, 1)
            dve.wait_ge(late_in, 16)
            dve.wait_ge(br_rs, 2)
            for c in range(NC):
                dve.scalar_tensor_tensor(X[:, c, :], X[:, c, :], SS[:, 4 + c:5 + c], NFB, ALU.mult, ALU.mult).then_inc(x2_d, 1)
            norm_dve(dve, 2)
            dve.wait_ge(lb_exp, 1)
            link(dve.reciprocal(LBS[:, 6:9], LBS[:, 3:6]))
            link(dve.tensor_tensor(LBS[:, 3:6], LBS[:, 3:6], LBS[:, 6:9], ALU.mult))
            link(dve.tensor_tensor(LBS[:, 0:3], LBS[:, 3:6], LBS[:, 3:6], ALU.subtract))
            dve.tensor_scalar(LBS[:, 9:12], LBS[:, 0:3], -1.0, 1.0, ALU.mult, ALU.add).then_inc(lb_d, 1)
            dve.wait_ge(pos_in, 32)
            link(dve.tensor_copy(TRG[:, 1, :], TRG[:, 0, :].bitcast(I32)))
            link(dve.tensor_scalar(TRG[:, 1, :], TRG[:, 1, :], COLS[:, 52:53], None, ALU.mult))
            for k, quarter in ((2, 0.0), (3, 0.25)):
                if k == 2:
                    dve.wait_ge(x2_d, 4)
                link(dve.tensor_scalar(TRG[:, 0, :].bitcast(I32), TRG[:, 1, :], 1.0 / TWO_PI, quarter, ALU.mult, ALU.add))
                link(dve.tensor_copy(RT, TRG[:, 0, :].bitcast(I32)))
                link(dve.scalar_tensor_tensor(TRG[:, k, :], RT, -TURN[0], TRG[:, 1, :], ALU.mult, ALU.add))
                link(dve.scalar_tensor_tensor(TRG[:, k, :], RT, -TURN[1], TRG[:, k, :], ALU.mult, ALU.add))
                link(dve.scalar_tensor_tensor(TRG[:, k, :], RT, -TURN[2], TRG[:, k, :], ALU.mult, ALU.add))
                if quarter:
                    link(dve.tensor_scalar(TRG[:, k, :], TRG[:, k, :], TWO_PI / 4, None, ALU.add))
                dve.tensor_scalar(TRG[:, k, :], TRG[:, k, :], PI_IN, -PI_IN, ALU.min, ALU.max).then_inc(trig_r, 1)
            for n in range(H0, J0 + 3):
                split_lo(dve, 0, n // 2, n % 2)
                if I0 <= n < J0:
                    dve.wait_ge(gsig, n - I0 + 1)
                    if n == I0:
                        dve.wait_ge(mrow_out, 16)
                    for m in range(2):
                        tile = 2 * (n - I0) + m
                        ins = dve.scalar_tensor_tensor(G2[:, tile, :], PS[:, 2 * (n % 2) + m, :], COLS[:, 35 + tile:36 + tile],
                                                       SG[:, n % 2, m, :], ALU.mult, ALU.mult)
                        if m:
                            ins.then_inc(g2_out, 1)
                        else:
                            link.inc(ins)
            for n in range(J0 + 3, J0 + 6):
                j = n - J0 - 3
                split_lo(dve, 0, n // 2, n % 2)
                for a in (2 * j, 2 * j + 1):
                    dve.wait_ge(perm_mm, a + 1)
                    if a:
                        dve.wait_ge(rope_d, a)
                    dve.tensor_tensor(RT, PS[:, 4 + a % 4, :], SINS, ALU.mult).then_inc(rope_s, 1)
                dve.wait_ge(hsig, 2 * j + 1)
                dve.scalar_tensor_tensor(HQ[:, j, :], PS[:, 2 * (n % 2), :], 0.125, SG[:, n % 2, 0, :], ALU.mult, ALU.mult).then_inc(hq_d, 1)
            split_lo(dve, 0, (J0 + 6) // 2, 0)
            split_lo(dve, 0, (J0 + 7) // 2, 1)
            dve.wait_ge(ga_l, 3)
            dve.scalar_tensor_tensor(TRG[:, 2, :], TRG[:, 0, :], 0.0, TRG[:, 1, :], ALU.min, ALU.subtract).then_inc(ga_m, 1)

            def head_norm(tile):
                dve.wait_ge(hn_rt, tile + 1)
                dve.reciprocal(SQT, SQT).then_inc(hn_d, 1)
                dve.wait_ge(hn_d, 3 * tile + 1)
                dve.tensor_tensor(SQT, SQT, PS[:, 6, :], ALU.mult).then_inc(hn_d, 1)
                dve.wait_ge(hn_d, 3 * tile + 2)
                dve.tensor_tensor(G2[:, tile, :], G2[:, tile, :], SQT, ALU.mult).then_inc(hn_d, 1)
            dve.wait_ge(ga_d, 1)
            for h in range(6):
                b = 3 * (h % 2)
                dve.wait_ge(ret_s, h + 1)
                dve.wait_ge(d_in, 16 * (h + 1))
                if h >= 2:
                    dve.wait_ge(ret_o, h - 1)
                A = AB[:, h % 2, :]
                link.inc(dve.tensor_tensor(A[:, 0:512].rearrange("p (c s) -> p c s", c=4), PS[:, b, :].rearrange("p (c s) -> p c s", c=4),
                                           DT[:, 0:P].unsqueeze(1).broadcast_to([P, 4, P]), ALU.mult))
                link.inc(dve.tensor_tensor(A[:, 512:896], PS[:, b + 1, 0:384], DT[:, P:512], ALU.mult))
                link.inc(dve.tensor_tensor(A[:, 1152:1280], PS[:, b + 1, 384:512], DT[:, P:256], ALU.mult))
                link.wait()
                dve.tensor_tensor(A[:, 896:1152], PS[:, b + 2, 0:256], DT[:, P:384], ALU.mult).then_inc(ret_a, 1)
                if h % 2:
                    head_norm(h // 2)
            dve.wait_ge(ret_o, 6)
            dve.memset(AB[:, :, 0:512], 0.0).then_inc(a_zero, 1)
            dve.wait_ge(a_zero, 1)
            dve.wait_ge(mask_in, 16)
            for p in range(5):
                for lev in range(-1, 7):
                    for hh in range(2):
                        cnt = 20 * p + 2 * (lev + 1) + hh
                        dve.wait_ge(lvl_s, cnt + 1)
                        if p and lev == -1:
                            dve.wait_ge(pass_o, p)
                        dve.copy_predicated(AB[:, hh, 0:512].rearrange("p (c s) -> p c s", c=4),
                                            MASK[:, lev + 1, :].unsqueeze(1).broadcast_to([P, 4, P]),
                                            PS[:, cnt % 6, :].rearrange("p (c s) -> p c s", c=4)).then_inc(lvl_a, 1)
                        dve.wait_ge(lvl_a, 16 * p + 2 * (lev + 1) + hh + 1)
                    if p and lev == 0:
                        head_norm(2 + p)
            head_norm(7)
            for n in range(K0, M0):
                if n < M0 - 1:
                    split_lo(dve, 0, n // 2, n % 2)
                if n % 2:
                    h = (n - K0) // 2
                    dve.wait_ge(gm_in, 16)
                    for c in range(NC):
                        if c < 3:
                            dve.wait_ge(wo2_chunk, 3 * h + c + 1)
                        else:
                            dve.wait_ge(unit_done, n + 1)
                        x = 4 * h + c
                        if x >= 2:
                            dve.wait_ge(wo2_add, x - 1)
                        dve.tensor_tensor(TMPK[:, x % 2, :], PS[:, 4 * h + c, :], GMB[:, HALF * h:HALF * h + HALF], ALU.mult).then_inc(wo2_t, 1)
            dve.wait_ge(moe_in, 144)
            link(dve.scalar_tensor_tensor(ROW_A, ROW_A, 1.0, ROW_N, ALU.add, ALU.mult))
            for c in range(NC):
                dve.wait_ge(norm_xn, NC * 3 + c + 1)
                dve.tensor_tensor(XN[:, c, :], XN[:, c, :], ROW_A, ALU.mult).then_inc(h2_m, 1)
            link.inc(dve.memset(GPAD, NEG))
            for k in range(KD):
                dve.wait_ge(norm_hi, KD * 3 + k + 1)
                dve.tensor_tensor(UL[:, k, :], PS[:, 4 + k % 4, :], UH[:, k, :].bitcast(F32), ALU.subtract).then_inc(norm_lo, 1)
            dve.wait_ge(lg_mm, 1)
            link(dve.tensor_tensor(LG, PS[:, 0, 0:256].rearrange("p (c n) -> p c n", c=4)[:, :, 0:N_LOG],
                                   B_LOG.unsqueeze(1).broadcast_to([P, NC, N_LOG]), ALU.add))
            link(dve.tensor_copy(GPAD[:, :, 0:4], LG[:, :, 0:4]))
            for c in range(NC):
                link.inc(dve.max(GTOP[:, c, :], GPAD[:, c, :]))
            link.wait()
            for c in range(NC):
                link.inc(dve.max_index(GTI[:, c, :], GTOP[:, c, :], GPAD[:, c, :]))
            dve.tensor_tensor(RS[:, 0:4, :].rearrange("p g c -> p c g"), LG[:, :, 0:4], GTOP[:, :, 0:1].broadcast_to([P, NC, 4]), ALU.subtract).then_inc(rt_arg, 1)
            link.wait()
            link(dve.tensor_copy(RS[:, 10, :], GTI[:, :, 0]))
            link(dve.tensor_tensor(OHG, IOTA[:, 0:4].unsqueeze(1).broadcast_to([P, NC, 4]), RS[:, 10, :].unsqueeze(2).broadcast_to([P, NC, 4]), ALU.is_equal))
            link(dve.tensor_tensor(EIG, LG[:, :, 4:N_LOG].rearrange("p c (g e) -> p c g e", g=4), OHG.unsqueeze(3).broadcast_to([P, NC, 4, 8]), ALU.mult))
            link(dve.tensor_reduce(ELOG, EIG.rearrange("p c g e -> p c e g"), AX.X, ALU.add))
            for c in range(NC):
                link.inc(dve.max(ETOP[:, c, :], ELOG[:, c, :]))
            link.wait()
            for c in range(NC):
                link.inc(dve.max_index(ETI[:, c, :], ETOP[:, c, :], ELOG[:, c, :]))
            dve.tensor_tensor(RS[:, 8, :], ETOP[:, :, 1], ETOP[:, :, 0], ALU.subtract).then_inc(rt_arg, 1)
            link.wait()
            for k in range(2):
                link(dve.tensor_copy(RS[:, 11 + k, :], ETI[:, :, k]))
                link(dve.scalar_tensor_tensor(RS[:, 11 + k, :], RS[:, 10, :], 8.0, RS[:, 11 + k, :], ALU.mult, ALU.add))
                link(dve.tensor_tensor(OH[:, k, :, :], IOTA[:, 0:N_EXP].unsqueeze(1).broadcast_to([P, NC, N_EXP]), RS[:, 11 + k, :].unsqueeze(2).broadcast_to([P, NC, N_EXP]), ALU.is_equal))
            dve.tensor_tensor(OHS, OH[:, 0, :, :], OH[:, 1, :, :], ALU.add).then_inc(oh_d, 1)
            dve.wait_ge(rt_exp, 1)
            link(dve.tensor_reduce(RS[:, 13, :], RS[:, 4:8, :].rearrange("p g c -> p c g"), AX.X, ALU.add))
            dve.wait_ge(rt_exp, 2)
            link(dve.tensor_scalar(RS[:, 10, :], RS[:, 9, :], 1.0, None, ALU.add))
            link(dve.tensor_tensor(RS[:, 13, :], RS[:, 13, :], RS[:, 10, :], ALU.mult))
            link(dve.reciprocal(RS[:, 14, :], RS[:, 13, :]))
            link(dve.tensor_tensor(RS[:, 15, :], RS[:, 14, :], RS[:, 9, :], ALU.mult))
            dve.wait_ge(pos_mm, 1)
            link(dve.tensor_tensor(NBC, PS[:, 1, 0:N_EXP].unsqueeze(2).broadcast_to([P, N_EXP, 8]), T64[:, 0:8].unsqueeze(1).broadcast_to([P, N_EXP, 8]), ALU.is_gt))
            link.inc(dve.memset(ENDA[:, 0:32], 0.0))
            link.inc(dve.memset(ENDB[:, 0:32], 0.0))
            link(dve.tensor_reduce(NB, NBC, AX.X, ALU.add))
            link(dve.tensor_copy(ENDA[:, 32:64], NB))
            a, b = ENDA, ENDB
            for shift in (1, 2, 4, 8, 16):
                link(dve.tensor_tensor(b[:, 32:64], a[:, 32:64], a[:, 32 - shift:64 - shift], ALU.add))
                a, b = b, a
            END = a[:, 32:64]
            link(dve.tensor_tensor(ECMP, END[0:1, :].unsqueeze(1).broadcast_to([1, 52, N_EXP]), IOTA[0:1, 0:52].unsqueeze(2).broadcast_to([1, 52, N_EXP]), ALU.is_le))
            link(dve.tensor_reduce(EB, ECMP, AX.X, ALU.add))
            link(dve.tensor_scalar(EBI, EB, float(N_EXP - 1), None, ALU.min))
            link(dve.tensor_scalar(NR[:, 31:32], END[0:1, 31:32], 0.5, None, ALU.mult))
            link(dve.tensor_tensor(NR[:, 0:28], IOTA[0:1, 0:28], NR[:, 31:32].broadcast_to([1, 28]), ALU.is_lt))
            link(dve.tensor_reduce(NR[:, 30:31], NR[:, 0:28], AX.X, ALU.add))
            dve.tensor_scalar(NRI, NR[:, 30:31], -2.0, None, ALU.add).then_inc(route_d, 1)
            link(dve.tensor_tensor(b[:, 32:64], END, NB, ALU.subtract))
            link(dve.scalar_tensor_tensor(POSX, b[:, 32:64].unsqueeze(1).broadcast_to([P, NC, N_EXP]), float(BLOCK),
                                          PS[:, 2, 0:128].rearrange("p (c e) -> p c e", c=NC), ALU.mult, ALU.add))
            for k in range(2):
                link.inc(dve.tensor_tensor(SLX[:, 4 * k:4 * k + 4, :], OH[:, k, :, :], POSX, ALU.mult))
            link.wait()
            link(dve.tensor_reduce(SLOT, SLX, AX.X, ALU.add))
            link.inc(dve.tensor_copy(SLOTI, SLOT))
            link(dve.tensor_tensor(GE, SLOT.unsqueeze(2).broadcast_to([P, 8, 52]), T64[:, 0:52].unsqueeze(1).broadcast_to([P, 8, 52]), ALU.is_ge))
            link(dve.tensor_reduce(BP, GE, AX.X, ALU.add))
            link(dve.tensor_scalar(BP, BP, -1.0, None, ALU.add))
            link(dve.scalar_tensor_tensor(SLOT, BP, -float(BLOCK), SLOT, ALU.mult, ALU.add))
            link.inc(dve.tensor_tensor(JHOT, IOTA.unsqueeze(1).broadcast_to([P, 8, BLOCK]), SLOT.unsqueeze(2).broadcast_to([P, 8, BLOCK]), ALU.is_equal))
            link(dve.tensor_tensor(BHOT, IOTA[:, 0:52].unsqueeze(1).broadcast_to([P, 8, 52]), BP.unsqueeze(2).broadcast_to([P, 8, 52]), ALU.is_equal))
            for k in range(2):
                dve.tensor_tensor(BHOT[:, 4 * k:4 * k + 4, :], BHOT[:, 4 * k:4 * k + 4, :], TOK.unsqueeze(2).broadcast_to([P, NC, 52]), ALU.mult).then_inc(jb_d, 1)
            dve.wait_ge(idx_mm, 1)
            dve.tensor_copy(IDXT, PS[0:BLOCK, 3, 0:52]).then_inc(idx_d, 1)
            dve.wait_ge(route_d, 1)
            n2 = dve.value_load(NRI, min_val=0, max_val=MAX_BLOCKS // 2 - 2) + 2

            def x_lo(b):
                dve.wait_ge(xt_hi, b + 1)
                dve.tensor_tensor(ATL[:, 0, :], PS[:, 2, :], ATH[:, 0, :].bitcast(F32), ALU.subtract).then_inc(xt_lo, 1)

            def w_lo(i, x, part):
                dve.wait_ge(hi_ready, 3 * (2 * i + x) + M0 + part + 1)
                dve.tensor_tensor(ELO[x][part], EXRAW[x][:, UNIT * part:UNIT * part + UNIT], EHI[x][part].bitcast(F32), ALU.subtract).then_inc(lo_ready, 1)

            def hidden(b, x):
                dve.wait_ge(m_sig, b + 1)
                dve.tensor_tensor(SGM, SGM, PS[0:BLOCK, x, 0:256], ALU.mult).then_inc(m_silu, 1)
                dve.wait_ge(m_silu, b + 1)
                dve.tensor_tensor(HR, SGM, PS[0:BLOCK, x, 256:512], ALU.mult).then_inc(m_hid, 1)
                x_lo(b + 1)
                dve.wait_ge(m_hi, b + 1)
                dve.tensor_tensor(HTL, PS[:, 3, 0:2 * BLOCK].rearrange("p (k s) -> p k s", k=2), HTH.bitcast(F32), ALU.subtract).then_inc(m_lo, 1)

            def step(i, x):
                w_lo(i, x, 0)
                w_lo(i, x, 1)
                if not (first(i) and x == 0):
                    hidden(2 * i + x - 1, 1 - x)
                w_lo(i, x, 2)
            x_lo(0)
            for x in range(2):
                step(0, x)
            with dve.Fori(1, n2) as i:
                for x in range(2):
                    step(i, x)
            hidden(2 * n2 - 1, 1)
            for c in range(NC):
                dve.wait_ge(yc_in[c], 32)
                link(dve.tensor_scalar(YW[:, c, :], YC[:, c, 0, :], RS[:, 14, c:c + 1], None, ALU.mult))
                link(dve.scalar_tensor_tensor(YW[:, c, :], YC[:, c, 1, :], RS[:, 15, c:c + 1], YW[:, c, :], ALU.mult, ALU.add))
                link(dve.tensor_tensor(YW[:, c, :], YW[:, c, :], ROW_G, ALU.mult))
                dve.tensor_tensor(X[:, c, :], X[:, c, :], YW[:, c, :], ALU.add).then_inc(fin_x, 1)
            dve.wait_ge(norm_rs, 2 * 4 + 2)
            dve.wait_ge(fin_x, NC)
            for c in range(NC):
                dve.scalar_tensor_tensor(X[:, c, :], X[:, c, :], SS[:, 4 + c:5 + c], ROW_F, ALU.mult, ALU.mult).then_inc(fin_d, 1)
        @block.gpsimd
        def _(pool):
            link = Link(pool, pool_link)
            pool.wait_ge(const_in, 16 * NCONST)
            norm_pool(pool, 0)
            pool.wait_ge(z_out, NU_A)
            for g in range(4):
                src = PZ[:, 2 * g:2 * g + 2, :]
                cur = src
                for lev in range(g + 1):
                    d = 1 << lev
                    dst = PB[:, lev % 2, :, :]
                    link.inc(pool.tensor_copy(dst[:, :, 0:d], cur[:, :, 0:d]))
                    link(pool.tensor_tensor(dst[:, :, d:S], cur[:, :, d:S], cur[:, :, 0:S - d], ALU.add))
                    cur = dst
                w = 2 << g
                link(pool.tensor_tensor(cur[:, :, 0:16], cur[:, :, 0:16], PINV[:, g, :].unsqueeze(1).broadcast_to([PG, 2, 16]), ALU.mult))
                link(pool.tensor_scalar(cur, cur, 1.0 / w, None, ALU.mult))
                ins = pool.tensor_tensor(src, cur, src, ALU.subtract)
                if g == 3:
                    ins.then_inc(pooled, 1)
                else:
                    link(ins)
            for q in range(2):
                pool.wait_ge(att_c, 6)
                pool.wait_ge(eg_e, q + 1)
                pool.tensor_tensor(OT[:, q, :, :], OT[:, q, :, :], EG, ALU.mult).then_inc(wsum, 1)
                pool.wait_ge(wsum, 3 * q + 1)
                pool.tensor_tensor(OT[:, q, 0, :], OT[:, q, 0, :], OT[:, q, 1, :], ALU.add).then_inc(wsum, 1)
                pool.wait_ge(wsum, 3 * q + 2)
                pool.tensor_tensor(OT[:, q, 0, :], OT[:, q, 0, :], OT[:, q, 2, :], ALU.add).then_inc(wsum, 1)

            with pool.Fori(0, 4) as j:
                pool.wait_ge(t1_d, j + 1)
                pool.wait_ge(t2_d, j + 1)
                pool.tensor_tensor(MG[:, bass.ds(2 * j, 2), :], T1, T2, ALU.add).then_inc(mg_d, 1)
            pool.wait_ge(t1_d, 4)
            pool.wait_ge(at_lo, 2)
            pool.memset(ACC, 0.0).then_inc(acc_init, 1)
            pool.wait_ge(acc_init, 1)
            pool.dma_start(ACC[0:1, :], t["b_ada"]).then_inc(b_in, 16)
            norm_pool(pool, 1)
            with pool.Fori(0, 4) as gi:
                for s in range(4):
                    pool.wait_ge(hid_hi, 4 * gi + s + 1)
                    pool.tensor_tensor(VL[:, 2 * s:2 * s + 2, :], SQ[:, s % 2, :, :], VH[:, 2 * s:2 * s + 2, :].bitcast(F32),
                                       ALU.subtract).then_inc(hid_lo, 1)

            pool.wait_ge(br_sq, NC)
            pool.tensor_scalar(SS[:, 0:4], SS[:, 0:4], 1.0 / D, EPS, ALU.mult, ALU.add).then_inc(br_rs, 1)
            pool.wait_ge(br_rs, 1)
            pool.tensor_tensor(SS[:, 4:8], SS[:, 0:4], COLS[:, 60:64], ALU.pow).then_inc(br_rs, 1)
            norm_pool(pool, 2)
            pool.wait_ge(lb_d, 1)
            pool.wait_ge(trig_d, 2)
            for j in range(3):
                for a in (2 * j, 2 * j + 1):
                    pool.wait_ge(perm_mm, a + 1)
                    pool.tensor_tensor(RQK[:, a, :], RQK[:, a, :], COS, ALU.mult).then_inc(rope_c, 1)
                    pool.wait_ge(rope_c, a + 1)
                    pool.wait_ge(rope_s, a + 1)
                    pool.tensor_tensor(RQK[:, a, :], RQK[:, a, :], RT, ALU.add).then_inc(rope_d, 1)
                pool.wait_ge(hsig, 2 * j + 2)
                n = J0 + 3 + j
                pool.tensor_scalar(HF[:, j, :], SG[:, n % 2, 1, :], LBS[:, 9 + j:10 + j], LBS[:, j:j + 1], ALU.mult, ALU.add).then_inc(hf_d, 1)
                pool.wait_ge(hf_d, 3 * j + 1)
                pool.tensor_scalar(HF[:, j, :], HF[:, j, :], 1e-30, None, ALU.max).then_inc(hf_d, 1)
                pool.tensor_scalar(HK[:, j, :], HK[:, j, :], LBS[:, 9 + j:10 + j], None, ALU.mult).then_inc(hf_d, 1)
            pool.wait_ge(hf_d, 9)
            pool.wait_ge(hq_d, 3)
            pool.wait_ge(ga_d, 1)
            pool.wait_ge(z2_out, 10)
            pool.wait_ge(ret_o, 6)

            def head_lo(tile):
                pool.wait_ge(hn_hi, tile + 1)
                pool.tensor_tensor(VL[:, tile, :], G2[:, tile, :], VH[:, tile, :].bitcast(F32), ALU.subtract).then_inc(hn_lo, 1)
            for tile in range(3):
                head_lo(tile)
            for p in range(5):
                q_, k_, f_ = (HQ[:, p, :], HK[:, p, :], HF[:, p, :]) if p < 3 else (GQ, GK, GF)
                link.inc(pool.tensor_copy(PP, f_))
                link(pool.memset(UB, 1.0))
                for lev in range(9):
                    m = 1 << lev
                    v = lambda x: x.rearrange("p (n two m) -> p n two m", two=2, m=m)
                    if 9 * p + lev >= 2:
                        pool.wait_ge(lvl_s, 20 * ((9 * p + lev - 2) // 9) + 2 * ((9 * p + lev - 2) % 9) + 4)
                    qk = v(QKL[:, lev % 2, :]) if (9 * p + lev) % 2 == lev % 2 else v(QKL[:, (9 * p + lev) % 2, :])
                    link.inc(pool.tensor_tensor(qk[:, :, 0, :], v(k_)[:, :, 0, :], v(UB)[:, :, 0, :], ALU.mult))
                    pool.tensor_tensor(qk[:, :, 1, :], v(q_)[:, :, 1, :], v(PP)[:, :, 1, :], ALU.mult).then_inc(lvl_qk, 1)
                    if lev < 8:
                        sh = [P, S // (2 * m), m]
                        link.wait()
                        pool.wait_ge(lvl_qk, 9 * p + lev + 1)
                        link(pool.tensor_tensor(v(UB)[:, :, 0, :], v(UB)[:, :, 0, :], v(PP)[:, :, 1, m - 1:m].broadcast_to(sh), ALU.mult))
                        link(pool.tensor_tensor(v(PP)[:, :, 1, :], v(PP)[:, :, 1, :], v(PP)[:, :, 0, m - 1:m].broadcast_to(sh), ALU.mult))
                    else:
                        link.wait()
                        pool.wait_ge(lvl_qk, 9 * p + lev + 1)
                    if p and lev == 3:
                        head_lo(2 + p)
            head_lo(7)
            for x in range(8):
                h, c = x // 4, x % 4
                pool.wait_ge(wo2_t, x + 1)
                xs = X[:, c, HALF * h:HALF * h + HALF]
                pool.tensor_tensor(xs, xs, TMPK[:, x % 2, :], ALU.add).then_inc(wo2_add, 1)

            def rstd(j):
                pool.wait_ge(norm_sq, NC * j + NC)
                pool.tensor_scalar(SS[:, 0:4], SS[:, 0:4], 1.0 / D, EPS, ALU.mult, ALU.add).then_inc(norm_rs, 1)
                pool.wait_ge(norm_rs, 2 * j + 1)
                pool.tensor_tensor(SS[:, 4:8], SS[:, 0:4], COLS[:, 60:64], ALU.pow).then_inc(norm_rs, 1)
            rstd(3)
            pool.wait_ge(wr_hi, 1)
            pool.tensor_tensor(ATL[:, 0, 0:KD * N_LOG], WR, ATH[:, 0, 0:KD * N_LOG].bitcast(F32), ALU.subtract).then_inc(wr_lo, 1)
            for c in range(NC):
                pool.wait_ge(h2_m, c + 1)
                pool.tensor_tensor(XN[:, c, :], XN[:, c, :], ROW_B, ALU.add).then_inc(h2_d, 1)
            pool.wait_ge(hd_out, 16 * NC)
            pool.wait_ge(idx_d, 1)
            pool.wait_ge(route_d, 1)
            n2 = pool.value_load(NRI, min_val=0, max_val=MAX_BLOCKS // 2 - 2) + 2

            def gather(b, x, guard):
                if guard is not None:
                    pool.wait_ge(xt_tr, b - 1)
                    pool.wait_ge(xg_in[x], guard)
                pool.tensor_copy(IDXC[:, x:x + 1], IDXT[:, bass.ds(b, 1)])
                pool.drain()
                pool.indirect_dma_start(XG[:, x, :], None, t["h2"], bass.IndirectOffsetOnAxis(ap=IDXC[:, x:x + 1], axis=0)).then_inc(xg_in[x], 16)
            gather(0, 0, None)
            gather(1, 1, None)
            with pool.Fori(1, n2) as i:
                gather(2 * i, 0, 16 * i)
                gather(2 * i + 1, 1, 16 * i)
            gather(2 * n2, 0, 16 * n2)
            pool.wait_ge(idx_d, 1)
            pool.wait_ge(y_out[0], 16 * n2)
            pool.wait_ge(y_out[1], 16 * n2)
            for c in range(NC):
                for k in range(2):
                    pool.indirect_dma_start(YC[:, c, k, :], None, t["y"], bass.IndirectOffsetOnAxis(ap=SLOTI[:, 4 * k + c:4 * k + c + 1], axis=0)).then_inc(yc_in[c], 16)
            rstd(4)

        @block.tensor
        def _(pe):
            pe.wait_ge(const_in, 16 * NCONST)
            norm_pe(pe, 0)
            pe.wait_ge(norm_lo, KD)
            for n in range(A0, B0):
                unit_is_in(pe, n)
                if n >= 2:
                    pe.wait_ge(z_out, n - 1)
                for m in range(2):
                    last = feature(pe, n % 2, m, PG, 2 * PG, U, 2 * (n % 2) + m)
                last.then_inc(unit_done, 1)
            with pe.Fori(0, NU_B // 2) as i:
                for s in range(2):
                    unit_is_in(pe, 2 * i + B0 + s)
                    pe.wait_ge(z_out, 2 * i + B0 + s - 1)
                    for m in range(2):
                        last = feature(pe, s, m, P, 256, U, 2 * s + m)
                    last.then_inc(unit_done, 1)
            for n in range(C0, D0):
                unit_is_in(pe, n)
                pe.wait_ge(z_out, n - 1)
                for c in range(NC):
                    for k in range(KD):
                        tok = slice(P * c, P * c + P) if n == C0 else slice(c, S, 4)
                        last = three(pe, PS[:, 2 * (n % 2) + c // 2, 256 * (c % 2):256 * (c % 2) + 256], (UH[:, k, tok], UL[:, k, tok]),
                                     wpair(n % 2, 256 * k, 256), k == 0, k == KD - 1)
                last.then_inc(unit_done, 1)
            unit_is_in(pe, D0)
            pe.wait_ge(pool_lo, 1)
            pe.wait_ge(z_out, D0)
            for g in range(4):
                for m in range(2):
                    for k in range(2):
                        last = three(pe, PS[0:PG, 2 * g + m, :], wpair(D0 % 2, 192 * (2 * g + k) + PG * m, PG, PG),
                                     (VH[0:PG, 2 * g + k, :], VL[0:PG, 2 * g + k, :]), k == 0, k == 1)
            last.then_inc(unit_done, 1)

            def transposes(n):
                w = len(blks(heads[n][0]))
                pe.wait_ge(att_e, 4 * (n + 1))
                if n:
                    pe.wait_ge(att_p, n)
                for x, (c, b) in enumerate(blks(heads[n][0])):
                    last = pe.transpose(PS[:, 4 + x // 4, P * (x % 4):P * (x % 4) + P], SBUFS[:, n % 2, c, P * b:P * b + P], IDN[:, :])
                last.then_inc(att_t, 1)

            def av(n):
                g, q, hh = heads[n]
                r0 = 64 * hh
                hd = 4 * g + 2 * q + hh
                pe.wait_ge(att_p, n + 1)
                if n >= 4:
                    pe.wait_ge(att_c, n // 2 - 1)
                for x, (c, b) in enumerate(blks(g)):
                    kc = c - 1 + b if g == 0 else c
                    last = pe.matmul(PS[r0:r0 + 64, 6 + (n // 2) % 2, P * c:P * c + P], VT[:, kc, 64 * hd:64 * hd + 64], PTB[:, n % 2, x, :],
                                     start=(b == 0 or c == 0), stop=(b == 1 or g > 0))
                last.then_inc(att_o, 1)

            pe.wait_ge(mix_out, 8)
            for n, (g, q, hh) in enumerate(heads):
                r = slice(64 * hh, 64 * hh + 64)
                b = 2 * (n % 2)
                if n >= 2:
                    pe.wait_ge(att_m, n - 1)
                qt, kt = QK[r, 2 * g + q, :], QK[r, 6 + 2 * g + q, :]
                for c in range(NC):
                    if g == 0:
                        o, k0, kn = (P, 0, P) if c == 0 else (0, P * (c - 1), 2 * P)
                        out = PS[:, b + c // 2, 256 * (c % 2) + o:256 * (c % 2) + o + kn]
                        last = pe.matmul(out, qt[:, P * c:P * c + P], kt[:, k0:k0 + kn], start=True, stop=True)
                    else:
                        last = pe.matmul(PS[:, b, P * c:P * c + P], qt[:, c::4], kt[:, c::4], start=True, stop=True)
                last.then_inc(att_s, 1)
                if n >= 1:
                    transposes(n - 1)
                if n >= 2:
                    av(n - 2)
            transposes(11)
            av(10)
            pe.wait_ge(att_m, 12)
            for c in range(NC):
                last = pe.transpose(PS[0:48, 0, P * c:P * c + P], ST[:, c, :], IDN[:, :])
            last.then_inc(st_tr, 1)
            av(11)
            pe.wait_ge(st_row, 2)

            def stat_rows(bank, q, col):
                for g in range(3):
                    for hh in range(2):
                        r = st_col(g, q, hh) + col
                        last = pe.matmul(PS[64 * hh:64 * hh + 64, bank + g, :], IDN[0:48, r:r + 1].broadcast_to([48, 64]), RW,
                                         start=True, stop=True)
                return last
            for q in range(2):
                if q:
                    pe.wait_ge(eg_d, 3)
                stat_rows(1, q, 0).then_inc(nm_bc, 1)
                if q:
                    pe.wait_ge(den_d, 1)
                else:
                    pe.wait_ge(att_c, 6)
                stat_rows(4, q, 4).then_inc(l_bc, 1)
            pe.wait_ge(mixed_lo, 1)
            pe.wait_ge(at_lo, 2)

            def branches(j):
                for s, (src, rows, kc) in enumerate(((U, P, 8), (V, PG, 8), (U, P, 8), (AT, P, 2))):
                    unit_is_in(pe, 4 * j + E0 + s)
                    if not first(j):
                        pe.wait_ge((gp_sig, t1_d, ga_sig, t2_d)[s], j)
                    for m in range(2):
                        last = feature(pe, s % 2, m, P, 256, src, 2 * s + m, rows, kc)
                    last.then_inc(unit_done, 1)
            peeled(pe, 4, branches)
            pe.wait_ge(t2_d, 4)
            for n in range(F0, G0):
                h, kh = (n - F0) // 2, (n - F0) % 2
                unit_is_in(pe, n)
                pe.wait_ge(mg_lo, 4 * kh + 4)
                tokens(pe, n % 2, U, 4 * kh, 4 * h, wo_chunk, kh == 0, kh == 1)
            norm_pe(pe, 1)
            pe.wait_ge(norm_lo, KD + KD)

            def mlp(gi):
                for s in range(8):
                    unit_is_in(pe, 8 * gi + G0 + s)
                    if s < 4:
                        if s >= 2:
                            pe.wait_ge(sq_d, 4 * gi + s - 1)
                        elif not first(gi):
                            pe.wait_ge(mo_add, 8 * gi - 2 + 2 * s)
                        for m in range(2):
                            last = feature(pe, s % 2, m, P, 256, U, 2 * (s % 2) + m)
                        last.then_inc(unit_done, 1)
                    else:
                        h, kh = (s - 4) // 2, s % 2
                        pe.wait_ge(hid_lo, 4 * gi + 2 * kh + 2)
                        pe.wait_ge(sq_d, 4 * gi + 4) if h else None
                        tokens(pe, s % 2, V, 4 * kh, 4 * (1 - h), mo_chunk, kh == 0, kh == 1)
            peeled(pe, 4, mlp)

            pe.wait_ge(ada_d, 24)
            pe.wait_ge(mo_add, 32)
            for k in range(16):
                last = pe.matmul(PS[:, 0, k:k + 1], ACC[:, P * k:P * k + P], COLS[:, 59:60], start=True, stop=True)
            last.then_inc(mod_mm, 1)
            for r, src in enumerate((2 * D, 2 * D + HALF, 3 * D, 3 * D + HALF, 4 * D, 4 * D + HALF, 5 * D, 5 * D + HALF)):
                if r >= 3:
                    pe.wait_ge(mrow_d, r - 2)
                pe.matmul(PS[0:1, 1 + r % 3, :], COLS[:, 59:60], ACC[:, src:src + HALF], start=True, stop=True).then_inc(mrow_mm, 1)
            norm_pe(pe, 2)
            pe.wait_ge(norm_lo, KD * 2 + KD)
            pe.wait_ge(mrow_d, 8)
            for n in range(H0, J0 + 6):
                unit_is_in(pe, n)
                if n < I0 + 2:
                    if n >= H0 + 2:
                        pe.wait_ge(z2_out, n - H0 - 1)
                elif n < J0 + 2:
                    pe.wait_ge(g2_out, n - I0 - 1)
                elif n < J0 + 5:
                    pe.wait_ge(z2_out, 4 + n - J0 - 1)
                if n >= J0 + 5:
                    pe.wait_ge(hq_d, n - J0 - 4)
                    pe.wait_ge(hsig, 2 * (n - J0 - 4))
                if n < I0:
                    for c in range(NC):
                        for k in range(KD):
                            tok = slice(P * c, P * c + P)
                            last = three(pe, PS[:, 2 * (n % 2) + c // 2, 256 * (c % 2):256 * (c % 2) + 256], (UH[:, k, tok], UL[:, k, tok]),
                                         wpair(n % 2, 256 * k, 256), k == 0, k == KD - 1)
                else:
                    for m in range(2):
                        last = feature(pe, n % 2, m, P, 256, U, 2 * (n % 2) + m)
                last.then_inc(unit_done, 1)
                if n == J0 + 3:
                    pe.wait_ge(z2_out, 7)
                    pe.wait_ge(pos_in, 32)
                    for a in range(6):
                        if a >= 4:
                            pe.wait_ge(rope_s, a - 3)
                        pe.matmul(PS[:, 4 + a % 4, :], PERM, RQK[:, a, :], start=True, stop=True).then_inc(perm_mm, 1)
            n = J0 + 6
            unit_is_in(pe, n)
            pe.wait_ge(hq_d, 2)
            pe.wait_ge(hsig, 4)
            for m in range(2):
                last = feature(pe, 0, m, P, 256, U, m)
            last.then_inc(unit_done, 1)
            n = J0 + 7
            unit_is_in(pe, n)
            pe.wait_ge(hq_d, 3)
            pe.wait_ge(hsig, 6)
            feature(pe, 1, 0, 16, 16, U, 2).then_inc(ga_mm, 1)
            pe.wait_ge(z2_out, 10)
            pe.matmul(PS[:, 3, :], WH[0:16, 1, P:2 * P].bitcast(F32), GA, start=True, stop=False)
            pe.matmul(PS[:, 3, :], WL[0:16, 1, P:2 * P].bitcast(F32), GA, start=False, stop=True).then_inc(unit_done, 1)

            def mean_square(tile):
                pe.wait_ge(hn_sq, tile + 1)
                pe.matmul(PS[:, 7, :], ONESB[:, :], SQT, start=True, stop=True).then_inc(hn_mm, 1)

            def weigh(hh, head, signal):
                A = AB[:, hh, :]
                off = {0: 512, 1: 896, 2: 1152}
                out = PS[64 * (head % 2):64 * (head % 2) + 64, 6, :]
                for cs in range(NC):
                    val = V2[:, cs, 64 * head:64 * head + 64]
                    if cs < 3:
                        n_off = P * (3 - cs)
                        if cs == 0:
                            pe.matmul(out[:, 0:P], val, A[:, 0:P], start=True, stop=False, skip_group_check=True)
                        else:
                            pe.matmul(out[:, P * cs:P * cs + P], val, A[:, P * cs:P * cs + P], start=False, stop=False, skip_group_check=True)
                        last = pe.matmul(out[:, P * (cs + 1):S], val, A[:, off[cs]:off[cs] + n_off], start=False, stop=False, skip_group_check=True)
                    else:
                        last = pe.matmul(out[:, P * cs:S], val, A[:, P * cs:P * cs + P], start=False, stop=True, skip_group_check=True)
                last.then_inc(signal, 1)

            pe.wait_ge(ga_x, 1)
            pe.wait_ge(rope_d, 6)
            for h in range(7):
                if h < 6:
                    b, r0 = 3 * (h % 2), 64 * (h % 2)
                    q_, k_ = RQK[r0:r0 + 64, h // 2, :], RQK[r0:r0 + 64, 3 + h // 2, :]
                    if h >= 2:
                        pe.wait_ge(ret_a, h - 1)
                    else:
                        pe.wait_ge(hq_d, 3)
                    for c in range(NC):
                        pe.matmul(PS[:, b, P * c:P * c + P], k_[:, P * c:P * c + P], q_[:, P * c:P * c + P], start=True, stop=True)
                    pe.matmul(PS[:, b + 1, 0:384], k_[:, 0:P], q_[:, P:S], start=True, stop=True)
                    pe.matmul(PS[:, b + 1, 384:512], k_[:, 2 * P:3 * P], q_[:, 3 * P:S], start=True, stop=True)
                    pe.matmul(PS[:, b + 2, 0:256], k_[:, P:2 * P], q_[:, 2 * P:S], start=True, stop=True).then_inc(ret_s, 1)
                if h >= 3 and h % 2:
                    mean_square(h // 2 - 1)
                if h:
                    pe.wait_ge(ret_a, h)
                    if h >= 3 and h % 2:
                        pe.wait_ge(hn_d, 3 * (h // 2 - 1) + 2)
                    weigh((h - 1) % 2, h - 1, ret_o)
            mean_square(2)

            pe.wait_ge(hf_d, 9)
            for p in range(5):
                q_, k_ = (HQ[:, p, :], HK[:, p, :]) if p < 3 else (GQ, GK)
                for lev in range(-1, 9):
                    for hh in range(2):
                        if p < 3:
                            r = slice(64 * hh, 64 * hh + 64)
                        else:
                            r = slice(64 * (p - 3) + 32 * hh, 64 * (p - 3) + 32 * hh + 32)
                        cnt = 20 * p + 2 * (lev + 1) + hh
                        bank = cnt % 6
                        if cnt >= 6:
                            before = cnt - 6
                            bp, bl, bh = before // 20, (before % 20) // 2 - 1, before % 2
                            if bl < 7:
                                pe.wait_ge(lvl_a, 16 * bp + 2 * (bl + 1) + bh + 1)
                            else:
                                pe.wait_ge(lvl_b, 8 * bp + 4 * (bl - 7) + 2 * bh + 2)
                        elif cnt == 0:
                            pe.wait_ge(ret_a, 6)
                        if lev < 0:
                            left, right = k_, q_
                        else:
                            if hh == 0:
                                pe.wait_ge(lvl_qk, 9 * p + lev + 1)
                            left = right = QKL[:, (9 * p + lev) % 2, :]
                        if lev < 7:
                            for c in range(NC):
                                last = pe.matmul(PS[:, bank, P * c:P * c + P], left[r, P * c:P * c + P], right[r, P * c:P * c + P], start=True, stop=True)
                        elif lev == 7:
                            pe.matmul(PS[:, bank, 0:P], left[r, 0:P], right[r, P:2 * P], start=True, stop=True)
                            last = pe.matmul(PS[:, bank, P:2 * P], left[r, 2 * P:3 * P], right[r, 3 * P:S], start=True, stop=True)
                        else:
                            pe.matmul(PS[:, bank, 0:256], left[r, 0:P], right[r, 256:S], start=True, stop=True)
                            last = pe.matmul(PS[:, bank, 256:512], left[r, P:2 * P], right[r, 256:S], start=True, stop=True)
                        last.then_inc(lvl_s, 1)
                pe.wait_ge(hn_d, 3 * (p + 2) + 2)
                pe.wait_ge(lvl_a, 16 * (p + 1))
                pe.wait_ge(lvl_b, 8 * (p + 1))
                head = 6 + 2 * p
                weigh(0, head, pass_h)
                weigh(1, head + 1, pass_o)
                mean_square(3 + p)

            for n in range(K0, M0):
                h, kh = (n - K0) // 2, (n - K0) % 2
                unit_is_in(pe, n)
                pe.wait_ge(hn_lo, 4 * kh + 4)
                if h:
                    pe.wait_ge(hn_d, 24)
                tokens(pe, n % 2, V, 4 * kh, 4 * h, wo2_chunk, kh == 0, kh == 1)
            pe.wait_ge(h2_d, NC)
            for k in range(KD):
                if k >= 4:
                    pe.wait_ge(norm_lo, KD * 3 + k - 3)
                for c in range(NC):
                    last = pe.transpose(PS[:, 4 + k % 4, c * P:(c + 1) * P], XN[:, c, k * P:(k + 1) * P], IDN[:, :])
                last.then_inc(norm_tr, 1)
            pe.wait_ge(norm_lo, KD * 3 + KD)
            pe.wait_ge(wr_lo, 1)
            for c in range(NC):
                for k in range(KD):
                    tok = slice(P * c, P * c + P)
                    w = slice(N_LOG * k, N_LOG * k + N_LOG)
                    last = three(pe, PS[:, 0, 64 * c:64 * c + N_LOG], (UH[:, k, tok], UL[:, k, tok]), (ATH[:, 0, w], ATL[:, 0, w]), k == 0, k == KD - 1)
            last.then_inc(lg_mm, 1)
            pe.wait_ge(oh_d, 1)
            for c in range(NC):
                last = pe.matmul(PS[:, 1, 0:N_EXP], ONES, OHS[:, c, :], start=c == 0, stop=c == NC - 1)
            for c in range(NC):
                for before in range(c + 1):
                    last = pe.matmul(PS[:, 2, N_EXP * c:N_EXP * c + N_EXP], ONES if before < c else TRI, OHS[:, before, :],
                                     start=before == 0, stop=before == c)
            last.then_inc(pos_mm, 1)
            pe.wait_ge(jb_d, 2)
            for x in range(8):
                last = pe.matmul(PS[0:BLOCK, 3, 0:52], JHOT[:, x, :], BHOT[:, x, :], start=x == 0, stop=x == 7)
            last.then_inc(idx_mm, 1)
            pe.wait_ge(idx_d, 1)
            pe.wait_ge(route_d, 1)
            n2 = pe.value_load(NRI, min_val=0, max_val=MAX_BLOCKS // 2 - 2) + 2

            def x_tr(i, b, x):
                pe.wait_ge(xg_in[x], 16 * i + 16)
                if not (isinstance(b, int) and b == 0):
                    pe.wait_ge(xt_lo, b)
                pe.matmul(PS[:, 2, 0:BLOCK], XG[:, x, 0:P], IDN[0:BLOCK, 0:BLOCK], start=True, stop=True)
                for k in range(1, KD):
                    last = pe.transpose(PS[:, 2, BLOCK * k:BLOCK * k + BLOCK], XG[:, x, P * k:P * k + P], IDN[0:BLOCK, 0:BLOCK])
                last.then_inc(xt_tr, 1)

            def down(b, x):
                pe.wait_ge(m_lo, b + 1)
                unit_is_in(pe, 3 * b + M0 + 2)
                if not (isinstance(b, int) and b < 2):
                    pe.wait_ge(y_cp, b - 1)
                hi, lo = EHI[x][2], ELO[x][2]
                for h in range(2):
                    for k in range(2):
                        w = slice(D * k + HALF * h, D * k + HALF * h + HALF)
                        last = three(pe, PS[0:BLOCK, 4 + 2 * x + h, :], (HTH[:, k, :], HTL[:, k, :]), (hi[:, w], lo[:, w]), k == 0, k == 1)
                last.then_inc(m_down, 1)

            def step(i, x):
                b = 2 * i + x
                pe.wait_ge(xt_lo, b + 1)
                if not first(i):
                    pe.wait_ge(m_hid, b - 1)
                for part in range(2):
                    unit_is_in(pe, 3 * b + M0 + part)
                    hi, lo = EHI[x][part], ELO[x][part]
                    for k in range(4):
                        w = slice(HALF * k, HALF * k + HALF)
                        last = three(pe, PS[0:BLOCK, x, :], (XTH[:, 4 * part + k, :], XTL[:, 4 * part + k, :]), (hi[:, w], lo[:, w]),
                                     part == 0 and k == 0, part == 1 and k == 3)
                    last.then_inc(unit_done, 1)
                x_tr(i + x, b + 1, 1 - x)
                if not (first(i) and x == 0):
                    down(b - 1, 1 - x)
                pe.wait_ge(m_hid, b + 1)
                pe.matmul(PS[:, 3, 0:BLOCK], HR[:, 0:P], IDN[0:BLOCK, 0:BLOCK], start=True, stop=True)
                last = pe.transpose(PS[:, 3, BLOCK:2 * BLOCK], HR[:, P:2 * P], IDN[0:BLOCK, 0:BLOCK])
                last.then_inc(ht_tr, 1)
            x_tr(0, 0, 0)
            for i in range(2):
                for x in range(2):
                    step(i, x)
            with pe.Fori(2, n2) as i:
                for x in range(2):
                    step(i, x)
            down(2 * n2 - 1, 1)


POOL_TAPS = 16
HEADS_GRP = 4
ATT_HEADS = 12
RET_HEADS = 6
HEAD_DIM = 64


def _rows(w, n0, n, kp=P):
    return w[:, n0:n0 + n].reshape(w.shape[0] // kp, kp, n).transpose(1, 0, 2)


def _unit(a):
    u = np.zeros((P, UNIT), np.float32)
    u[:a.shape[0], :a[0].size] = a.reshape(a.shape[0], -1)
    return u


def _columns(w, *spans):
    return np.concatenate([w[:, a:b] for a, b in spans], 1)


def _square(w, units, h_cols=HALF):
    for h in range(2):
        for kh in range(2):
            units.append(_unit(_rows(w[HALF * kh:HALF * kh + HALF], HALF * h, HALF)))


def _weight_units(t):
    u = []
    w = t["w_in"][0]
    for j in range(4):
        u.append(_unit(_rows(w, 2304 + 192 * j, 192)))
    for j in range(6):
        u.append(_unit(_rows(w, 256 * j, 256)))
    for j in range(3):
        u.append(_unit(_rows(w, 1536 + 256 * j, 256)))
    u.append(_unit(t["w_pool_grp"][0].reshape(4, 2, PG, 2 * PG).transpose(2, 0, 1, 3)))
    for j in range(4):
        u.append(_unit(_rows(w, 4096 + 256 * j, 256)))
        u.append(_unit(_rows(t["w_pool_out"][0], 256 * j, 256, PG)))
        u.append(_unit(_rows(w, 3072 + 256 * j, 256)))
        u.append(_unit(_rows(t["w_att_out"][0], 256 * j, 256)))
    _square(t["w_out"][0], u)
    for g in range(4):
        for s in range(4):
            u.append(_unit(_rows(t["w_mlp_in"][0], D * g + 256 * s, 256)))
        _square(t["w_mlp_out"][0][D * g:D * g + D], u)
    w = t["w_in_2"][0]
    values = _columns(w, (768, 1152), (2304, 2688), (3328, 3584))
    gates = _columns(w, (1152, 1536), (2688, 3072), (3584, 3840))
    for part in (values, gates):
        for j in range(4):
            u.append(_unit(_rows(part, 256 * j, 256)))
    for j in range(3):
        u.append(_unit(_rows(w, 256 * j, 256)))
    for j in range(3):
        u.append(_unit(_rows(_columns(w, (1536 + P * j, 1664 + P * j), (1920 + P * j, 2048 + P * j)), 0, 256)))
    u.append(_unit(_rows(w, 3072, 256)))
    ga = _unit(_rows(w, 3840, 16))
    ga[:16, P:2 * P] = t["gla_wa2_2"][0]
    u.append(ga)
    _square(t["w_out_2"][0], u)
    return np.stack(u)


def _expert_units(t):
    rows = []
    for e in range(N_EXP):
        gate_up = np.concatenate([t["expert_w_gate_2"][0, e], t["expert_w_up_2"][0, e]], 1)
        rows.append(np.concatenate([_unit(_rows(gate_up[:HALF], 0, HALF)), _unit(_rows(gate_up[HALF:], 0, HALF)),
                                    _unit(_rows(t["expert_w_down_2"][0, e], 0, D))], 1))
    return np.stack(rows)


def _cols(t):
    f = np.float32
    c = np.zeros((P, 64), f)
    c[:, 0:8] = t["norm_mix_g"][0].reshape(8, P).T
    c[:PG, 8:16] = t["pool_scale"][0].reshape(8, PG).T
    c[:, 16:24] = t["norm_mlp_g"][0].reshape(8, P).T
    c[:, 24:32] = t["c_2"][0].reshape(8, P).T
    c[:, 32:35] = t["hgrn_lb_logits_2"][0].reshape(3, P).T
    c[:, 35:43] = np.concatenate([t["ret_norm_2"][0], t["hgrn_norm_2"][0], t["gla_norm_2"][0]]).reshape(8, P).T
    c[:, 43:51] = t["norm_mix_2"][0].reshape(8, P).T
    c[:, 51] = t["gla_ba_2"][0]
    c[:, 52] = np.tile((f(10000.0) ** (-np.arange(0, 64, 2, dtype=f) / 64)).astype(f), 4)
    c[:, 53] = np.tile(np.repeat([-1.0, 1.0], 32), 2)
    c[:, 58] = EPS
    c[:, 59] = 1.0
    c[:, 60:64] = -0.5
    return c


def _constants():
    f = np.float32
    c = {"ident": np.eye(P, dtype=f)}
    inv = np.ones((PG, 4, POOL_TAPS), f)
    for g in range(4):
        w = 2 << g
        for i in range(POOL_TAPS):
            inv[:, g, i] = w / min(i + 1, w)
    c["pool_inv"] = inv
    slopes = (2.0 ** (-8.0 * (np.arange(ATT_HEADS) + 1.0) / ATT_HEADS)).astype(f)
    bias = np.full((P, 2048), NEG, f)
    q = np.arange(P)[:, None]
    band = P + q - np.arange(2 * P)[None]
    own = q - np.arange(P)[None]
    for h in range(HEADS_GRP):
        bias[:, 256 * h:256 * h + 256] = np.where((band >= 0) & (band <= P), -(slopes[h] * band.astype(f)), f(NEG))
        far = (4 * own).astype(f)
        bias[:, 1024 + P * h:1024 + P * h + P] = np.where(own >= 0, -(slopes[4 + h] * far), f(NEG))
        bias[:, 1536 + P * h:1536 + P * h + P] = np.where((own >= 0) & (own % 4 == 0), -(slopes[8 + h] * far), f(NEG))
    c["bias"] = bias
    blocks = np.zeros((P, P), f)
    blocks[:64, :64] = blocks[64:, 64:] = 1 / 64
    c["ones_block"] = blocks
    perm = np.zeros((P, P), f)
    for m in range(P):
        perm[((m // 32) ^ 1) * 32 + m % 32, m] = 1
    c["perm"] = perm
    decay = np.zeros((RET_HEADS, P, S), f)
    key, tok = np.arange(P)[:, None], np.arange(S)[None]
    for h in range(RET_HEADS):
        lg = np.log1p(-2.0 ** (-5.0 - h))
        decay[h] = np.where(tok >= key, HEAD_DIM ** -0.5 * np.exp(lg * np.maximum(tok - key, 0)), 0)
    c["decay"] = decay
    masks = np.zeros((P, 8, P), np.int32)
    tok = np.arange(P)[None]
    masks[:, 0] = key == tok
    for lev in range(7):
        m = 1 << lev
        masks[:, 1 + lev] = (key // (2 * m) == tok // (2 * m)) & ((key // m) % 2 == 0) & ((tok // m) % 2 == 1)
    c["masks"] = masks
    c["iota"] = np.tile(np.arange(BLOCK, dtype=f), (P, 1))
    route = np.zeros((P, 448), f)
    route[:, 0:P] = np.triu(np.ones((P, P)), 1)
    route[:, P:2 * P] = 1
    route[:, 2 * P:2 * P + NC] = np.arange(S).reshape(NC, P).T
    route[:, 384:448] = BLOCK * np.arange(64)
    c["route_consts"] = route
    return c


def kernel(**inputs):
    import concourse.bacc as bacc
    from concourse.bass_utils import run_bass_kernel_spmd

    t = {name: np.asarray(a) for name, a in inputs.items()}
    data = _constants()
    data["x"] = np.ascontiguousarray(t["x"][0].reshape(NC, P, D).transpose(1, 0, 2))
    data["w"] = _weight_units(t)
    data["w_exp"] = _expert_units(t)
    data["cols"] = _cols(t)
    data["w_ada"] = np.ascontiguousarray(t["w_ada_2"][0].reshape(KD, P, 3, UNIT).transpose(0, 2, 1, 3).reshape(3 * KD, P, UNIT))
    data["b_ada"] = t["b_ada_2"]
    data["norm_final_g"] = t["norm_final_g"]
    data["positions"] = t["positions_2"][0]
    data["norm_ffn"] = t["norm_ffn_2"][0]
    data["norm_final_2"] = t["norm_final_2"]
    data["w_router"] = np.ascontiguousarray(_rows(
        np.concatenate([t["router_group_w_2"][0], t["router_expert_w_2"][0]], 1), 0, N_LOG).reshape(P, KD * N_LOG))
    data["b_router"] = np.concatenate([t["router_group_b_2"][0], t["router_expert_b_2"][0]])

    nc = bacc.Bacc("TRN2", target_bir_lowering=False, num_devices=1, dynamic_dma_scratch_size=4096)
    aps, arrays = {}, {}
    for name, a in data.items():
        arrays["in_" + name] = a
        aps[name] = nc.dram_tensor("in_" + name, list(a.shape), mybir.dt.from_np(a.dtype), kind="ExternalInput").ap()
    aps["mod_row"] = nc.dram_tensor("mod_row", [1, 4 * D], F32, kind="Internal").ap()
    aps["h2"] = nc.dram_tensor("h2", [S, D], F32, kind="Internal").ap()
    aps["y"] = nc.dram_tensor("y", [MAX_BLOCKS * BLOCK, D], F32, kind="Internal").ap()
    aps["out"] = nc.dram_tensor("out", [1, S, D], F32, kind="ExternalOutput").ap()
    build(nc, aps)
    result = run_bass_kernel_spmd(nc, [arrays], core_ids=[0])
    return result.results[0]["out"]
```
